# Optimizing a Trainium2 kernel written in Bass

```python
import jax
import jax.numpy as jnp
from jax import lax
import numpy as np

D_MODEL = 1024
BATCH = 1
SEQ = 128
DEPTH = 2
DEC_BATCH = 1
DEC_SEQ = 1024
PAST_LEN = 128

GRID_W = 64
EPS = 1e-6
CHUNK = 64
Q_BLOCK = 128

MLA_HEADS = 4
Q_LORA = 256
KV_LORA = 128
NOPE_DIM = 64
ROPE_DIM = 32
MLA_V_DIM = 64
ROPE_BASE = 10000.0
MLA_SCALE = (NOPE_DIM + ROPE_DIM) ** -0.5

GLA_HEADS = 4
GLA_DK = 64
GLA_DV = 64
GLA_GATE_RANK = 16
GLA_TAU = 16.0

GDN_HEADS = 8
GDN_DK = 64
GDN_DV = 64
CONV_W = 3

N_EXPERTS = 16
EXPERT_FF = 1024
EC_CAPACITY = 2

MLA_W = MLA_HEADS * MLA_V_DIM
GLA_QK = GLA_HEADS * GLA_DK
GLA_W = GLA_HEADS * GLA_DV
GDN_QK = GDN_HEADS * GDN_DK
GDN_W = GDN_HEADS * GDN_DV
MIX_W = MLA_W + GLA_W + GDN_W
IN_SIZES = (Q_LORA, KV_LORA, ROPE_DIM,
            GLA_QK, GLA_QK, GLA_W, 2 * GLA_GATE_RANK, GLA_W,
            GDN_QK, GDN_QK, GDN_W, GDN_W, 2 * GDN_HEADS, 2 * GDN_HEADS)
IN_DIM = sum(IN_SIZES)

kernel_name = 'hybrid_mla_gla_gdn_ec_flow_step'

def split_cols(t, sizes):
    outs, start = [], 0
    for s in sizes:
        outs.append(t[..., start:start + s])
        start += s
    return outs

def rms_norm(x, g):
    xf = x.astype(jnp.float32)
    y = xf * lax.rsqrt(jnp.mean(xf * xf, axis=-1, keepdims=True) + EPS)
    return (y * g.astype(jnp.float32)).astype(x.dtype)

def l2_norm(x):
    xf = x.astype(jnp.float32)
    return (xf * lax.rsqrt(jnp.sum(xf * xf, axis=-1, keepdims=True) + EPS)).astype(x.dtype)

def flip(t):
    return jnp.flip(t, axis=1)

def axial_rope(x):
    n = x.shape[1]
    rows = n // GRID_W
    row = jnp.repeat(jnp.arange(rows), GRID_W).astype(jnp.float32)
    col = jnp.tile(jnp.arange(GRID_W), rows).astype(jnp.float32)
    half = ROPE_DIM // 2
    freqs = ROPE_BASE ** (-jnp.arange(0, half, 2, dtype=jnp.float32) / half)
    ang = jnp.concatenate([row[:, None] * freqs, col[:, None] * freqs], axis=-1)
    ang = ang.reshape((n,) + (1,) * (x.ndim - 3) + (half,))
    cos, sin = jnp.cos(ang), jnp.sin(ang)
    xf = x.astype(jnp.float32)
    x1, x2 = xf[..., 0::2], xf[..., 1::2]
    out = jnp.stack([x1 * cos - x2 * sin, x1 * sin + x2 * cos], axis=-1)
    return out.reshape(x.shape).astype(x.dtype)

def block_attention(q, k, v, scale):
    b, nq, h, dk = q.shape
    nb = nq // Q_BLOCK
    qb = jnp.moveaxis(q.reshape(b, nb, Q_BLOCK, h, dk), 1, 0)

    def one_block(qi):
        s = jnp.einsum('bqhd,bkhd->bhqk', qi, k).astype(jnp.float32) * scale
        p = jax.nn.softmax(s, axis=-1).astype(v.dtype)
        return jnp.einsum('bhqk,bkhd->bqhd', p, v)

    o = lax.map(one_block, qb)
    return jnp.moveaxis(o, 0, 1).reshape(b, nq, h, v.shape[-1])

def expand_kv(ckv, w_kv_b):
    b, n, _ = ckv.shape
    kv = (ckv @ w_kv_b).reshape(b, n, MLA_HEADS, NOPE_DIM + MLA_V_DIM)
    return kv[..., :NOPE_DIM], kv[..., NOPE_DIM:]

def heads_bcast(t):
    return jnp.broadcast_to(t[:, :, None, :], t.shape[:2] + (MLA_HEADS, t.shape[-1]))

def short_conv(x, w):
    c = x.shape[-1]
    y = lax.conv_general_dilated(x, w[:, None, :].astype(x.dtype), window_strides=(1,),
                                 padding=[(CONV_W // 2, CONV_W // 2)],
                                 dimension_numbers=('NWC', 'WIO', 'NWC'), feature_group_count=c)
    return jax.nn.silu(y)

def gla_chunked(q, k, v, log_a, s0):
    out_dtype = v.dtype
    b, n, h, _ = q.shape
    nc = n // CHUNK

    def chunks(t):
        return t.astype(jnp.float32).reshape(b, nc, CHUNK, h, t.shape[-1])

    q, k, v, log_a = chunks(q), chunks(k), chunks(v), chunks(log_a)
    g = jnp.cumsum(log_a, axis=2)
    g_last = g[:, :, -1:]
    q_dec = q * jnp.exp(g)
    k_inv = k * jnp.exp(-g)
    k_end = k * jnp.exp(g_last - g)
    causal = jnp.tril(jnp.ones((CHUNK, CHUNK), dtype=bool))
    a = jnp.where(causal, jnp.einsum('bnihk,bnjhk->bnhij', q_dec, k_inv), 0.0)
    o_intra = jnp.einsum('bnhij,bnjhv->bnihv', a, v)

    def step(s, inp):
        qc, kc, vc, dc = inp
        o = jnp.einsum('bihk,bhkv->bihv', qc, s)
        s = s * dc[..., None] + jnp.einsum('bihk,bihv->bhkv', kc, vc)
        return s, o

    xs = tuple(jnp.moveaxis(t, 1, 0) for t in (q_dec, k_end, v, jnp.exp(g_last[:, :, 0])))
    s_fin, o_inter = lax.scan(step, s0.astype(jnp.float32), xs)
    o = o_intra + jnp.moveaxis(o_inter, 0, 1)
    return o.reshape(b, n, h, -1).astype(out_dtype), s_fin.astype(out_dtype)

def gdn_chunked(q, k, v, beta, log_a, s0):
    out_dtype = v.dtype
    b, n, h, _ = q.shape
    nc = n // CHUNK

    def chunks(t):
        return t.astype(jnp.float32).reshape((b, nc, CHUNK) + t.shape[2:])

    q, k, v, beta, log_a = (chunks(t) for t in (q, k, v, beta, log_a))
    g = jnp.cumsum(log_a, axis=2)
    gh = jnp.swapaxes(g, 2, 3)
    diff = gh[..., :, None] - gh[..., None, :]
    incl = jnp.tril(jnp.ones((CHUNK, CHUNK), dtype=bool))
    strict = jnp.tril(jnp.ones((CHUNK, CHUNK), dtype=bool), k=-1)
    k_beta = k * beta[..., None]
    m = jnp.einsum('bnihk,bnjhk->bnhij', k_beta, k) * jnp.exp(jnp.where(strict, diff, -jnp.inf))
    eye = jnp.broadcast_to(jnp.eye(CHUNK, dtype=jnp.float32), m.shape)
    t_inv = lax.linalg.triangular_solve(m, eye, left_side=True, lower=True, unit_diagonal=True)
    u = jnp.einsum('bnhij,bnjhv->bnihv', t_inv, v * beta[..., None])
    w = jnp.einsum('bnhij,bnjhk->bnihk', t_inv, k_beta * jnp.exp(g)[..., None])
    qk = jnp.einsum('bnihk,bnjhk->bnhij', q, k) * jnp.exp(jnp.where(incl, diff, -jnp.inf))
    q_dec = q * jnp.exp(g)[..., None]
    g_last = g[:, :, -1]
    k_end = k * jnp.exp(g_last[:, :, None] - g)[..., None]

    def step(s, inp):
        qc, kc, uc, wc, ac, dl = inp
        v_new = uc - jnp.einsum('bihk,bhkv->bihv', wc, s)
        o = jnp.einsum('bihk,bhkv->bihv', qc, s) + jnp.einsum('bhij,bjhv->bihv', ac, v_new)
        s = s * jnp.exp(dl)[..., None, None] + jnp.einsum('bihk,bihv->bhkv', kc, v_new)
        return s, o

    xs = tuple(jnp.moveaxis(t, 1, 0) for t in (q_dec, k_end, u, w, qk, g_last))
    s_fin, o = lax.scan(step, s0.astype(jnp.float32), xs)
    o = jnp.moveaxis(o, 0, 1)
    return o.reshape(b, n, h, -1).astype(out_dtype), s_fin.astype(out_dtype)

def bidirectional(scan_fn, shared, gates_f, gates_b, s0):
    o_f, s_f = scan_fn(*shared, *gates_f, s0[:, 0])
    o_b, s_b = scan_fn(*[flip(t) for t in shared], *[flip(t) for t in gates_b], s0[:, 1])
    return o_f + flip(o_b), jnp.stack([s_f, s_b], axis=1)

def token_mixers(xm, l, W, ctx_cache):
    b, n, _ = xm.shape
    dtype = xm.dtype
    f32 = jnp.float32
    proj = xm @ W['w_in'][l]
    (q_lat, kv_lat, k_rope, gla_q, gla_k, gla_v, gla_glr, gla_z,
     gdn_q, gdn_k, gdn_v, gdn_z, gdn_b, gdn_a) = split_cols(proj, IN_SIZES)

    q = (rms_norm(q_lat, W['mla_q_norm'][l]) @ W['mla_wq_b'][l]).reshape(b, n, MLA_HEADS, NOPE_DIM + ROPE_DIM)
    q_nope, q_rope = q[..., :NOPE_DIM], q[..., NOPE_DIM:]
    ckv = rms_norm(kv_lat, W['mla_kv_norm'][l])
    k_nope, v = expand_kv(ckv, W['mla_wkv_b'][l])
    if ctx_cache is None:
        qa = jnp.concatenate([q_nope, q_rope], axis=-1)
        ka = jnp.concatenate([k_nope, heads_bcast(k_rope)], axis=-1)
        va = v
        s0_gla = jnp.zeros((b, 2, GLA_HEADS, GLA_DK, GLA_DV), dtype)
        s0_gdn = jnp.zeros((b, 2, GDN_HEADS, GDN_DK, GDN_DV), dtype)
    else:
        ckv_c, kr_c, s0_gla, s0_gdn = ctx_cache
        lc = ckv_c.shape[1]
        k_nope_c, v_c = expand_kv(ckv_c, W['mla_wkv_b'][l])
        zr_lat = jnp.zeros((b, n, MLA_HEADS, ROPE_DIM), dtype)
        zr_ctx = jnp.zeros((b, lc, MLA_HEADS, ROPE_DIM), dtype)
        qa = jnp.concatenate([q_nope, axial_rope(q_rope), q_rope], axis=-1)
        k_lat = jnp.concatenate([k_nope, heads_bcast(axial_rope(k_rope)), zr_lat], axis=-1)
        k_ctx = jnp.concatenate([k_nope_c, zr_ctx, heads_bcast(kr_c)], axis=-1)
        ka = jnp.concatenate([k_ctx, k_lat], axis=1)
        va = jnp.concatenate([v_c, v], axis=1)
    o_mla = block_attention(qa, ka, va, MLA_SCALE).reshape(b, n, MLA_W)

    gq = gla_q.reshape(b, n, GLA_HEADS, GLA_DK) * (GLA_DK ** -0.5)
    gk = gla_k.reshape(b, n, GLA_HEADS, GLA_DK)
    gv = gla_v.reshape(b, n, GLA_HEADS, GLA_DV)
    gla_la = []
    for d in range(2):
        lr = gla_glr[..., d * GLA_GATE_RANK:(d + 1) * GLA_GATE_RANK]
        logit = (lr @ W['gla_wg'][l, d] + W['gla_bg'][l, d]).astype(f32)
        gla_la.append((jax.nn.log_sigmoid(logit) / GLA_TAU).reshape(b, n, GLA_HEADS, GLA_DK))
    o_gla, st_gla = bidirectional(gla_chunked, (gq, gk, gv), (gla_la[0],), (gla_la[1],), s0_gla)
    o_gla = rms_norm(o_gla, W['gla_out_norm'][l]) * jax.nn.silu(gla_z.reshape(b, n, GLA_HEADS, GLA_DV))

    qkv = short_conv(jnp.concatenate([gdn_q, gdn_k, gdn_v], axis=-1), W['gdn_conv'][l])
    dq, dk, dv = split_cols(qkv, (GDN_QK, GDN_QK, GDN_W))
    dq = l2_norm(dq.reshape(b, n, GDN_HEADS, GDN_DK)) * (GDN_DK ** -0.5)
    dk = l2_norm(dk.reshape(b, n, GDN_HEADS, GDN_DK))
    dv = dv.reshape(b, n, GDN_HEADS, GDN_DV)
    gdn_gates = []
    for d in range(2):
        sl = slice(d * GDN_HEADS, (d + 1) * GDN_HEADS)
        beta = jax.nn.sigmoid(gdn_b[..., sl].astype(f32))
        la = -jnp.exp(W['gdn_a_log'][l, d].astype(f32)) * jax.nn.softplus(
            gdn_a[..., sl].astype(f32) + W['gdn_dt_bias'][l, d].astype(f32))
        gdn_gates.append((beta, la))
    o_gdn, st_gdn = bidirectional(gdn_chunked, (dq, dk, dv), gdn_gates[0], gdn_gates[1], s0_gdn)
    o_gdn = rms_norm(o_gdn, W['gdn_out_norm'][l]) * jax.nn.silu(gdn_z.reshape(b, n, GDN_HEADS, GDN_DV))

    o = jnp.concatenate([o_mla, o_gla.reshape(b, n, GLA_W), o_gdn.reshape(b, n, GDN_W)], axis=-1)
    out = o @ W['w_out'][l]
    new = (ckv, k_rope, st_gla, st_gdn) if ctx_cache is None else None
    return out, new

def expert_choice_ffn(xm, l, W):
    b, n, d = xm.shape
    t = b * n
    xf = xm.reshape(t, d)
    aff = jax.nn.softmax((xf @ W['w_router'][l]).astype(jnp.float32), axis=-1)
    cap = EC_CAPACITY * t // N_EXPERTS
    gate, idx = lax.top_k(aff.T, cap)
    xe = xf[idx]
    h = jax.nn.silu(jnp.einsum('ecd,edf->ecf', xe, W['w_e1'][l])) * jnp.einsum('ecd,edf->ecf', xe, W['w_e3'][l])
    ye = jnp.einsum('ecf,efd->ecd', h, W['w_e2'][l]) * gate[..., None].astype(xm.dtype)
    out = jnp.zeros_like(xf).at[idx.reshape(-1)].add(ye.reshape(-1, d))
    return out.reshape(b, n, d)

def trunk_layer(x, l, W, cond, ctx_cache):
    mod = jax.nn.silu(cond) @ W['w_mod'][l] + W['b_mod'][l]
    sh1, sc1, g1, sh2, sc2, g2 = jnp.split(mod[:, None, :], 6, axis=-1)
    nrm = W['sandwich_norms'][l]
    xm = rms_norm(x, nrm[0]) * (1 + sc1) + sh1
    y, new = token_mixers(xm, l, W, ctx_cache)
    x = x + g1 * rms_norm(y, nrm[1])
    xm = rms_norm(x, nrm[2]) * (1 + sc2) + sh2
    x = x + g2 * rms_norm(expert_choice_ffn(xm, l, W), nrm[3])
    return x, new

def setup_inputs(seed: int = 0) -> dict:
    key = jax.random.key(seed)
    ks = iter(jax.random.split(key, 40))
    f32 = jnp.float32

    def nrm(shape, scale):
        return jax.random.normal(next(ks), shape, f32) * scale

    def gain(shape):
        return 1.0 + nrm(shape, 0.02)

    dt = jnp.exp(jax.random.uniform(next(ks), (DEPTH, 2, GDN_HEADS), f32,
                                    minval=float(np.log(1e-3)), maxval=float(np.log(1e-1))))
    return {
        'x_prompt': nrm((BATCH, SEQ, D_MODEL), 1.0),
        'x_sample': nrm((DEC_BATCH, DEC_SEQ, D_MODEL), 1.0),
        'cache_ckv': nrm((DEC_BATCH, DEPTH, PAST_LEN, KV_LORA), 1.0),
        'cache_krope': nrm((DEC_BATCH, DEPTH, PAST_LEN, ROPE_DIM), 1.0),
        'state_gla': nrm((DEC_BATCH, DEPTH, 2, GLA_HEADS, GLA_DK, GLA_DV), 0.2),
        'state_gdn': nrm((DEC_BATCH, DEPTH, 2, GDN_HEADS, GDN_DK, GDN_DV), 0.2),
        'c': nrm((DEC_BATCH, D_MODEL), 1.0),
        'c_ctx': nrm((D_MODEL,), 1.0),
        'w_in': nrm((DEPTH, D_MODEL, IN_DIM), D_MODEL ** -0.5),
        'mla_q_norm': gain((DEPTH, Q_LORA)),
        'mla_wq_b': nrm((DEPTH, Q_LORA, MLA_HEADS * (NOPE_DIM + ROPE_DIM)), Q_LORA ** -0.5),
        'mla_kv_norm': gain((DEPTH, KV_LORA)),
        'mla_wkv_b': nrm((DEPTH, KV_LORA, MLA_HEADS * (NOPE_DIM + MLA_V_DIM)), KV_LORA ** -0.5),
        'gla_wg': nrm((DEPTH, 2, GLA_GATE_RANK, GLA_QK), GLA_GATE_RANK ** -0.5),
        'gla_bg': nrm((DEPTH, 2, GLA_QK), 0.1),
        'gla_out_norm': gain((DEPTH, GLA_DV)),
        'gdn_conv': nrm((DEPTH, CONV_W, 2 * GDN_QK + GDN_W), CONV_W ** -0.5),
        'gdn_a_log': jnp.log(jax.random.uniform(next(ks), (DEPTH, 2, GDN_HEADS), f32, minval=1.0, maxval=16.0)),
        'gdn_dt_bias': dt + jnp.log(-jnp.expm1(-dt)),
        'gdn_out_norm': gain((DEPTH, GDN_DV)),
        'w_out': nrm((DEPTH, MIX_W, D_MODEL), MIX_W ** -0.5),
        'w_mod': nrm((DEPTH, D_MODEL, 6 * D_MODEL), 0.5 * D_MODEL ** -0.5),
        'b_mod': nrm((DEPTH, 6 * D_MODEL), 0.02),
        'sandwich_norms': gain((DEPTH, 4, D_MODEL)),
        'w_router': nrm((DEPTH, D_MODEL, N_EXPERTS), D_MODEL ** -0.5),
        'w_e1': nrm((DEPTH, N_EXPERTS, D_MODEL, EXPERT_FF), D_MODEL ** -0.5),
        'w_e3': nrm((DEPTH, N_EXPERTS, D_MODEL, EXPERT_FF), D_MODEL ** -0.5),
        'w_e2': nrm((DEPTH, N_EXPERTS, EXPERT_FF, D_MODEL), EXPERT_FF ** -0.5),
    }

def reference(x_prompt, x_sample, cache_ckv, cache_krope, state_gla, state_gdn, c, c_ctx,
              w_in, mla_q_norm, mla_wq_b, mla_kv_norm, mla_wkv_b, gla_wg, gla_bg, gla_out_norm,
              gdn_conv, gdn_a_log, gdn_dt_bias, gdn_out_norm, w_out, w_mod, b_mod, sandwich_norms,
              w_router, w_e1, w_e3, w_e2):
    W = dict(w_in=w_in, mla_q_norm=mla_q_norm, mla_wq_b=mla_wq_b, mla_kv_norm=mla_kv_norm,
             mla_wkv_b=mla_wkv_b, gla_wg=gla_wg, gla_bg=gla_bg, gla_out_norm=gla_out_norm,
             gdn_conv=gdn_conv, gdn_a_log=gdn_a_log, gdn_dt_bias=gdn_dt_bias, gdn_out_norm=gdn_out_norm,
             w_out=w_out, w_mod=w_mod, b_mod=b_mod, sandwich_norms=sandwich_norms,
             w_router=w_router, w_e1=w_e1, w_e3=w_e3, w_e2=w_e2)

    xp = x_prompt
    ckv_l, kr_l, sg_l, sd_l = [], [], [], []
    for l in range(DEPTH):
        xp, (ckv, kr, sg, sd) = trunk_layer(xp, l, W, c_ctx[None, :], None)
        ckv_l.append(ckv)
        kr_l.append(kr)
        sg_l.append(sg)
        sd_l.append(sd)

    xs = x_sample
    for l in range(DEPTH):
        xs, _ = trunk_layer(xs, l, W, c,
                            (cache_ckv[:, l], cache_krope[:, l], state_gla[:, l], state_gdn[:, l]))

    return (xp, xs, jnp.stack(ckv_l, axis=1), jnp.stack(kr_l, axis=1),
            jnp.stack(sg_l, axis=1), jnp.stack(sd_l, axis=1))


_drawn_inputs = setup_inputs


def setup_inputs(seed=0):
    import zlib

    import numpy as np

    out = dict(_drawn_inputs(seed))
    spreads = {}
    factors = {'cache_krope': 3.393, 'state_gla': 16.743, 'mla_q_norm': 3.997, 'gla_out_norm': 3.07}
    for name, (base, spread) in spreads.items():
        noise = np.random.default_rng([zlib.crc32(name.encode()), seed]).standard_normal(out[name].shape)
        drawn = base * np.exp(spread * noise) if base else spread * noise
        out[name] = jnp.asarray(drawn.astype(out[name].dtype))
    for name, factor in factors.items():
        out[name] = (out[name] * factor).astype(out[name].dtype)
    return out
```

```python
from contextlib import ExitStack, contextmanager

import numpy as np
import concourse.bass as bass
from concourse import mybir

F32 = mybir.dt.float32
I32 = mybir.dt.int32
U32 = mybir.dt.uint32
ALU = mybir.AluOpType
ACT = mybir.ActivationFunctionType
AX = mybir.AxisListType

P = 128
D = 1024
KD = D // P
DEPTH = 2
SEQ = 128
DEC = 1024
PAST = 128
ROWS = SEQ + DEC
TILES = ROWS // P
EPS = 1e-6
GRID_W = 64
H_MLA, NOPE, ROPE, VD = 4, 64, 32, 64
QL, KVL = 256, 128
QD = NOPE + ROPE
MLA_SCALE = float(NOPE + ROPE) ** -0.5
ROPE_BASE = 10000.0
H_GLA, GK = 4, 64
RANK = 16
TAU = 16.0
H_GDN = 8
GQ = H_GLA * GK
DQ = H_GDN * GK
IN_DIM = 3552
C_QLAT, C_KVLAT, C_KROPE = 0, 256, 384
C_GQ, C_GK, C_GV, C_GLR, C_GZ = 416, 672, 928, 1184, 1216
C_DQ, C_DK, C_DV, C_DZ, C_DB, C_DA = 1472, 1984, 2496, 3008, 3520, 3536
E_N = 16
FF = 1024
KF = FF // P
CAP_S = 2 * DEC // E_N
CAP_P = 2 * SEQ // E_N
CAP = CAP_S + CAP_P
NEG = -1e30


class Steps:

    def __init__(self):
        self.count = 0

    def __call__(self):
        self.count += 1
        return 1

    @property
    def n(self):
        assert self.count > 0
        return self.count

    def restart(self):
        self.count = 0


class Stage:
    def __init__(self, nc, name, ctx):
        self.nc, self.name, self.ctx, self.sems = nc, name, ctx, []

    def sb(self, name, shape, dt=F32):
        return self.ctx.enter_context(self.nc.sbuf_tensor(f"{self.name}_{name}", shape, dt))

    def ps(self, name, shape, dt=F32):
        return self.ctx.enter_context(self.nc.psum_tensor(f"{self.name}_{name}", shape, dt))

    def sem(self, name):
        s = self.ctx.enter_context(self.nc.semaphore(f"{self.name}_{name}"))
        self.sems.append(s)
        if not name.endswith("_steps"):
            self.nc.gpsimd.sem_inc(s, 1)
        return s

    def block(self):
        self.nc.all_engine_barrier()
        return self.nc.Block()


@contextmanager
def stage(nc, name):
    with ExitStack() as ctx:
        st = Stage(nc, name, ctx)
        yield st
        for s in st.sems:
            nc.gpsimd.sem_clear(s)
        nc.all_engine_barrier()


def bc(ap, shape):
    return ap.to_broadcast(shape)


class Turns:

    def __init__(self, base):
        self.base, self.n = base, 0

    def next(self):
        self.n += 1
        return self.base + (self.n + 1)


def load_constants(nc, T, B):
    with stage(nc, "init") as st:
        loaded, zeroed, stored = st.sem("loaded"), st.sem("zeroed"), st.sem("stored")
        with st.block() as block:
            @block.vector
            def _(dve):
                dve.memset(B.zero[:], 0.0).then_inc(zeroed, 1)
                dve.memset(B.ones[:], 1.0).then_inc(zeroed, 1)
                dve.memset(B.eps[:], EPS).then_inc(zeroed, 1)

            @block.sync
            def _(sp):
                n = 0
                for dst, src in ((B.masks[:], T["masks"]), (B.rope[:], T["rope"]), (B.ids[:], T["ids"]),
                                 (B.x[:, 0, :], T["x_prompt"][0]),
                                 (B.x[:, 1:TILES, :], T["x_sample"][0].rearrange("(t p) d -> p t d", p=P))):
                    sp.dma_start(dst, src).then_inc(loaded, 16)
                    n += 16
                sp.wait_ge(zeroed, 4)
                for row in (0, 1 + SEQ, 2 + ROWS):
                    sp.dma_start(T["proj"][row, :].rearrange("(p c) -> p c", c=32), B.zero[0:IN_DIM // 32, :]).then_inc(stored, 16)
                sp.wait_ge(loaded, n + 1)
                sp.wait_ge(stored, 49)


def modulation(nc, T, B, l):
    NB = 512
    with stage(nc, "mod") as st:
        cond = st.sb("cond", [P, 2, KD])
        e = st.sb("e", [P, 2, KD])
        w = st.sb("w", [P, 2, KD, NB])
        row = st.sb("row", [2, 6 * D])
        bias = st.sb("bias", [2, 6 * D])
        colT = st.sb("colT", [P, 2, 4, KD])
        gainT = st.sb("gainT", [P, 2, KD])
        gain = st.sb("gain", [P, 2, D])
        acc = st.ps("acc", [P, 2, 512])
        cond_in, w_in = st.sem("cond_in"), [st.sem("w_in0"), st.sem("w_in1")]
        exp_done, silu_done, prod_done, row_done = (st.sem(x) for x in ("exp_done", "silu_done", "prod_done", "row_done"))
        row_out, table_in, step_sem = st.sem("row_out"), st.sem("table_in"), st.sem("dve_steps")
        with st.block() as block:
            @block.sync
            def _(sp):
                sp.dma_start(cond[:, 0, :], T["c_ctx"].rearrange("(k p) -> p k", p=P)).then_inc(cond_in, 16)
                sp.dma_start(cond[:, 1, :], T["c"][0].rearrange("(k p) -> p k", p=P)).then_inc(cond_in, 16)
                sp.dma_start(bias[:], T["b_mod"][l].partition_broadcast(2)).then_inc(cond_in, 16)
                wsrc = T["w_mod"].rearrange("l (k p) n -> l p k n", p=P)
                with sp.Fori(0, 6) as n:
                    col = sp.snap(n * (2 * NB))
                    for s in range(2):
                        sp.wait_ge(prod_done, n * 2 + 1)
                        sp.dma_start(w[:, s], wsrc[l, :, :, bass.ds(col + s * NB, NB)]).then_inc(w_in[s], 16)
                sp.wait_ge(row_done, 13)
                sp.dma_start(T["mod"], row[:]).then_inc(row_out, 16)
                sp.wait_ge(row_out, 17)
                n = 0
                for c in range(2):
                    for i, j in enumerate((0, 1, 3, 4)):
                        sp.dma_start(colT[:, c, i, :], T["mod"][c, j * D:(j + 1) * D].rearrange("(k p) -> p k", p=P)).then_inc(table_in, 16)
                    for i, j in enumerate((2, 5)):
                        sp.dma_start(B.gate[:, i, c, :], T["mod"][c, j * D:(j + 1) * D].partition_broadcast(P)).then_inc(table_in, 16)
                for i in range(2):
                    sp.dma_start(gainT[:, i, :], T["sandwich_norms"][l, 2 * i].rearrange("(k p) -> p k", p=P)).then_inc(table_in, 16)
                    sp.dma_start(gain[:, i, :], T["sandwich_norms"][l, 2 * i + 1].partition_broadcast(P)).then_inc(table_in, 16)

            @block.scalar
            def _(act):
                act.wait_ge(cond_in, 49)
                act.activation(e[:], cond[:], ACT.Exp, scale=-1.0).then_inc(exp_done, 1)

            @block.tensor
            def _(pe):
                pe.wait_ge(silu_done, 2)
                with pe.Fori(0, 6) as n:
                    for s in range(2):
                        pe.wait_ge(w_in[s], n * 16 + 17)
                        pe.wait_ge(row_done, n * 2 + 1)
                        for k in range(KD):
                            mm = pe.matmul(acc[0:2, s, :], e[:, :, k], w[:, s, k, :], start=k == 0, stop=k == KD - 1)
                        mm.then_inc(prod_done, 1)

            @block.vector
            def _(dve):
                own, step = step_sem, Steps()
                dve.wait_ge(exp_done, 2)
                dve.tensor_scalar(e[:], e[:], 1.0, None, ALU.add).then_inc(own, step())
                dve.wait_ge(own, step.n)
                dve.reciprocal(e[:], e[:]).then_inc(own, step())
                dve.wait_ge(own, step.n)
                dve.tensor_tensor(e[:], e[:], cond[:], ALU.mult).then_inc(silu_done, 1)
                for n in range(12):
                    dve.wait_ge(prod_done, n + 2)
                    c = slice(n * NB, (n + 1) * NB)
                    dve.tensor_tensor(row[:, c], acc[0:2, n % 2, :], bias[:, c], ALU.add).then_inc(row_done, 1)
                dve.wait_ge(table_in, 16 * 16 + 1)
                for c in range(2):
                    for i in range(2):
                        dve.scalar_tensor_tensor(B.scale[:, c, i, :], colT[:, c, 2 * i + 1, :], 1.0, gainT[:, i, :], ALU.add, ALU.mult).then_inc(own, step())
                        dve.tensor_copy(B.shift[:, c, i, :], colT[:, c, 2 * i, :]).then_inc(own, step())
                        dve.tensor_tensor(B.gate[:, i, c, :], B.gate[:, i, c, :], gain[:, i, :], ALU.mult).then_inc(own, step())
                dve.wait_ge(own, step.n)


def input_norm(nc, T, B, l, xmT):
    with stage(nc, "norm") as st:
        sq = st.sb("sq", [P, D])
        ss = st.sb("ss", [P, 1])
        xhat = st.sb("xhat", [P, D])
        tr = st.ps("tr", [P, KD, P])
        rs_done, xhat_done, tr_done, ev_done = (st.sem(x) for x in ("rs_done", "xhat_done", "tr_done", "ev_done"))
        act_steps, dve_steps = st.sem("act_steps"), st.sem("dve_steps")
        with st.block() as block:
            @block.scalar
            def _(act):
                own, step = act_steps, Steps()

                def body(t):
                    act.wait_ge(xhat_done, t + 1)
                    act.activation(sq[:], B.x[:, t, :], ACT.Square, accum_out=ss[:]).then_inc(own, step())
                    act.wait_ge(own, step.n)
                    act.activation(ss[:], ss[:], ACT.Ln, bias=B.eps[:, 0:1], scale=1.0 / D).then_inc(own, step())
                    act.wait_ge(own, step.n)
                    act.activation(ss[:], ss[:], ACT.Exp, scale=-0.5).then_inc(rs_done, 1)
                    act.wait_ge(own, step.n)
                    act.sem_clear(own)
                    step.restart()
                with act.Fori(0, TILES) as t:
                    body(t)

            @block.vector
            def _(dve):
                own, step = dve_steps, Steps()

                def body(t, c):
                    dve.wait_ge(rs_done, t + 2)
                    dve.tensor_scalar(xhat[:], B.x[:, t, :], ss[:, 0:1], None, ALU.mult).then_inc(xhat_done, 1)
                    dve.wait_ge(tr_done, t + 2)
                    for k in range(KD):
                        dve.tensor_scalar(xmT[:, k, bass.ds(t * P, P)], tr[:, k, :], B.scale[:, c, 0, k:k + 1],
                                               B.shift[:, c, 0, k:k + 1], ALU.mult, ALU.add).then_inc(own, step())
                    dve.wait_ge(own, step.n)
                    dve.sem_clear(own)
                    step.restart()
                body(0, 0)
                with dve.Fori(1, TILES) as t:
                    body(t, 1)

            @block.tensor
            def _(pe):
                with pe.Fori(0, TILES) as t:
                    pe.wait_ge(xhat_done, t + 2)
                    for k in range(KD):
                        mm = pe.transpose(tr[:, k, :], xhat[:, k * P:(k + 1) * P], B.ident)
                    mm.then_inc(tr_done, 1)


def proj_row(t):
    return 1 if isinstance(t, int) and t == 0 else t * P + 2


def input_projection(nc, T, B, l, xmT):
    NB = IN_DIM // 8
    BANKS = 3
    with stage(nc, "proj") as st:
        w = st.sb("w", [P, 2, KD, NB])
        out = st.sb("out", [P, BANKS, NB])
        acc = st.ps("acc", [P, BANKS, 512])
        w_in = [st.sem("w_in0"), st.sem("w_in1")]
        prod_done, copied = st.sem("prod_done"), st.sem("copied")
        stored = [st.sem(f"stored{i}") for i in range(BANKS)]
        with st.block() as block:
            @block.sync
            def _(sp):
                wsrc = T["w_in"].rearrange("l (k p) n -> l p k n", p=P)
                with sp.Fori(0, 4) as n:
                    for s in range(2):
                        col = sp.snap(n * (2 * NB) + s * NB)
                        sp.wait_ge(prod_done, n * (2 * TILES) + 1)
                        if s == 1:
                            sp.wait_ge(prod_done, n * (2 * TILES) + 1)
                        sp.dma_start(w[:, s], wsrc[l, :, :, bass.ds(col, NB)]).then_inc(w_in[s], 16)

            @block.tensor
            def _(pe):
                with pe.Fori(0, 4) as n:
                    for s in range(2):
                        pe.wait_ge(w_in[s], n * 16 + 17)
                        for t in range(TILES):
                            i = s * TILES + t
                            b = i % BANKS
                            if i >= BANKS:
                                pe.wait_ge(copied, n * (2 * TILES) + (i - BANKS + 1) + 1)
                            else:
                                pe.wait_ge(copied, n * (2 * TILES) + 1)
                            for k in range(KD):
                                mm = pe.matmul(acc[:, b, 0:NB], xmT[:, k, t * P:(t + 1) * P], w[:, s, k, :],
                                               start=k == 0, stop=k == KD - 1)
                            mm.then_inc(prod_done, 1)

            @block.vector
            def _(dve):
                with dve.Fori(0, 4) as n:
                    for i in range(2 * TILES):
                        b = i % BANKS
                        dve.wait_ge(prod_done, n * (2 * TILES) + (i + 1) + 1)
                        dve.wait_ge(stored[b], n * (16 * 2 * TILES // BANKS) + 16 * (i // BANKS) + 1)
                        dve.tensor_copy(out[:, b, :], acc[:, b, 0:NB]).then_inc(copied, 1)

            @block.scalar
            def _(act):
                with act.Fori(0, 4) as n:
                    for i in range(2 * TILES):
                        b, s, t = i % BANKS, i // TILES, i % TILES
                        r = proj_row(t)
                        col = act.snap(n * (2 * NB) + s * NB)
                        act.wait_ge(copied, n * (2 * TILES) + (i + 1) + 1)
                        act.dma_start(T["proj"][r:r + P, bass.ds(col, NB)], out[:, b, :]).then_inc(stored[b], 16)
                for b in range(BANKS):
                    act.wait_ge(stored[b], 4 * 16 * 2 * TILES // BANKS + 1)


def rotate(own, step, dve, out, x, cos, sin, tmp):
    x1, x2 = x[..., 0::2], x[..., 1::2]
    dve.tensor_tensor(tmp[0], x1, cos, ALU.mult).then_inc(own, step())
    dve.tensor_tensor(tmp[1], x2, sin, ALU.mult).then_inc(own, step())
    dve.tensor_tensor(tmp[2], x1, sin, ALU.mult).then_inc(own, step())
    dve.tensor_tensor(tmp[3], x2, cos, ALU.mult).then_inc(own, step())
    dve.wait_ge(own, step.n)
    dve.tensor_tensor(out[..., 0::2], tmp[0], tmp[1], ALU.subtract).then_inc(own, step())
    dve.tensor_tensor(out[..., 1::2], tmp[2], tmp[3], ALU.add).then_inc(own, step())


def latent_attention(nc, T, B, l):
    with nc.sbuf_tensor("keysT", [P, H_MLA, 10 * P], F32) as keysT, nc.sbuf_tensor("values", [P, 10, H_MLA, VD], F32) as values:
        latent_keys(nc, T, B, l, keysT, values)
        attend(nc, T, B, l, keysT, values, True)
        attend(nc, T, B, l, keysT, values, False)


def latent_keys(nc, T, B, l, keysT, values):
    with stage(nc, "keys") as st:
        kin = st.sb("kin", [P, KVL + ROPE])
        ckv = st.sb("ckv", [P, KVL])
        ckvT = st.sb("ckvT", [P, P])
        ka = st.sb("ka", [P, H_MLA, P])
        kr = st.sb("kr", [P, ROPE])
        tmp = st.sb("tmp", [P, 4, ROPE // 2])
        sq = st.sb("sq", [P, KVL])
        rs = st.sb("rs", [P, 1])
        gain = st.sb("gain", [P, KVL])
        wkv = st.sb("wkv", [P, 512])
        tr, kv, trk = st.ps("tr", [P, 512]), st.ps("kv", [P, 512]), st.ps("trk", [P, H_MLA, P])
        w_in, k_in, rs_done, to_pe, from_pe, turn_done, stored = (
            st.sem(x) for x in ("w_in", "k_in", "rs_done", "to_pe", "from_pe", "turn_done", "stored"))
        asem, dsem = st.sem("act_steps"), st.sem("dve_steps")

        def turns(eng, body):
            body(0, "prompt")
            body(1, "context")
            with eng.Fori(2, 10) as s:
                body(s, "sample")

        with st.block() as block:
            @block.sync
            def _(sp):
                sp.dma_start(wkv[:], T["mla_wkv_b"][l]).then_inc(w_in, 16)
                sp.dma_start(gain[:], T["mla_kv_norm"][l].partition_broadcast(P)).then_inc(w_in, 16)

                def body(s, kind):
                    if kind == "sample":
                        r = sp.snap(s * P - (P - 2))
                    sp.wait_ge(turn_done, s + 1)
                    if kind == "context":
                        sp.dma_start(kin[:, 0:KVL], T["cache_ckv"][0, l]).then_inc(k_in, 16)
                        sp.dma_start(kin[:, KVL:], T["cache_krope"][0, l]).then_inc(k_in, 16)
                    else:
                        src = T["proj"][1:1 + P] if kind == "prompt" else T["proj"][bass.ds(r, P)]
                        sp.dma_start(kin[:, 0:KVL], src[:, C_KVLAT:C_KROPE]).then_inc(k_in, 16)
                        sp.dma_start(kin[:, KVL:], src[:, C_KROPE:C_GQ]).then_inc(k_in, 16)
                    if kind == "prompt":
                        sp.wait_ge(to_pe, 2)
                        sp.dma_start(T["new_ckv"][0, l], ckv[:]).then_inc(stored, 16)
                        sp.dma_start(T["new_krope"][0, l], kin[:, KVL:]).then_inc(stored, 16)
                        sp.wait_ge(stored, 33)
                turns(sp, body)

            @block.scalar
            def _(act):
                own, step = asem, Steps()

                def body(s, kind):
                    act.wait_ge(k_in, s * 32 + 33)
                    act.activation(sq[:], kin[:, 0:KVL], ACT.Square, accum_out=rs[:]).then_inc(own, step())
                    act.wait_ge(own, step.n)
                    act.activation(rs[:], rs[:], ACT.Ln, bias=B.eps[:, 0:1], scale=1.0 / KVL).then_inc(own, step())
                    act.wait_ge(own, step.n)
                    act.activation(rs[:], rs[:], ACT.Exp, scale=-0.5).then_inc(rs_done, 1)
                    act.wait_ge(own, step.n)
                    act.sem_clear(own)
                    step.restart()
                    act.wait_ge(turn_done, s + 2)
                turns(act, body)

            @block.tensor
            def _(pe):
                pe.wait_ge(w_in, 33)

                def body(s, kind):
                    op = Turns(s * 3)
                    pe.wait_ge(to_pe, op.next())
                    pe.transpose(tr[:, 0:P], ckv[:], B.ident).then_inc(from_pe, 1)
                    pe.wait_ge(to_pe, op.next())
                    pe.matmul(kv[:], ckvT[:], wkv[:], start=True, stop=True).then_inc(from_pe, 1)
                    pe.wait_ge(to_pe, op.next())
                    for h in range(H_MLA):
                        mm = pe.transpose(trk[:, h, :], ka[:, h, :], B.ident)
                    mm.then_inc(from_pe, 1)
                turns(pe, body)

            @block.vector
            def _(dve):
                own, step = dsem, Steps()
                dve.memset(ka[:], 0.0).then_inc(own, step())
                dve.wait_ge(own, step.n)
                dve.wait_ge(own, step.n)
                dve.sem_clear(own)
                step.restart()
                dve.wait_ge(w_in, 33)

                def body(s, kind):
                    pr = Turns(s * 3)
                    dve.wait_ge(rs_done, s + 2)
                    if kind == "prompt":
                        pass
                    if kind == "context":
                        dve.wait_ge(stored, 33)
                        dve.tensor_copy(ckv[:], kin[:, 0:KVL]).then_inc(to_pe, 1)
                    else:
                        dve.scalar_tensor_tensor(ckv[:], kin[:, 0:KVL], rs[:, 0:1], gain[:], ALU.mult, ALU.mult).then_inc(to_pe, 1)
                    dve.wait_ge(from_pe, pr.next())
                    dve.tensor_copy(ckvT[:], tr[:, 0:P]).then_inc(to_pe, 1)
                    raw = kin[:, KVL:]
                    if kind == "sample":
                        rotate(own, step, dve, kr[:], raw, B.rope[:, s - 1, 0, :], B.rope[:, s - 1, 1, :], [tmp[:, i, :] for i in range(4)])
                        dve.wait_ge(own, step.n)
                        if True:
                            dve.tensor_copy(ka[:, :, NOPE:QD], kr[:].unsqueeze(1).to_broadcast([P, H_MLA, ROPE])).then_inc(own, step())
                            dve.memset(ka[:, :, QD:P], 0.0).then_inc(own, step())
                    else:
                        dve.tensor_copy(ka[:, :, QD:P], raw.unsqueeze(1).to_broadcast([P, H_MLA, ROPE])).then_inc(own, step())
                    dve.wait_ge(from_pe, pr.next())
                    kvh = kv[:].rearrange("p (h e) -> p h e", h=H_MLA)
                    dve.tensor_copy(ka[:, :, 0:NOPE], kvh[:, :, 0:NOPE]).then_inc(own, step())
                    dve.tensor_copy(values[:, s, :, :], kvh[:, :, NOPE:]).then_inc(own, step())
                    dve.wait_ge(own, step.n)
                    dve.sem_inc(to_pe, 1)
                    dve.wait_ge(from_pe, pr.next())
                    dve.tensor_copy(keysT[:, :, bass.ds(s * P, P)], trk[:]).then_inc(own, step())
                    dve.wait_ge(own, step.n)
                    dve.wait_ge(own, step.n)
                    dve.sem_clear(own)
                    step.restart()
                    dve.sem_inc(turn_done, 1)
                turns(dve, body)


def attend(nc, T, B, l, keysT, values, prompt):
    NK = 1 if prompt else 9
    K0 = 0 if prompt else 1
    W = NK * P
    with stage(nc, "attp" if prompt else "atts") as st:
        qin = st.sb("qin", [P, QL])
        sq = st.sb("sq", [P, QL])
        rs = st.sb("rs", [P, 1])
        qlT = st.sb("qlT", [P, 2, P])
        q = st.sb("q", [P, H_MLA, QD])
        qa = st.sb("qa", [P, H_MLA, P])
        qaT = st.sb("qaT", [P, H_MLA, P])
        tmp = st.sb("tmp", [P, 4, H_MLA, ROPE // 2])
        gainT = st.sb("gainT", [P, 2])
        wq = st.sb("wq", [P, 2, H_MLA * QD])
        prob = st.sb("prob", [P, 2, W])
        probT = st.sb("probT", [P, 2, W])
        mx = st.sb("mx", [P, H_MLA])
        den = st.sb("den", [P, H_MLA])
        out = st.sb("out", [P, H_MLA, VD])
        score, turned = st.ps("score", [P, 1536]), st.ps("turned", [P, 1536])
        misc, acc = st.ps("misc", [P, 512]), st.ps("acc", [P, 512])
        mixed = [acc[:, 0:VD], misc[:, 0:VD]]
        w_in, q_in, rs_done, q_ready, q_prod = (st.sem(x) for x in ("w_in", "q_in", "rs_done", "q_ready", "q_prod"))
        score_done, max_done, exp_done, turn_done, probT_done, pv_done, out_done, stored = (st.sem(x) for x in (
            "score_done", "max_done", "exp_done", "turn_done", "probT_done", "pv_done", "out_done", "stored"))
        asem, dsem = st.sem("act_steps"), st.sem("dve_steps")

        def turns(eng, body):
            if prompt:
                body(0)
            else:
                with eng.Fori(0, TILES - 1) as i:
                    body(i)

        with st.block() as block:
            @block.sync
            def _(sp):
                sp.dma_start(wq[:], T["mla_wq_b"][l].rearrange("(k p) n -> p k n", p=P)).then_inc(w_in, 16)
                sp.dma_start(gainT[:], T["mla_q_norm"][l].rearrange("(k p) -> p k", p=P)).then_inc(w_in, 16)

                def body(i):
                    if not prompt:
                        r = sp.snap(i * P + (P + 2))
                    sp.wait_ge(out_done, i + 1)
                    src = T["proj"][1:1 + P] if prompt else T["proj"][bass.ds(r, P)]
                    sp.dma_start(qin[:], src[:, 0:QL]).then_inc(q_in, 16)
                turns(sp, body)

            @block.scalar
            def _(act):
                own, step = asem, Steps()

                def body(i):
                    act.wait_ge(q_in, i * 16 + 17)
                    act.activation(sq[:], qin[:], ACT.Square, accum_out=rs[:]).then_inc(own, step())
                    act.wait_ge(own, step.n)
                    act.activation(rs[:], rs[:], ACT.Ln, bias=B.eps[:, 0:1], scale=1.0 / QL).then_inc(own, step())
                    act.wait_ge(own, step.n)
                    act.activation(rs[:], rs[:], ACT.Exp, scale=-0.5).then_inc(rs_done, 1)
                    for h in range(H_MLA):
                        act.wait_ge(max_done, i * H_MLA + (h + 1) + 1)
                        act.activation(prob[:, h % 2, :], score[:, 0:W], ACT.Exp, bias=mx[:, h:h + 1], scale=MLA_SCALE,
                                       accum_out=den[:, h:h + 1]).then_inc(exp_done, 1)
                    act.wait_ge(own, step.n)
                    act.sem_clear(own)
                    step.restart()
                    row = 0 if prompt else act.snap(i * P + P)
                    act.wait_ge(out_done, i + 2)
                    act.dma_start(T["mla_out"][bass.ds(row, P), :], out[:].rearrange("p h e -> p (h e)")).then_inc(stored, 16)
                turns(act, body)
                act.wait_ge(stored, 16 * (1 if prompt else TILES - 1) + 1)

            @block.tensor
            def _(pe):
                pe.wait_ge(w_in, 33)

                def body(i):
                    ready = Turns(i * 3)
                    pe.wait_ge(out_done, i + 1)
                    pe.wait_ge(q_in, i * 16 + 17)
                    for k in range(2):
                        mm = pe.transpose(misc[:, k * P:(k + 1) * P], qin[:, k * P:(k + 1) * P], B.ident)
                    mm.then_inc(q_prod, 1)
                    pe.wait_ge(q_ready, ready.next())
                    for k in range(2):
                        mm = pe.matmul(misc[:, 0:H_MLA * QD], qlT[:, k, :], wq[:, k, :], start=k == 0, stop=k == 1)
                    mm.then_inc(q_prod, 1)
                    pe.wait_ge(q_ready, ready.next())
                    for h in range(H_MLA):
                        mm = pe.transpose(misc[:, h * P:(h + 1) * P], qa[:, h, :], B.ident)
                    mm.then_inc(q_prod, 1)
                    pe.wait_ge(q_ready, ready.next())

                    def scores(h):
                        pe.wait_ge(exp_done, i * H_MLA + h + 1)
                        for c in range(0, W, 512):
                            n = min(512, W - c)
                            mm = pe.matmul(score[:, c:c + n], qaT[:, h, :], keysT[:, h, K0 * P + c:K0 * P + c + n], start=True, stop=True)
                        mm.then_inc(score_done, 1)
                    scores(0)
                    for h in range(H_MLA):
                        if h + 1 < H_MLA:
                            scores(h + 1)
                        pe.wait_ge(exp_done, i * H_MLA + (h + 1) + 1)
                        pe.wait_ge(probT_done, i * H_MLA + h + 1)
                        for k in range(NK):
                            mm = pe.transpose(turned[:, k * P:(k + 1) * P], prob[:, h % 2, k * P:(k + 1) * P], B.ident)
                        mm.then_inc(turn_done, 1)
                        pe.wait_ge(probT_done, i * H_MLA + (h + 1) + 1)
                        for k in range(NK):
                            mm = pe.matmul(mixed[h % 2], probT[:, h % 2, k * P:(k + 1) * P], values[:, K0 + k, h, :],
                                           start=k == 0, stop=k == NK - 1)
                        mm.then_inc(pv_done, 1)
                turns(pe, body)

            @block.vector
            def _(dve):
                own, step = dsem, Steps()
                dve.wait_ge(w_in, 33)

                def body(i):
                    prod = Turns(i * 3)
                    dve.wait_ge(q_prod, prod.next())
                    for k in range(2):
                        dve.tensor_scalar(qlT[:, k, :], misc[:, k * P:(k + 1) * P], gainT[:, k:k + 1], None, ALU.mult).then_inc(own, step())
                    dve.wait_ge(own, step.n)
                    dve.sem_inc(q_ready, 1)
                    dve.wait_ge(q_prod, prod.next())
                    dve.wait_ge(rs_done, i + 2)
                    dve.tensor_scalar(q[:].rearrange("p h e -> p (h e)"), misc[:, 0:H_MLA * QD], rs[:, 0:1], None, ALU.mult).then_inc(own, step())
                    dve.wait_ge(own, step.n)
                    dve.tensor_copy(qa[:, :, 0:NOPE], q[:, :, 0:NOPE]).then_inc(own, step())
                    dve.tensor_copy(qa[:, :, QD:P], q[:, :, NOPE:QD]).then_inc(own, step())
                    t = 0 if prompt else i + 1
                    cos, sin = (B.rope[:, t, j, :].unsqueeze(1).to_broadcast([P, H_MLA, ROPE // 2]) for j in range(2))
                    rotate(own, step, dve, qa[:, :, NOPE:QD], q[:, :, NOPE:QD], cos, sin, [tmp[:, j] for j in range(4)])
                    dve.wait_ge(own, step.n)
                    dve.sem_inc(q_ready, 1)
                    dve.wait_ge(q_prod, prod.next())
                    dve.tensor_copy(qaT[:].rearrange("p h e -> p (h e)"), misc[:]).then_inc(q_ready, 1)

                    def softmax_max(h):
                        dve.wait_ge(score_done, i * H_MLA + (h + 1) + 1)
                        dve.tensor_reduce(mx[:, h:h + 1], score[:, 0:W], AX.X, ALU.max).then_inc(own, step())
                        dve.wait_ge(own, step.n)
                        dve.tensor_scalar(mx[:, h:h + 1], mx[:, h:h + 1], -MLA_SCALE, None, ALU.mult).then_inc(max_done, 1)

                    def output(h):
                        dve.wait_ge(pv_done, i * H_MLA + (h + 1) + 1)
                        dve.reciprocal(den[:, h:h + 1], den[:, h:h + 1]).then_inc(own, step())
                        dve.wait_ge(own, step.n)
                        dve.tensor_scalar(out[:, h, :], mixed[h % 2], den[:, h:h + 1], None, ALU.mult).then_inc(own, step())
                    softmax_max(0)
                    for h in range(H_MLA):
                        if h + 1 < H_MLA:
                            softmax_max(h + 1)
                        dve.wait_ge(turn_done, i * H_MLA + (h + 1) + 1)
                        dve.tensor_copy(probT[:, h % 2, :], turned[:, 0:W]).then_inc(probT_done, 1)
                        if h == 0:
                            dve.wait_ge(stored, i * 16 + 1)
                        if h:
                            output(h - 1)
                    output(H_MLA - 1)
                    dve.wait_ge(own, step.n)
                    dve.sem_clear(own)
                    step.restart()
                    dve.sem_inc(out_done, 1)
                turns(dve, body)


def scan_inputs(nc, T, B, l):
    CW = 3 * DQ
    GB, GL = 2 * H_GDN, 2 * GQ
    with stage(nc, "gate") as st:
        taps = st.sb("taps", [P, 3, CW])
        wc = st.sb("wc", [P, 3, CW])
        y, tmp, e = st.sb("y", [P, CW]), st.sb("tmp", [P, CW]), st.sb("e", [P, CW])
        ss = st.sb("ss", [P, 2 * H_GDN])
        ba = st.sb("ba", [P, 2 * GB])
        eb = st.sb("eb", [P, 2, GB])
        ab = st.sb("ab", [P, GB])
        gates = st.sb("gates", [P, 2 * GB])
        alog, dt = st.sb("alog", [P, GB]), st.sb("dt", [P, GB])
        lr = st.sb("lr", [P, 2, RANK])
        lrT = st.sb("lrT", [RANK, 2, P])
        wg = st.sb("wg", [RANK, 2, GQ])
        bg = st.sb("bg", [P, GL])
        logit, absl, la = st.sb("logit", [P, GL]), st.sb("absl", [P, GL]), st.sb("la", [P, GL])
        ptr, pl = st.ps("ptr", [P, 2, P]), st.ps("pl", [P, GL])
        w_in, t_in, to_act, from_act, to_pe, from_pe, ready, stored = (
            st.sem(x) for x in ("w_in", "t_in", "to_act", "from_act", "to_pe", "from_pe", "ready", "stored"))
        asem, dsem, psem = st.sem("act_steps"), st.sem("dve_steps"), st.sem("pool_steps")
        mixed = st.sem("mixed")

        def turns(eng, body):
            body(0)
            with eng.Fori(1, TILES) as t:
                body(t)

        with st.block() as block:
            @block.sync
            def _(sp):
                for dst, src in ((wc[:].rearrange("p a c -> p (a c)"), T["gdn_conv"][l].rearrange("a c -> (a c)").partition_broadcast(P)),
                                 (alog[:], T["gdn_a_log"][l].rearrange("a c -> (a c)").partition_broadcast(P)),
                                 (dt[:], T["gdn_dt_bias"][l].rearrange("a c -> (a c)").partition_broadcast(P)),
                                 (bg[:], T["gla_bg"][l].rearrange("a c -> (a c)").partition_broadcast(P)),
                                 (wg[:], T["gla_wg"][l].rearrange("a r c -> r a c"))):
                    sp.dma_start(dst, src).then_inc(w_in, 16)

                def body(t):
                    first = isinstance(t, int)
                    rows = [j if first else sp.snap(t * P + (1 + j)) for j in range(3)]
                    out_row = 0 if first else sp.snap(t * P)
                    sp.wait_ge(ready, t + 1)
                    for j in range(3):
                        sp.dma_start(taps[:, j, :], T["proj"][bass.ds(rows[j], P), C_DQ:C_DZ]).then_inc(t_in, 16)
                    sp.dma_start(ba[:], T["proj"][bass.ds(rows[1], P), C_DB:IN_DIM]).then_inc(t_in, 16)
                    sp.dma_start(lr[:].rearrange("p a r -> p (a r)"), T["proj"][bass.ds(rows[1], P), C_GLR:C_GZ]).then_inc(t_in, 16)
                    sp.wait_ge(ready, t + 2)
                    sp.dma_start(T["qkv"][bass.ds(out_row, P), :], y[:]).then_inc(stored, 16)
                    sp.dma_start(T["gates"][bass.ds(out_row, P), :], gates[:]).then_inc(stored, 16)
                    sp.dma_start(T["gla_la"][bass.ds(out_row, P), :], la[:]).then_inc(stored, 16)
                turns(sp, body)
                sp.wait_ge(stored, 48 * TILES + 1)

            @block.tensor
            def _(pe):
                pe.wait_ge(w_in, 81)

                def body(t):
                    pe.wait_ge(t_in, t * 80 + 81)
                    for d in range(2):
                        mm = pe.transpose(ptr[0:RANK, d, :], lr[:, d, :], B.ident)
                    mm.then_inc(from_pe, 1)
                    pe.wait_ge(to_pe, t + 2)
                    for d in range(2):
                        mm = pe.matmul(pl[:, d * GQ:(d + 1) * GQ], lrT[:, d, :], wg[:, d, :], start=True, stop=True)
                    mm.then_inc(from_pe, 1)
                turns(pe, body)

            @block.gpsimd
            def _(pool):
                own, step = psem, Steps()
                pool.wait_ge(w_in, 81)

                def body(t):
                    pool.wait_ge(t_in, t * 80 + 81)
                    pool.wait_ge(stored, t * 48 + 1)
                    pool.tensor_tensor(tmp[:], taps[:, 0, :], wc[:, 0, :], ALU.mult).then_inc(own, step())
                    pool.tensor_tensor(taps[:, 2, :], taps[:, 2, :], wc[:, 2, :], ALU.mult).then_inc(own, step())
                    pool.wait_ge(own, step.n)
                    pool.tensor_tensor(tmp[:], tmp[:], taps[:, 2, :], ALU.add).then_inc(mixed, 1)
                    pool.wait_ge(own, step.n)
                    pool.sem_clear(own)
                    step.restart()
                turns(pool, body)

            @block.scalar
            def _(act):
                own, step = asem, Steps()
                act.wait_ge(w_in, 81)
                act.activation(alog[:], alog[:], ACT.Exp).then_inc(own, step())
                act.wait_ge(own, step.n)
                act.wait_ge(own, step.n)
                act.sem_clear(own)
                step.restart()

                def body(t):
                    go = Turns(t * 4)
                    act.wait_ge(to_act, go.next())
                    act.activation(eb[:, 0, :], ba[:, 0:GB], ACT.Exp, scale=-1.0).then_inc(own, step())
                    act.activation(eb[:, 1, :], ab[:], ACT.Exp, scale=-1.0).then_inc(own, step())
                    act.wait_ge(own, step.n)
                    act.activation(eb[:, 1, :], eb[:, 1, :], ACT.Ln, bias=B.ones[:, 0:1]).then_inc(from_act, 1)
                    act.wait_ge(to_act, go.next())
                    act.activation(absl[:], absl[:], ACT.Exp, scale=-1.0).then_inc(own, step())
                    act.wait_ge(own, step.n)
                    act.activation(absl[:], absl[:], ACT.Ln, bias=B.ones[:, 0:1]).then_inc(from_act, 1)
                    act.wait_ge(to_act, go.next())
                    act.activation(e[:], y[:], ACT.Exp, scale=-1.0).then_inc(from_act, 1)
                    act.wait_ge(to_act, go.next())
                    act.activation(ss[:], ss[:], ACT.Ln, bias=B.eps[:, 0:1]).then_inc(own, step())
                    act.wait_ge(own, step.n)
                    act.activation(ss[:], ss[:], ACT.Exp, scale=-0.5).then_inc(from_act, 1)
                    act.wait_ge(own, step.n)
                    act.sem_clear(own)
                    step.restart()
                turns(act, body)

            @block.vector
            def _(dve):
                own, step = dsem, Steps()
                dve.wait_ge(w_in, 81)

                def body(t):
                    back = Turns(t * 4)
                    prod = Turns(t * 2)
                    dve.wait_ge(t_in, t * 80 + 81)
                    dve.wait_ge(stored, t * 48 + 1)
                    x = ba[:, GB:]
                    dve.tensor_tensor(x, x, dt[:], ALU.add).then_inc(own, step())
                    dve.wait_ge(own, step.n)
                    dve.scalar_tensor_tensor(ab[:], x, -1.0, x, ALU.mult, ALU.max).then_inc(own, step())
                    dve.wait_ge(own, step.n)
                    dve.sem_inc(to_act, 1)
                    dve.wait_ge(from_pe, prod.next())
                    dve.tensor_copy(lrT[:], ptr[0:RANK, :, :]).then_inc(to_pe, 1)
                    dve.wait_ge(from_act, back.next())
                    dve.scalar_tensor_tensor(eb[:, 1, :], x, 0.0, eb[:, 1, :], ALU.max, ALU.add).then_inc(own, step())
                    dve.wait_ge(own, step.n)
                    dve.scalar_tensor_tensor(gates[:, GB:], eb[:, 1, :], -1.0, alog[:], ALU.mult, ALU.mult).then_inc(own, step())
                    dve.tensor_scalar(eb[:, 0, :], eb[:, 0, :], 1.0, None, ALU.add).then_inc(own, step())
                    dve.wait_ge(own, step.n)
                    dve.reciprocal(gates[:, 0:GB], eb[:, 0, :]).then_inc(own, step())
                    dve.wait_ge(from_pe, prod.next())
                    dve.tensor_tensor(logit[:], pl[:], bg[:], ALU.add).then_inc(own, step())
                    dve.wait_ge(own, step.n)
                    dve.scalar_tensor_tensor(absl[:], logit[:], -1.0, logit[:], ALU.mult, ALU.max).then_inc(own, step())
                    dve.wait_ge(own, step.n)
                    dve.sem_inc(to_act, 1)
                    dve.tensor_tensor(y[:], taps[:, 1, :], wc[:, 1, :], ALU.mult).then_inc(own, step())
                    dve.wait_ge(own, step.n)
                    dve.wait_ge(mixed, t + 2)
                    dve.tensor_tensor(y[:], y[:], tmp[:], ALU.add).then_inc(own, step())
                    dve.wait_ge(own, step.n)
                    dve.wait_ge(from_act, back.next())
                    dve.sem_inc(to_act, 1)
                    dve.scalar_tensor_tensor(la[:], logit[:], 0.0, absl[:], ALU.min, ALU.subtract).then_inc(own, step())
                    dve.wait_ge(own, step.n)
                    dve.tensor_scalar(la[:], la[:], 1.0 / TAU, None, ALU.mult).then_inc(own, step())
                    dve.wait_ge(from_act, back.next())
                    dve.tensor_scalar(e[:], e[:], 1.0, None, ALU.add).then_inc(own, step())
                    dve.wait_ge(own, step.n)
                    dve.reciprocal(e[:], e[:]).then_inc(own, step())
                    dve.wait_ge(own, step.n)
                    dve.tensor_tensor(y[:], y[:], e[:], ALU.mult).then_inc(own, step())
                    dve.wait_ge(own, step.n)
                    dve.tensor_tensor(e[:, 0:2 * DQ], y[:, 0:2 * DQ], y[:, 0:2 * DQ], ALU.mult).then_inc(own, step())
                    dve.wait_ge(own, step.n)
                    dve.tensor_reduce(ss[:], e[:, 0:2 * DQ].rearrange("p (h e) -> p h e", e=GK), AX.X, ALU.add).then_inc(own, step())
                    dve.wait_ge(own, step.n)
                    dve.sem_inc(to_act, 1)
                    dve.wait_ge(from_act, back.next())
                    dve.tensor_scalar(ss[:, 0:H_GDN], ss[:, 0:H_GDN], float(GK) ** -0.5, None, ALU.mult).then_inc(own, step())
                    dve.wait_ge(own, step.n)
                    qk = y[:, 0:2 * DQ].rearrange("p (h e) -> p h e", e=GK)
                    dve.tensor_tensor(qk, qk, ss[:].unsqueeze(2).to_broadcast([P, 2 * H_GDN, GK]), ALU.mult).then_inc(own, step())
                    dve.wait_ge(own, step.n)
                    dve.sem_clear(own)
                    step.restart()
                    dve.sem_inc(ready, 1)
                turns(dve, body)


LEVELS = 7
PE_N, DVE_N, ACT_N, POOL_N = 25, 22, 8, 2 + LEVELS


def scan(nc, T, B, l, prompt):
    N = 1 if prompt else TILES - 1
    H, G = H_GDN, H_GLA
    with stage(nc, "scanp" if prompt else "scans") as st:
        both = lambda name, shape: [st.sb(f"{name}{d}", shape) for d in range(2)]
        qkv, gla, gla_la, gate = both("qkv", [P, 3, H, GK]), both("gla", [P, 3, G, GK]), both("gla_la", [P, GQ]), both("gate", [P, 16])
        decay = both("decay", [P, H, P])
        S, ST = both("S", [P, H, P]), [both("Sa", [P, H, P]), both("Sb", [P, H, P])]
        A, Ti, TT, Y = both("A", [P, H, P]), both("Ti", [P, H, P]), both("TT", [P, H, P]), both("Y", [P, H, P])
        kT, qT = both("kT", [GK, H, P]), both("qT", [GK, H, P])
        nwT = kT
        Rk, Rv, kend, VN = both("Rk", [P, H, GK]), both("Rv", [P, H, GK]), both("kend", [P, H, GK]), both("VN", [P, H, GK])
        s_d, s_g, s_m = both("s_d", [GK, H, GK]), both("s_g", [GK, G, GK]), both("s_m", [GK, G, GK])
        gg, eg = both("gg", [P, 3, H]), both("eg", [P, 3, H])
        mid, emid = both("mid", [GK, G, 3]), both("emid", [GK, G, 3])
        E, Ei = both("E", [P, G, GK]), both("Ei", [P, G, GK])
        gkv = both("gkv", [GK, G, GK])
        out = both("out", [P, 768])
        gT = [TT[d][0:GK] for d in range(2)]
        gA = both("gA", [P, G, P])
        qd, ki = E, Ei
        pX, pY = [st.ps(f"pX{d}", [P, H, P]) for d in range(2)], [st.ps(f"pY{d}", [P, H, P]) for d in range(2)]
        fpe, fdve, fact, fpool = ([st.sem(f"{x}_done{d}") for d in range(2)] for x in ("pe", "dve", "act", "pool"))
        arrived, stored, s_in = ([st.sem(f"{x}{d}") for d in range(2)] for x in ("arrived", "stored", "state_in"))
        asem, dsem, passed = st.sem("act_steps"), st.sem("dve_steps"), st.sem("passed")
        cum = [B.masks[:, 1, :], B.masks[:, 2, :]]
        anchored = [B.masks[:, 3, :], B.masks[:, 4, :]]
        mid_col = [B.midcols[:, 0:2], B.midcols[:, 2:4]]
        kd, qdl, vd = [qkv[d][:, 1] for d in range(2)], [qkv[d][:, 0] for d in range(2)], [qkv[d][:, 2] for d in range(2)]
        last = {}

        def heads(ap, n, w):
            return ap.unsqueeze(2).to_broadcast([ap.shape[0], n, w])

        def over(ap, n):
            return ap.unsqueeze(1).to_broadcast([ap.shape[0], n, ap.shape[1]])

        bank = lambda p, b: p[:].rearrange("p (b h) c -> p b (h c)", b=2)[:, b, :].rearrange("p (h e) -> p h e", e=GK)

        def turns(eng, body):
            if prompt:
                body(0)
            else:
                with eng.Fori(0, N) as t:
                    body(t)

        with st.block() as block:
            @block.sync
            def _(sp):
                if not prompt:
                    for d in range(2):
                        sp.dma_start(s_d[d][:], T["state_gdn"][0, l, d].rearrange("h k v -> k h v")).then_inc(s_in[d], 16)
                        sp.dma_start(s_g[d][:], T["state_gla"][0, l, d].rearrange("h k v -> k h v")).then_inc(s_in[d], 16)

                def body(t):
                    if prompt:
                        row, prow = [0, 0], [1, 1]
                    else:
                        row = [sp.snap(t * P + P), sp.snap(t * -P + N * P)]
                        prow = [sp.snap(t * P + P + 2), sp.snap(t * -P + (N * P + 2))]
                    for d in range(2):
                        sp.wait_ge(fdve[d], t * DVE_N + 1)
                        R, Q = bass.ds(row[d], P), bass.ds(prow[d], P)
                        for dst, src in ((gla_la[d][:], T["gla_la"][R, d * GQ:(d + 1) * GQ]),
                                         (gla[d][:].rearrange("p a h e -> p (a h e)"), T["proj"][Q, C_GQ:C_GLR]),
                                         (qkv[d][:].rearrange("p a h e -> p (a h e)"), T["qkv"][R, :]),
                                         (gate[d][:, 0:H], T["gates"][R, d * H:(d + 1) * H]),
                                         (gate[d][:, H:], T["gates"][R, 2 * H + d * H:2 * H + (d + 1) * H])):
                            sp.dma_start(dst, src).then_inc(arrived[d], 16)
                    for d in range(2):
                        sp.wait_ge(fdve[d], t * DVE_N + DVE_N + 1)
                        sp.dma_start(T["scan_b" if d else "scan_f"][bass.ds(row[d], P), :], out[d][:]).then_inc(stored[d], 16)
                turns(sp, body)
                n = N
                if prompt:
                    for d in range(2):
                        sp.dma_start(T["new_gdn"][0, l, d].rearrange("h k v -> k h v"), s_d[d][:]).then_inc(stored[d], 16)
                        sp.dma_start(T["new_gla"][0, l, d].rearrange("h k v -> k h v"), s_g[d][:]).then_inc(stored[d], 16)
                    n = 3
                for d in range(2):
                    sp.wait_ge(stored[d], 16 * n + 1)

            @block.tensor
            def _(pe):
                def body(t):
                    for d in range(2):
                        pe.wait_ge(arrived[d], t * 80 + 81)
                        pe.wait_ge(fdve[d], t * DVE_N + 1)
                        pe.matmul(pY[d][:, 0:2, :], anchored[d], gla_la[d][:], start=True, stop=True)
                        for h in range(G):
                            mm = pe.matmul(pX[d][0:GK, 0, 2 * h:2 * h + 2], gla_la[d][:, h * GK:(h + 1) * GK], mid_col[d], start=True, stop=True)
                        mm.then_inc(fpe[d], 1)
                    for d in range(2):
                        pe.wait_ge(fdve[d], t * DVE_N + 3)
                        pe.sem_inc(passed, 1)
                        for h in range(G):
                            pe.transpose(pX[d][0:GK, h, :], qd[d][:, h, :], B.ident)
                            mm = pe.transpose(pX[d][0:GK, G + h, :], ki[d][:, h, :], B.ident)
                        mm.then_inc(fpe[d], 1)
                    for d in range(2):
                        pe.wait_ge(fact[d], t * ACT_N + 4)
                        for h in range(G):
                            mm = pe.matmul(pY[d][:, h, :], gT[d][:, G + h, :], gT[d][:, h, :], start=True, stop=True)
                        mm.then_inc(fpe[d], 1)
                    for d in range(2):
                        pe.wait_ge(fdve[d], t * DVE_N + 4)
                        for h in range(G):
                            pe.matmul(bank(pX[d], 0)[:, h, :], gA[d][:, h, :], gla[d][:, 2, h, :], start=True, stop=False)
                            pe.matmul(bank(pX[d], 0)[:, h, :], gT[d][:, h, :], s_m[d][:, h, :], start=False, stop=True)
                        for h in range(G):
                            mm = pe.matmul(bank(pX[d], 1)[0:GK, h, :], ki[d][:, h, :], gla[d][:, 2, h, :], start=True, stop=True)
                        mm.then_inc(fpe[d], 1)
                    for d in range(2):
                        pe.wait_ge(fdve[d], t * DVE_N + 5)
                        la = gate[d][:, H:]
                        pe.matmul(pY[d][:, 0, 0:H], cum[d], la, start=True, stop=True)
                        pe.matmul(pY[d][:, 0, H:2 * H], B.ones[:], la, start=True, stop=True)
                        for h in range(H):
                            mm = pe.matmul(pX[d][:, h, :], la[:, h:h + 1].to_broadcast([P, P]), cum[d], start=True, stop=True)
                        mm.then_inc(fpe[d], 1)
                    for d in range(2):
                        pe.wait_ge(fdve[d], t * DVE_N + 6)
                        pe.sem_inc(passed, 1)
                        for h in range(H):
                            mm = pe.transpose(pY[d][0:GK, h, :], kd[d][:, h, :], B.ident)
                        mm.then_inc(fpe[d], 1)
                        for h in range(H):
                            mm = pe.transpose(pX[d][0:GK, h, :], qdl[d][:, h, :], B.ident)
                        mm.then_inc(fpe[d], 1)
                    for d in range(2):
                        pe.wait_ge(fact[d], t * ACT_N + 8)
                        for h in range(H):
                            pe.matmul(pX[d][:, h, :], kT[d][:, h, :], kT[d][:, h, :], start=True, stop=True)
                            mm = pe.matmul(pY[d][:, h, :], kT[d][:, h, :], qT[d][:, h, :], start=True, stop=True)
                        mm.then_inc(fpe[d], 1)
                    for v in range(LEVELS):
                        for d in range(2):
                            pe.wait_ge(fdve[d], t * DVE_N + (6 + 2 * v) + 1)
                            pe.wait_ge(fpool[d], t * POOL_N + (2 + v) + 1)
                            for h in range(H):
                                mm = pe.matmul(pX[d][:, h, :], ST[v % 2][d][:, h, :], Ti[d][:, h, :] if v else B.ident, start=True, stop=True)
                            mm.then_inc(fpe[d], 1)
                        for d in range(2):
                            pe.wait_ge(fdve[d], t * DVE_N + (7 + 2 * v) + 1)
                            for h in range(H):
                                if 0 < v < LEVELS - 1:
                                    pe.matmul(pY[d][:, h, :], TT[d][:, h, :], Y[d][:, h, :], start=True, stop=True)
                                mm = pe.matmul(pX[d][:, h, :], Y[d][:, h, :], TT[d][:, h, :] if v else B.ident, start=True, stop=True)
                            mm.then_inc(fpe[d], 1)
                    for d in range(2):
                        pe.wait_ge(fdve[d], t * DVE_N + 21)
                        pe.wait_ge(fpool[d], t * POOL_N + 10)
                        for h in range(H):
                            mm = pe.matmul(pX[d][0:GK, h, :], Rk[d][:, h, :], TT[d][:, h, :], start=True, stop=True)
                        mm.then_inc(fpe[d], 1)
                    for d in range(2):
                        pe.wait_ge(fact[d], t * ACT_N + 9)
                        for h in range(H):
                            pe.matmul(bank(pY[d], 0)[:, h, :], TT[d][:, h, :], Rv[d][:, h, :], start=True, stop=False)
                            mm = pe.matmul(bank(pY[d], 0)[:, h, :], nwT[d][:, h, :], s_d[d][:, h, :], start=False, stop=True)
                        mm.then_inc(fpe[d], 1)
                    for d in range(2):
                        pe.wait_ge(fdve[d], t * DVE_N + 22)
                        for h in range(H):
                            pe.matmul(bank(pX[d], 0)[:, h, :], qT[d][:, h, :], s_d[d][:, h, :], start=True, stop=True)
                            pe.matmul(bank(pX[d], 1)[:, h, :], A[d][:, h, :], VN[d][:, h, :], start=True, stop=True)
                            mm = pe.matmul(bank(pY[d], 1)[0:GK, h, :], kend[d][:, h, :], VN[d][:, h, :], start=True, stop=True)
                        mm.then_inc(fpe[d], 1)
                turns(pe, body)

            @block.scalar
            def _(act):
                own, step = asem, Steps()

                def body(t):
                    for d in range(2):
                        act.wait_ge(fpe[d], t * PE_N + 2)
                        y = pY[d][:, 0:2, :].rearrange("p a c -> p (a c)")
                        act.activation(E[d][:].rearrange("p h e -> p (h e)"), y, ACT.Exp).then_inc(own, step())
                        act.activation(Ei[d][:].rearrange("p h e -> p (h e)"), y, ACT.Exp, scale=-1.0).then_inc(fact[d], 1)
                        act.wait_ge(fdve[d], t * DVE_N + 2)
                        act.activation(emid[d][:], mid[d][:], ACT.Exp).then_inc(fact[d], 1)
                    for d in range(2):
                        act.wait_ge(fpe[d], t * PE_N + 3)
                        act.activation(gT[d], pX[d][0:GK], ACT.Copy).then_inc(fact[d], 1)
                    for d in range(2):
                        act.wait_ge(fdve[d], t * DVE_N + 6)
                        act.activation(eg[d][:], gg[d][:], ACT.Exp).then_inc(fact[d], 1)
                        act.activation(decay[d][:], decay[d][:], ACT.Exp).then_inc(fact[d], 1)
                        act.wait_ge(fpe[d], t * PE_N + 7)
                        act.activation(kT[d][:], pY[d][0:GK], ACT.Copy).then_inc(fact[d], 1)
                        act.wait_ge(fpe[d], t * PE_N + 8)
                        act.activation(qT[d][:], pX[d][0:GK], ACT.Copy).then_inc(fact[d], 1)
                    for d in range(2):
                        act.wait_ge(fpe[d], t * PE_N + 24)
                        act.activation(nwT[d][:], pX[d][0:GK], ACT.Copy, scale=-1.0).then_inc(fact[d], 1)
                    act.wait_ge(own, step.n)
                    act.sem_clear(own)
                    step.restart()
                turns(act, body)

            @block.gpsimd
            def _(pool):
                def body(t):
                    for d in range(2):
                        pool.wait_ge(fact[d], t * ACT_N + 6)
                        pool.tensor_tensor(decay[d][:], decay[d][:], over(cum[d], H), ALU.mult).then_inc(fpool[d], 1)
                    for v in range(LEVELS):
                        for d in range(2):
                            if v == 0:
                                pool.wait_ge(fdve[d], t * DVE_N + 7)
                            if v >= 2:
                                pool.wait_ge(fpe[d], t * PE_N + (9 + 2 * (v - 2)) + 1)
                            pool.tensor_tensor(ST[v % 2][d][:], S[d][:], over(B.masks[:, 5 + 7 * d + v, :], H), ALU.mult).then_inc(fpool[d], 1)
                    for d in range(2):
                        pool.tensor_tensor(kend[d][:], kd[d], heads(eg[d][:, 2, :], H, GK), ALU.mult)
                        pool.tensor_tensor(Rv[d][:], vd[d], heads(gate[d][:, 0:H], H, GK), ALU.mult)
                        pool.tensor_tensor(Rk[d][:], kd[d], heads(gg[d][:, 1, :], H, GK), ALU.mult).then_inc(fpool[d], 1)
                turns(pool, body)

            @block.vector
            def _(dve):
                own, step = dsem, Steps()
                for d in range(2):
                    dve.memset(gA[d][:], 0.0).then_inc(own, step())
                    if prompt:
                        dve.memset(s_d[d][:], 0.0).then_inc(own, step())
                        dve.memset(s_g[d][:], 0.0).then_inc(own, step())
                    else:
                        dve.wait_ge(s_in[d], 33)
                dve.wait_ge(own, step.n)
                dve.sem_clear(own)
                step.restart()

                def body(t):
                    for d in range(2):
                        dve.wait_ge(fpe[d], t * PE_N + 2)
                        mg = pX[d][0:GK, 0, 0:2 * G].rearrange("p (h a) -> p h a", a=2)
                        dve.tensor_copy(mid[d][:, :, 0:2], mg).then_inc(own, step())
                        dve.wait_ge(own, step.n)
                        dve.tensor_tensor(mid[d][:, :, 2], mid[d][:, :, 1], mid[d][:, :, 0], ALU.subtract).then_inc(fdve[d], 1)
                    for d in range(2):
                        dve.wait_ge(fact[d], t * ACT_N + 2)
                        dve.scalar_tensor_tensor(qd[d][:], gla[d][:, 0], float(GK) ** -0.5, E[d][:], ALU.mult, ALU.mult).then_inc(own, step())
                        dve.tensor_tensor(ki[d][:], gla[d][:, 1], Ei[d][:], ALU.mult).then_inc(fdve[d], 1)
                    for d in range(2):
                        dve.wait_ge(fact[d], t * ACT_N + 3)
                        dve.wait_ge(fpe[d], t * PE_N + 4)
                        dve.tensor_tensor(s_m[d][:], s_g[d][:], heads(emid[d][:, :, 0], G, GK), ALU.mult).then_inc(own, step())
                        dve.copy_predicated(gA[d][:], over(cum[d], G).bitcast(U32), pY[d][:, 0:G, :]).then_inc(fdve[d], 1)
                    for d in range(2):
                        dve.wait_ge(fpe[d], t * PE_N + 5)
                        dve.wait_ge(stored[d], t * 16 + 1)
                        dve.tensor_copy(out[d][:, 0:GQ].rearrange("p (h e) -> p h e", e=GK), bank(pX[d], 0)[:, 0:G, :]).then_inc(own, step())
                        dve.tensor_tensor(gkv[d][:], bank(pX[d], 1)[0:GK, 0:G, :], heads(emid[d][:, :, 2], G, GK), ALU.mult).then_inc(own, step())
                        dve.tensor_tensor(s_g[d][:], s_g[d][:], heads(emid[d][:, :, 1], G, GK), ALU.mult).then_inc(own, step())
                        dve.wait_ge(own, step.n)
                        dve.tensor_tensor(s_g[d][:], s_g[d][:], gkv[d][:], ALU.add).then_inc(fdve[d], 1)
                    for d in range(2):
                        dve.wait_ge(fpe[d], t * PE_N + 6)
                        dve.tensor_copy(gg[d][:, 0:2, :], pY[d][:, 0, 0:2 * H].rearrange("p (a h) -> p a h", h=H)).then_inc(own, step())
                        dve.wait_ge(own, step.n)
                        dve.tensor_tensor(gg[d][:, 2, :], gg[d][:, 1, :], gg[d][:, 0, :], ALU.subtract).then_inc(own, step())
                        for h in range(H):
                            dve.tensor_scalar(decay[d][:, h, :], pX[d][:, h, :], gg[d][:, 0, h:h + 1], 0.0, ALU.subtract, ALU.min).then_inc(own, step())
                        dve.wait_ge(own, step.n)
                        dve.sem_inc(fdve[d], 1)
                    for d in range(2):
                        dve.wait_ge(fact[d], t * ACT_N + 5)
                        dve.tensor_tensor(gg[d][:, 1, :], eg[d][:, 0, :], gate[d][:, 0:H], ALU.mult).then_inc(own, step())
                        dve.wait_ge(own, step.n)
                    for d in range(2):
                        dve.wait_ge(fpe[d], t * PE_N + 9)
                        dve.wait_ge(fpool[d], t * POOL_N + 2)
                        dve.tensor_tensor(S[d][:], pX[d][:], decay[d][:], ALU.mult).then_inc(own, step())
                        dve.tensor_tensor(A[d][:], pY[d][:], decay[d][:], ALU.mult).then_inc(own, step())
                        dve.wait_ge(own, step.n)
                        dve.sem_inc(fdve[d], 1)
                    for v in range(LEVELS):
                        for d in range(2):
                            dve.wait_ge(fpe[d], t * PE_N + (9 + 2 * v) + 1)
                            dve.tensor_tensor(Y[d][:], pX[d][:], heads(gate[d][:, 0:H], H, P), ALU.mult).then_inc(fdve[d], 1)
                        for d in range(2):
                            dve.wait_ge(fpe[d], t * PE_N + (10 + 2 * v) + 1)
                            if v == 0:
                                dve.wait_ge(fdve[d], t * DVE_N + 8)
                                dve.tensor_tensor(Ti[d][:], over(B.ident, H), Y[d][:], ALU.subtract).then_inc(own, step())
                                dve.tensor_tensor(TT[d][:], over(B.ident, H), pX[d][:], ALU.subtract).then_inc(own, step())
                            else:
                                if v < LEVELS - 1:
                                    dve.tensor_tensor(Ti[d][:], Ti[d][:], pY[d][:], ALU.subtract).then_inc(own, step())
                                dve.tensor_tensor(TT[d][:], TT[d][:], pX[d][:], ALU.subtract).then_inc(own, step())
                            dve.wait_ge(own, step.n)
                            dve.sem_inc(fdve[d], 1)
                    for d in range(2):
                        dve.wait_ge(fpe[d], t * PE_N + 25)
                        dve.tensor_copy(VN[d][:], bank(pY[d], 0)).then_inc(fdve[d], 1)
                    for d in range(2):
                        dve.wait_ge(fpe[d], t * PE_N + 26)
                        o = out[d][:, GQ:].rearrange("p (h e) -> p h e", e=GK)
                        dve.tensor_tensor(o, bank(pX[d], 0), heads(eg[d][:, 0, :], H, GK), ALU.mult).then_inc(own, step())
                        dve.tensor_tensor(s_d[d][:], s_d[d][:], heads(eg[d][0:GK, 1, :], H, GK), ALU.mult).then_inc(own, step())
                        dve.wait_ge(own, step.n)
                        dve.tensor_tensor(o, o, bank(pX[d], 1), ALU.add).then_inc(own, step())
                        dve.tensor_tensor(s_d[d][:], s_d[d][:], bank(pY[d], 1)[0:GK], ALU.add).then_inc(own, step())
                        dve.wait_ge(own, step.n)
                        dve.sem_inc(fdve[d], 1)
                    dve.wait_ge(own, step.n)
                    dve.sem_clear(own)
                    step.restart()
                turns(dve, body)


def mixer_output(nc, T, B, l):
    W3 = 768
    NH = W3 // GK
    with stage(nc, "mixer") as st:
        wout = st.sb("wout", [P, KD, D])
        wr = st.sb("wr", [P, KD, E_N])
        gain = st.sb("gain", [P, 2, GK])
        o = st.sb("o", [P, D])
        ob, z, ez = st.sb("ob", [P, W3]), st.sb("z", [P, W3]), st.sb("ez", [P, W3])
        ss = st.sb("ss", [P, NH])
        rs = st.sb("rs", [P, 2])
        oT = st.sb("oT", [P, KD, P])
        sq = st.sb("sq", [P, D])
        branch = st.sb("branch", [P, D])
        xhat = st.sb("xhat", [P, D])
        xT = st.sb("xT", [P, KD, P])
        mx, den = st.sb("mx", [P, 1]), st.sb("den", [P, 1])
        ex = st.sb("ex", [P, E_N])
        af = st.sb("af", [P, E_N])
        affT = st.sb("affT", [E_N, ROWS])
        tr, acc = st.ps("tr", [P, KD, P]), st.ps("acc", [P, D])
        lg, at = st.ps("lg", [P, 512]), st.ps("at", [P, 512])
        w_in, t_in, from_act, from_dve, from_pe, stored = (
            st.sem(x) for x in ("w_in", "t_in", "act_done", "dve_done", "pe_done", "stored"))
        asem, dsem = st.sem("act_steps"), st.sem("dve_steps")
        xT_done, aff_done = st.sem("xT_done"), st.sem("aff_done")
        NA, ND, NP_ = 6, 6, 5

        def turns(eng, body):
            body(0)
            with eng.Fori(1, TILES) as t:
                body(t)

        with st.block() as block:
            @block.sync
            def _(sp):
                for dst, src in ((wout[:], T["w_out"][l].rearrange("(k p) n -> p k n", p=P)),
                                 (wr[:], T["w_router"][l].rearrange("(k p) n -> p k n", p=P)),
                                 (gain[:, 0, :], T["gla_out_norm"][l].partition_broadcast(P)),
                                 (gain[:, 1, :], T["gdn_out_norm"][l].partition_broadcast(P))):
                    sp.dma_start(dst, src).then_inc(w_in, 16)

                def body(t):
                    if isinstance(t, int):
                        row, prow = 0, 1
                    else:
                        row, prow = sp.snap(t * P), sp.snap(t * P + 2)
                    sp.wait_ge(from_dve, t * ND + 1)
                    R, Q = bass.ds(row, P), bass.ds(prow, P)
                    for dst, src in ((o[:, 0:256], T["mla_out"][R, :]), (o[:, 256:], T["scan_f"][R, :]), (ob[:], T["scan_b"][R, :]),
                                     (z[:, 0:GQ], T["proj"][Q, C_GZ:C_DQ]), (z[:, GQ:], T["proj"][Q, C_DZ:C_DB])):
                        sp.dma_start(dst, src).then_inc(t_in, 16)
                    sp.wait_ge(from_dve, t * ND + 5)
                    sp.dma_start(T["xhat"][R, :], xhat[:]).then_inc(stored, 16)
                turns(sp, body)
                sp.wait_ge(from_dve, ND * TILES + 1)
                sp.dma_start(T["affT"], affT[:]).then_inc(stored, 16)
                sp.wait_ge(stored, 16 * TILES + 17)

            @block.scalar
            def _(act):
                own, step = asem, Steps()

                def rsqrt(x, n):
                    act.activation(x, x, ACT.Ln, bias=B.eps[:, 0:1], scale=1.0 / n).then_inc(own, step())
                    act.wait_ge(own, step.n)
                    return act.activation(x, x, ACT.Exp, scale=-0.5)

                def body(t):
                    act.wait_ge(t_in, t * 80 + 81)
                    act.activation(ez[:], z[:], ACT.Exp, scale=-1.0).then_inc(from_act, 1)
                    act.wait_ge(from_dve, t * ND + 2)
                    rsqrt(ss[:], GK).then_inc(from_act, 1)
                    act.wait_ge(from_pe, t * NP_ + 2)
                    act.activation(oT[:], tr[:], ACT.Copy).then_inc(from_act, 1)
                    act.wait_ge(from_pe, t * NP_ + 3)
                    act.activation(sq[:], acc[:], ACT.Square, accum_out=rs[:, 0:1]).then_inc(own, step())
                    act.wait_ge(own, step.n)
                    rsqrt(rs[:, 0:1], D).then_inc(from_act, 1)
                    act.wait_ge(from_dve, t * ND + 4)
                    act.activation(sq[:], B.x[:, t, :], ACT.Square, accum_out=rs[:, 1:2]).then_inc(own, step())
                    act.wait_ge(own, step.n)
                    rsqrt(rs[:, 1:2], D).then_inc(from_act, 1)
                    act.wait_ge(from_dve, t * ND + 6)
                    act.activation(ex[:], lg[:, 0:E_N], ACT.Exp, bias=mx[:, 0:1], accum_out=den[:]).then_inc(from_act, 1)
                    act.wait_ge(own, step.n)
                    act.sem_clear(own)
                    step.restart()
                turns(act, body)

            @block.tensor
            def _(pe):
                pe.wait_ge(w_in, 65)

                def body(t):
                    pe.wait_ge(from_dve, t * ND + 3)
                    for k in range(KD):
                        mm = pe.transpose(tr[:, k, :], o[:, k * P:(k + 1) * P], B.ident)
                    mm.then_inc(from_pe, 1)
                    pe.wait_ge(from_act, t * NA + 4)
                    for n in range(2):
                        for k in range(KD):
                            mm = pe.matmul(acc[:, n * 512:(n + 1) * 512], oT[:, k, :], wout[:, k, n * 512:(n + 1) * 512], start=k == 0, stop=k == KD - 1)
                    mm.then_inc(from_pe, 1)
                    pe.wait_ge(from_dve, t * ND + 5)
                    for k in range(KD):
                        mm = pe.transpose(tr[:, k, :], xhat[:, k * P:(k + 1) * P], B.ident)
                    mm.then_inc(from_pe, 1)
                    pe.wait_ge(xT_done, t + 2)
                    for k in range(KD):
                        mm = pe.matmul(lg[:, 0:E_N], xT[:, k, :], wr[:, k, :], start=k == 0, stop=k == KD - 1)
                    mm.then_inc(from_pe, 1)
                    pe.wait_ge(aff_done, t + 2)
                    pe.transpose(at[0:E_N, 0:P], af[:], B.ident).then_inc(from_pe, 1)
                turns(pe, body)

            @block.vector
            def _(dve):
                own, step = dsem, Steps()
                dve.wait_ge(w_in, 65)

                def body(t):
                    c = 0 if isinstance(t, int) else 1
                    dve.wait_ge(t_in, t * 80 + 81)
                    m = o[:, 256:]
                    mh = m.rearrange("p (h e) -> p h e", e=GK)
                    dve.tensor_tensor(m, m, ob[:], ALU.add).then_inc(own, step())
                    dve.wait_ge(own, step.n)
                    dve.tensor_tensor(ob[:], m, m, ALU.mult).then_inc(own, step())
                    dve.wait_ge(own, step.n)
                    dve.tensor_reduce(ss[:], ob[:].rearrange("p (h e) -> p h e", e=GK), AX.X, ALU.add).then_inc(from_dve, 1)
                    dve.wait_ge(from_act, t * NA + 2)
                    dve.tensor_scalar(ez[:], ez[:], 1.0, None, ALU.add).then_inc(own, step())
                    dve.wait_ge(own, step.n)
                    dve.reciprocal(ez[:], ez[:]).then_inc(own, step())
                    dve.wait_ge(own, step.n)
                    dve.tensor_tensor(z[:], z[:], ez[:], ALU.mult).then_inc(own, step())
                    dve.wait_ge(own, step.n)
                    dve.wait_ge(from_act, t * NA + 3)
                    dve.tensor_tensor(mh, mh, ss[:].unsqueeze(2).to_broadcast([P, NH, GK]), ALU.mult).then_inc(own, step())
                    dve.wait_ge(own, step.n)
                    dve.tensor_tensor(mh[:, 0:H_GLA], mh[:, 0:H_GLA], gain[:, 0:1, :].to_broadcast([P, H_GLA, GK]), ALU.mult).then_inc(own, step())
                    dve.tensor_tensor(mh[:, H_GLA:], mh[:, H_GLA:], gain[:, 1:2, :].to_broadcast([P, H_GDN, GK]), ALU.mult).then_inc(own, step())
                    dve.wait_ge(own, step.n)
                    dve.tensor_tensor(m, m, z[:], ALU.mult).then_inc(from_dve, 1)
                    dve.wait_ge(from_act, t * NA + 5)
                    dve.scalar_tensor_tensor(branch[:], acc[:], rs[:, 0:1], B.gate[:, 0, c, :], ALU.mult, ALU.mult).then_inc(own, step())
                    dve.wait_ge(own, step.n)
                    dve.tensor_tensor(B.x[:, t, :], B.x[:, t, :], branch[:], ALU.add).then_inc(from_dve, 1)
                    dve.wait_ge(from_act, t * NA + 6)
                    dve.wait_ge(stored, t * 16 + 1)
                    dve.tensor_scalar(xhat[:], B.x[:, t, :], rs[:, 1:2], None, ALU.mult).then_inc(from_dve, 1)
                    dve.wait_ge(from_pe, t * NP_ + 4)
                    for k in range(KD):
                        dve.tensor_scalar(xT[:, k, :], tr[:, k, :], B.scale[:, c, 1, k:k + 1], B.shift[:, c, 1, k:k + 1], ALU.mult, ALU.add).then_inc(own, step())
                    dve.wait_ge(own, step.n)
                    dve.sem_inc(xT_done, 1)
                    dve.wait_ge(from_pe, t * NP_ + 5)
                    dve.tensor_reduce(mx[:], lg[:, 0:E_N], AX.X, ALU.max).then_inc(own, step())
                    dve.wait_ge(own, step.n)
                    dve.tensor_scalar(mx[:], mx[:], -1.0, None, ALU.mult).then_inc(from_dve, 1)
                    dve.wait_ge(from_act, t * NA + 7)
                    dve.reciprocal(den[:], den[:]).then_inc(own, step())
                    dve.wait_ge(own, step.n)
                    dve.tensor_scalar(af[:], ex[:], den[:, 0:1], None, ALU.mult).then_inc(own, step())
                    dve.wait_ge(own, step.n)
                    dve.tensor_copy(B.aff[:, t, :], af[:]).then_inc(own, step())
                    dve.sem_inc(aff_done, 1)
                    dve.wait_ge(from_pe, t * NP_ + 6)
                    dve.tensor_copy(affT[:, bass.ds(t * P, P)], at[0:E_N, 0:P]).then_inc(own, step())
                    dve.wait_ge(own, step.n)
                    dve.sem_clear(own)
                    step.restart()
                    dve.sem_inc(from_dve, 1)
                turns(dve, body)


def experts(nc, T, B, l):
    with nc.sbuf_tensor("slot_token", [P, 2, E_N + 1], I32) as token, nc.sbuf_tensor("slot_gate", [P, 2, E_N], F32) as gate:
        route(nc, T, B, l, token, gate)
        expert_ffn(nc, T, B, l, token, gate)


def route(nc, T, B, l, token, gate):
    NT = TILES - 1
    with stage(nc, "route") as st:
        row = st.sb("row", [P, 2, ROWS])
        junk = st.sb("junk", [P, DEC])
        part = st.sb("part", [P, TILES, 3])
        rank = st.sb("rank", [P, TILES])
        sel = st.sb("sel", [P, TILES, P])
        pair = st.sb("pair", [P, TILES, 2])
        later = st.sb("later", [P, P])
        zeros = st.sb("zeros", [P, D])
        slot = st.ps("slot", [P, 2, 512])
        row_in, sel_done, picked, ranked, slot_done = (
            [st.sem("row_in0"), st.sem("row_in1")], st.sem("sel_done"), st.sem("picked"), st.sem("ranked"), st.sem("slot_done"))
        zeroed, cleared, dsem = st.sem("zeroed"), st.sem("cleared"), st.sem("dve_steps")
        with st.block() as block:
            @block.sync
            def _(sp):
                with sp.Fori(0, E_N // 2) as i:
                    es = [sp.snap(i * 2 + s) for s in range(2)]
                    for s in range(2):
                        sp.wait_ge(ranked, i * 2 + 1)
                        sp.dma_start(row[:, s, :], T["affT"][bass.ds(es[s], 1), :].to_broadcast([P, ROWS])).then_inc(row_in[s], 16)

            @block.gpsimd
            def _(pool):
                pool.memset(zeros[:], 0.0).then_inc(zeroed, 1)

            @block.scalar
            def _(act):
                act.wait_ge(zeroed, 2)
                for t in range(TILES):
                    act.dma_start(T["moe"][t * P:(t + 1) * P, :], zeros[:]).then_inc(cleared, 16)
                act.wait_ge(cleared, 16 * TILES + 1)

            @block.vector
            def _(dve):
                own, step = dsem, Steps()
                dve.memset(part[:], 0.0).then_inc(own, step())
                dve.wait_ge(own, step.n)
                dve.tensor_tensor(later[:], B.masks[:, 2, :], B.ident, ALU.subtract).then_inc(own, step())
                dve.tensor_copy(pair[:, :, 0], B.ids[:, 0:TILES]).then_inc(own, step())
                dve.memset(token[:, :, E_N:], 0).then_inc(own, step())
                dve.wait_ge(own, step.n)
                dve.sem_clear(own)
                step.restart()
                with dve.Fori(0, E_N // 2) as i:
                    for s in range(2):
                        e = i * 2 + s
                        dve.wait_ge(row_in[s], i * 16 + 17)
                        r = row[:, s, :]
                        dve.wait_ge(picked, e + 1)
                        dve.tensor_copy(pair[:, :, 1], B.aff[:, :, e]).then_inc(own, step())
                        dve.wait_ge(own, step.n)
                        for t in range(TILES):
                            mine = pair[:, t, 1:2]
                            lo, hi = (0, SEQ) if t == 0 else (SEQ, ROWS)
                            a, b = t * P, (t + 1) * P
                            if a > lo:
                                dve.tensor_scalar(junk[:, 0:a - lo], r[:, lo:a], mine, 0.0, ALU.is_ge, ALU.add, accum_out=part[:, t, 0:1]).then_inc(own, step())
                            dve.tensor_scalar(junk[:, a - lo:hi - lo], r[:, a:hi], mine, 0.0, ALU.is_gt, ALU.add, accum_out=part[:, t, 1:2]).then_inc(own, step())
                            dve.wait_ge(own, step.n)
                            dve.scalar_tensor_tensor(junk[:, 0:P], r[:, a:b], mine, later[:], ALU.is_equal, ALU.mult, accum_out=part[:, t, 2:3]).then_inc(own, step())
                            dve.wait_ge(own, step.n)
                        dve.tensor_reduce(rank[:], part[:], AX.X, ALU.add).then_inc(own, step())
                        dve.wait_ge(own, step.n)
                        dve.sem_inc(ranked, 1)
                        slots = B.ids[:, TILES:TILES + P].unsqueeze(1).to_broadcast([P, TILES, P])
                        dve.tensor_tensor(sel[:], slots, rank[:].unsqueeze(2).to_broadcast([P, TILES, P]), ALU.is_equal).then_inc(own, step())
                        dve.wait_ge(own, step.n)
                        dve.sem_inc(sel_done, 1)
                        dve.wait_ge(picked, e + 2)
                        dve.tensor_copy(token[:, 0, bass.ds(e, 1)], slot[:, 0, 0:1]).then_inc(own, step())
                        dve.tensor_copy(gate[:, 0, bass.ds(e, 1)], slot[:, 0, 1:2]).then_inc(own, step())
                        dve.tensor_copy(token[0:CAP_P, 1, bass.ds(e, 1)], slot[0:CAP_P, 1, 0:1]).then_inc(own, step())
                        dve.tensor_copy(gate[0:CAP_P, 1, bass.ds(e, 1)], slot[0:CAP_P, 1, 1:2]).then_inc(own, step())
                        dve.wait_ge(own, step.n)
                        dve.sem_clear(own)
                        step.restart()
                        dve.sem_inc(slot_done, 1)

            @block.tensor
            def _(pe):
                with pe.Fori(0, E_N) as e:
                    pe.wait_ge(sel_done, e + 2)
                    for t in range(1, TILES):
                        pe.matmul(slot[:, 0, 0:2], sel[:, t, :], pair[:, t, :], start=t == 1, stop=t == TILES - 1)
                    pe.matmul(slot[0:CAP_P, 1, 0:2], sel[:, 0, 0:CAP_P], pair[:, 0, :], start=True, stop=True).then_inc(picked, 1)


def expert_ffn(nc, T, B, l, token, gate):
    RING = 4
    PER_BANK = 512 // CAP
    with stage(nc, "ffn") as st:
        w1, w3, w2 = (st.sb(x, [P, RING, KD, P]) for x in ("w1", "w3", "w2"))
        xe, xp = st.sb("xe", [P, D]), st.sb("xp", [CAP_P, D])
        idx = st.sb("idx", [P, 2, 2], I32)
        gt = st.sb("gt", [P, 2])
        xT = st.sb("xT", [P, KD, CAP])
        en = st.sb("en", [P, CAP])
        hT = st.sb("hT", [P, 2, CAP])
        yT = st.sb("yT", [P, KD, CAP])
        ye, yp = st.sb("ye", [P, D]), st.sb("yp", [CAP_P, D])
        acc, hb = st.ps("acc", [P, 3, 512]), st.ps("hb", [P, 2, 512])
        tr, trp = st.ps("tr", [P, D]), st.ps("trp", [P, 512])
        w_in = [st.sem(f"w_in{i}") for i in range(RING)]
        w_used = [st.sem(f"w_used{i}") for i in range(RING)]
        idx_done, turned, xT_done, h_prod, exp_done, h_done, acc_done, yT_done, y_turned, y_done = (
            st.sem(x) for x in ("idx_done", "turned", "xT_done", "h_prod", "exp_done", "h_done", "acc_done",
                                "yT_done", "y_turned", "y_done"))
        dsem, passed = st.sem("dve_steps"), st.sem("passed")
        rows_added = st.sem("rows_added")
        gathered, scattered = B.gathered, B.scattered
        part = lambda c: acc[:, c // PER_BANK, (c % PER_BANK) * CAP:(c % PER_BANK + 1) * CAP]

        with st.block() as block:
            @block.sync
            def _(sp):
                with sp.Fori(0, E_N) as e:
                    for j in range(KF):
                        s = j % RING
                        sp.wait_ge(w_used[s], e * (KF // RING) + j // RING + 1)
                        c = slice(j * P, (j + 1) * P)
                        sp.dma_start(w1[:, s], T["w_e1"][l, bass.ds(e, 1), :, c].rearrange("a (k p) n -> p (a k) n", p=P)).then_inc(w_in[s], 16)
                        sp.dma_start(w3[:, s], T["w_e3"][l, bass.ds(e, 1), :, c].rearrange("a (k p) n -> p (a k) n", p=P)).then_inc(w_in[s], 16)
                        sp.dma_start(w2[:, s].rearrange("p k n -> p (k n)"), T["w_e2"][l, bass.ds(e, 1), c, :].rearrange("a p n -> p (a n)")).then_inc(w_in[s], 16)

            @block.gpsimd
            def _(pool):
                def gather(slot):
                    for dst, n, i in ((xe, P, 0), (xp, CAP_P, 1)):
                        at = bass.IndirectOffsetOnAxis(ap=idx[0:n, slot, i:i + 1].bitcast(U32), axis=0)
                        pool.indirect_dma_start(dst[:], None, T["xhat"], at).then_inc(gathered, 16)

                pool.wait_ge(idx_done, 2)
                gather(0)
                with pool.Fori(0, E_N // 2) as i:
                    for s in range(2):
                        e = i * 2 + s
                        pool.wait_ge(turned, e + 2)
                        pool.wait_ge(idx_done, e + 3)
                        pool.sem_inc(passed, 1)
                        gather(1 - s)
                        pool.wait_ge(y_done, e + 2)
                        pool.sem_inc(passed, 1)
                        for src, n, k in ((ye, P, 0), (yp, CAP_P, 1)):
                            at = bass.IndirectOffsetOnAxis(ap=idx[0:n, s, k:k + 1].bitcast(U32), axis=0)
                            pool.indirect_dma_start(T["moe"], at, src[:], None, compute_op=ALU.add).then_inc(scattered, 16)
                        pool.wait_ge(scattered, l * (E_N * 32) + (e * 32 + 32))
                        pool.sem_inc(rows_added, 1)
                pool.wait_ge(gathered, l * ((E_N + 1) * 32) + (E_N + 1) * 32)

            @block.tensor
            def _(pe):
                with pe.Fori(0, E_N) as e:
                    pe.wait_ge(gathered, l * ((E_N + 1) * 32) + (e * 32 + 32))
                    pe.wait_ge(y_done, e + 1)
                    for k in range(KD):
                        pe.transpose(tr[:, k * P:(k + 1) * P], xe[:, k * P:(k + 1) * P], B.ident)
                    for k in range(KD):
                        mm = pe.transpose(trp[:, k * CAP_P:(k + 1) * CAP_P], xp[:, k * P:(k + 1) * P], B.ident[0:CAP_P, 0:CAP_P])
                    mm.then_inc(turned, 1)
                    pe.wait_ge(xT_done, e + 2)

                    def up_products(j):
                        s, b = j % RING, j % 2
                        pe.wait_ge(w_in[s], (e * (KF // RING) + j // RING) * 48 + 49)
                        if j >= 2:
                            pe.wait_ge(h_done, e * KF + (j - 1) + 1)
                        for i, w in enumerate((w1, w3)):
                            for k in range(KD):
                                mm = pe.matmul(hb[:, b, i * CAP:(i + 1) * CAP], w[:, s, k, :], xT[:, k, :], start=k == 0, stop=k == KD - 1)
                        mm.then_inc(h_prod, 1)

                    def down_products(j):
                        s, b = j % RING, j % 2
                        pe.wait_ge(h_done, e * KF + (j + 1) + 1)
                        for c in range(KD):
                            mm = pe.matmul(part(c), w2[:, s, c, :], hT[:, b, :], start=j == 0 and c % PER_BANK == 0,
                                           stop=j == KF - 1, skip_group_check=True)
                        mm.then_inc(w_used[s], 1)
                    for j in range(KF):
                        up_products(j)
                        if j:
                            down_products(j - 1)
                    down_products(KF - 1)
                    pe.wait_ge(yT_done, e + 2)
                    for k in range(KD):
                        pe.transpose(tr[:, k * P:(k + 1) * P], yT[:, k, 0:CAP_S], B.ident)
                    for k in range(KD):
                        mm = pe.transpose(hb[0:CAP_P, k // 4, (k % 4) * P:(k % 4 + 1) * P], yT[:, k, CAP_S:], B.ident)
                    mm.then_inc(y_turned, 1)

            @block.scalar
            def _(act):
                with act.Fori(0, E_N) as e:
                    for j in range(KF):
                        act.wait_ge(h_prod, e * KF + (j + 1) + 1)
                        act.wait_ge(h_done, e * KF + j + 1)
                        act.activation(en[:], hb[:, j % 2, 0:CAP], ACT.Exp, scale=-1.0).then_inc(exp_done, 1)

            @block.vector
            def _(dve):
                own, step = dsem, Steps()

                def index(e, slot):
                    dve.tensor_copy(idx[:, slot, 0:1], token[:, 0, bass.ds(e, 1)]).then_inc(own, step())
                    dve.tensor_copy(idx[0:CAP_P, slot, 1:2], token[0:CAP_P, 1, bass.ds(e, 1)]).then_inc(own, step())
                    dve.wait_ge(own, step.n)
                    dve.sem_inc(idx_done, 1)

                index(0, 0)
                dve.wait_ge(own, step.n)
                dve.sem_clear(own)
                step.restart()

                def body(e, s):
                    dve.tensor_copy(gt[:, 0:1], gate[:, 0, bass.ds(e, 1)]).then_inc(own, step())
                    dve.tensor_copy(gt[0:CAP_P, 1:2], gate[0:CAP_P, 1, bass.ds(e, 1)]).then_inc(own, step())
                    dve.wait_ge(turned, e + 2)
                    for k in range(KD):
                        dve.tensor_scalar(xT[:, k, 0:CAP_S], tr[:, k * P:(k + 1) * P], B.scale[:, 1, 1, k:k + 1], B.shift[:, 1, 1, k:k + 1], ALU.mult, ALU.add).then_inc(own, step())
                    tp = trp[:, 0:KD * CAP_P].rearrange("p (k n) -> p k n", n=CAP_P)
                    sc, sh = (a[:, 0, 1, :].unsqueeze(2).to_broadcast([P, KD, CAP_P]) for a in (B.scale, B.shift))
                    dve.tensor_tensor(xT[:, :, CAP_S:], tp, sc, ALU.mult).then_inc(own, step())
                    dve.wait_ge(own, step.n)
                    dve.tensor_tensor(xT[:, :, CAP_S:], xT[:, :, CAP_S:], sh, ALU.add).then_inc(own, step())
                    dve.wait_ge(own, step.n)
                    dve.sem_inc(xT_done, 1)
                    for j in range(KF):
                        b = j % 2
                        if j == 2:
                            dve.wait_ge(rows_added, e + 1)
                            index(e + 1, 1 - s)
                        dve.wait_ge(exp_done, e * KF + (j + 1) + 1)
                        dve.tensor_scalar(en[:], en[:], 1.0, None, ALU.add).then_inc(own, step())
                        dve.wait_ge(own, step.n)
                        dve.reciprocal(en[:], en[:]).then_inc(own, step())
                        dve.wait_ge(own, step.n)
                        dve.tensor_tensor(en[:], en[:], hb[:, b, 0:CAP], ALU.mult).then_inc(own, step())
                        dve.wait_ge(own, step.n)
                        dve.tensor_tensor(hT[:, b, :], en[:], hb[:, b, CAP:2 * CAP], ALU.mult).then_inc(h_done, 1)
                    for s in range(RING):
                        dve.wait_ge(w_used[s], e * (KF // RING) + (KF // RING) + 1)
                    for b in range(3):
                        n = min(PER_BANK, KD - b * PER_BANK)
                        dve.tensor_copy(yT[:, b * PER_BANK:b * PER_BANK + n, :].rearrange("p k n -> p (k n)"), acc[:, b, 0:n * CAP]).then_inc(own, step())
                    dve.wait_ge(own, step.n)
                    dve.sem_inc(yT_done, 1)
                    dve.wait_ge(y_turned, e + 2)
                    dve.tensor_scalar(ye[:], tr[:], gt[:, 0:1], None, ALU.mult).then_inc(own, step())
                    dve.tensor_scalar(yp[:], hb[0:CAP_P].rearrange("p b n -> p (b n)"), gt[0:CAP_P, 1:2], None, ALU.mult).then_inc(own, step())
                    dve.wait_ge(own, step.n)
                    dve.sem_clear(own)
                    step.restart()
                    dve.sem_inc(y_done, 1)
                with dve.Fori(0, E_N // 2) as i:
                    for s in range(2):
                        body(i * 2 + s, s)


def expert_residual(nc, T, B, l):
    with stage(nc, "resid") as st:
        y = st.sb("y", [P, 2, D])
        sq = st.sb("sq", [P, D])
        rs = st.sb("rs", [P, 2])
        y_in, rs_done, added = [st.sem("y_in0"), st.sem("y_in1")], st.sem("rs_done"), st.sem("added")
        asem, dsem = st.sem("act_steps"), st.sem("dve_steps")
        with st.block() as block:
            @block.sync
            def _(sp):
                for t in range(TILES):
                    sp.wait_ge(added, t - 1 + 1)
                    sp.dma_start(y[:, t % 2], T["moe"][t * P:(t + 1) * P, :]).then_inc(y_in[t % 2], 16)

            @block.scalar
            def _(act):
                own, step = asem, Steps()
                for t in range(TILES):
                    r = rs[:, t % 2:t % 2 + 1]
                    act.wait_ge(y_in[t % 2], 16 * (t // 2 + 1) + 1)
                    act.activation(sq[:], y[:, t % 2], ACT.Square, accum_out=r).then_inc(own, step())
                    act.wait_ge(own, step.n)
                    act.activation(r, r, ACT.Ln, bias=B.eps[:, 0:1], scale=1.0 / D).then_inc(own, step())
                    act.wait_ge(own, step.n)
                    act.activation(r, r, ACT.Exp, scale=-0.5).then_inc(rs_done, 1)

            @block.vector
            def _(dve):
                own, step = dsem, Steps()
                for t in range(TILES):
                    dve.wait_ge(rs_done, t + 2)
                    yt = y[:, t % 2]
                    dve.scalar_tensor_tensor(yt, yt, rs[:, t % 2:t % 2 + 1], B.gate[:, 1, 1 if t else 0, :], ALU.mult, ALU.mult).then_inc(own, step())
                    dve.wait_ge(own, step.n)
                    dve.tensor_tensor(B.x[:, t, :], B.x[:, t, :], yt, ALU.add).then_inc(added, 1)


def store_outputs(nc, T, B):
    with stage(nc, "store") as st:
        stored = st.sem("stored")
        with st.block() as block:
            @block.sync
            def _(sp):
                sp.dma_start(T["y_prompt"][0], B.x[:, 0, :]).then_inc(stored, 16)
                sp.dma_start(T["y_sample"][0].rearrange("(t p) d -> p t d", p=P), B.x[:, 1:TILES, :]).then_inc(stored, 16)
                sp.wait_ge(stored, 33)


class Buffers:
    pass


def host_constants():
    j, i = np.arange(P)[:, None], np.arange(P)[None, :]
    up_f = (j <= i).astype(np.float32)
    up_b = (j >= i).astype(np.float32)
    m = [np.eye(P, dtype=np.float32), up_f, up_b,
         up_f - up_f[:, P // 2 - 1:P // 2], up_b - up_b[:, P // 2:P // 2 + 1]]
    for back in (0, 1):
        b = 1
        while b < P:
            lev = (j // (2 * b) == i // (2 * b)) & (i % (2 * b) >= b) & (j % (2 * b) < b)
            m.append((lev.T if back else lev).astype(np.float32))
            b *= 2
    masks = np.stack(m, 1)
    half = ROPE // 2
    freqs = (ROPE_BASE ** (-np.arange(0, half, 2, dtype=np.float32) / half)).astype(np.float32)
    t = np.arange(DEC)
    row, col = (t // GRID_W).astype(np.float32), (t % GRID_W).astype(np.float32)
    ang = np.concatenate([row[:, None] * freqs, col[:, None] * freqs], -1)
    rope = np.stack([np.cos(ang), np.sin(ang)], 1).astype(np.float32)
    rope = np.concatenate([np.stack([np.ones((P, half)), np.zeros((P, half))], 1).astype(np.float32), rope])
    rope = np.ascontiguousarray(rope.reshape(TILES, P, 2, half).transpose(1, 0, 2, 3))
    ids = np.zeros((P, TILES + P + 4), np.float32)
    ids[:, :TILES] = np.arange(ROWS).reshape(TILES, P).T
    ids[:, TILES:TILES + P] = np.arange(P)[None, :]
    ids[:, TILES + P:] = np.stack([up_f[:, P // 2 - 1], np.ones(P), up_b[:, P // 2], np.ones(P)], 1)
    return {"masks": masks, "rope": rope, "ids": ids}


OUTS = [("y_prompt", (1, SEQ, D)), ("y_sample", (1, DEC, D)), ("new_ckv", (1, DEPTH, SEQ, KVL)),
        ("new_krope", (1, DEPTH, SEQ, ROPE)), ("new_gla", (1, DEPTH, 2, H_GLA, GK, GK)),
        ("new_gdn", (1, DEPTH, 2, H_GDN, GK, GK))]
SCRATCH = [("mod", (2, 6 * D)), ("proj", (ROWS + 3, IN_DIM)), ("qkv", (ROWS, 3 * DQ)), ("gates", (ROWS, 32)),
           ("gla_la", (ROWS, 2 * GQ)), ("mla_out", (ROWS, 256)), ("scan_f", (ROWS, 768)), ("scan_b", (ROWS, 768)),
           ("xhat", (ROWS, D)), ("affT", (E_N, ROWS)), ("moe", (ROWS, D))]


def build(nc, T, last_stage=99):
    with ExitStack() as ctx:
        B = Buffers()
        sb = lambda n, s: ctx.enter_context(nc.sbuf_tensor(n, s, F32))
        B.gathered = ctx.enter_context(nc.semaphore("gathered"))
        B.scattered = ctx.enter_context(nc.semaphore("scattered"))
        B.x = sb("x_res", [P, TILES, D])
        B.masks = sb("masks_sb", [P, 19, P])
        B.ident = B.masks[:, 0, :]
        B.rope = sb("rope_sb", [P, TILES, 2, ROPE // 2])
        B.ids = sb("ids_sb", [P, TILES + P + 4])
        B.midcols = B.ids[:, TILES + P:]
        B.zero = sb("zero", [P, 32])
        B.ones = sb("ones", [P, P])
        B.eps = sb("eps", [P, 1])
        B.scale = sb("scale", [P, 2, 2, KD])
        B.shift = sb("shift", [P, 2, 2, KD])
        B.gate = sb("gate", [P, 2, 2, D])
        B.aff = sb("aff", [P, TILES, E_N])
        ctx.enter_context(nc.allow_non_contiguous_dma(reason="small tables are turned on the way in"))
        load_constants(nc, T, B)
        with nc.Fori(0, DEPTH if last_stage > 8 else 1) as l:
            modulation(nc, T, B, l)
            with nc.sbuf_tensor("xmT", [P, KD, ROWS], F32) as xmT:
                if last_stage > 0:
                    input_norm(nc, T, B, l, xmT)
                if last_stage > 1:
                    input_projection(nc, T, B, l, xmT)
            if last_stage > 2:
                latent_attention(nc, T, B, l)
            if last_stage > 3:
                scan_inputs(nc, T, B, l)
            if last_stage > 4:
                scan(nc, T, B, l, True)
                scan(nc, T, B, l, False)
            if last_stage > 5:
                mixer_output(nc, T, B, l)
            if last_stage > 6:
                experts(nc, T, B, l)
            if last_stage > 7:
                expert_residual(nc, T, B, l)
        store_outputs(nc, T, B)


def kernel(**inputs):
    import concourse.bacc as bacc
    from concourse.bass_utils import run_bass_kernel_spmd

    nc = bacc.Bacc("TRN2", target_bir_lowering=False, num_devices=1)
    arrays, T = {}, {}
    for name, a in {**inputs, **host_constants()}.items():
        arrays[f"in_{name}"] = np.ascontiguousarray(a)
        T[name] = nc.dram_tensor(f"in_{name}", arrays[f"in_{name}"].shape, F32, kind="ExternalInput").ap()
    for name, shape in OUTS:
        T[name] = nc.dram_tensor(f"out_{name}", shape, F32, kind="ExternalOutput").ap()
    for name, shape in SCRATCH:
        T[name] = nc.dram_tensor(f"scratch_{name}", shape, F32, kind="Internal").ap()
    build(nc, T)
    r = run_bass_kernel_spmd(nc, [arrays], core_ids=[0])
    return tuple(r.results[0][f"out_{name}"] for name, _ in OUTS)
```

```python
from contextlib import ExitStack, contextmanager

import numpy as np
import concourse.bass as bass
from concourse import mybir

F32 = mybir.dt.float32
I32 = mybir.dt.int32
U32 = mybir.dt.uint32
ALU = mybir.AluOpType
ACT = mybir.ActivationFunctionType
AX = mybir.AxisListType

P = 128
D = 1024
KD = D // P
DEPTH = 2
SEQ = 128
DEC = 1024
PAST = 128
ROWS = SEQ + DEC
TILES = ROWS // P
EPS = 1e-6
GRID_W = 64
H_MLA, NOPE, ROPE, VD = 4, 64, 32, 64
QL, KVL = 256, 128
QD = NOPE + ROPE
MLA_SCALE = float(NOPE + ROPE) ** -0.5
ROPE_BASE = 10000.0
H_GLA, GK = 4, 64
RANK = 16
TAU = 16.0
H_GDN = 8
GQ = H_GLA * GK
DQ = H_GDN * GK
IN_DIM = 3552
C_QLAT, C_KVLAT, C_KROPE = 0, 256, 384
C_GQ, C_GK, C_GV, C_GLR, C_GZ = 416, 672, 928, 1184, 1216
C_DQ, C_DK, C_DV, C_DZ, C_DB, C_DA = 1472, 1984, 2496, 3008, 3520, 3536
E_N = 16
FF = 1024
KF = FF // P
CAP_S = 2 * DEC // E_N
CAP_P = 2 * SEQ // E_N
CAP = CAP_S + CAP_P
NEG = -1e30


class Steps:

    def __init__(self):
        self.count = 0

    def __call__(self):
        self.count += 1
        return 1

    @property
    def n(self):
        assert self.count > 0
        return self.count

    def restart(self):
        self.count = 0


class Stage:
    def __init__(self, nc, name, ctx):
        self.nc, self.name, self.ctx, self.sems = nc, name, ctx, []

    def sb(self, name, shape, dt=F32):
        return self.ctx.enter_context(self.nc.sbuf_tensor(f"{self.name}_{name}", shape, dt))

    def ps(self, name, shape, dt=F32):
        return self.ctx.enter_context(self.nc.psum_tensor(f"{self.name}_{name}", shape, dt))

    def sem(self, name):
        s = self.ctx.enter_context(self.nc.semaphore(f"{self.name}_{name}"))
        self.sems.append(s)
        if not name.endswith("_steps"):
            self.nc.gpsimd.sem_inc(s, 1)
        return s

    def block(self):
        self.nc.all_engine_barrier()
        return self.nc.Block()


@contextmanager
def stage(nc, name):
    with ExitStack() as ctx:
        st = Stage(nc, name, ctx)
        yield st
        for s in st.sems:
            nc.gpsimd.sem_clear(s)
        nc.all_engine_barrier()


def bc(ap, shape):
    return ap.to_broadcast(shape)


class Turns:

    def __init__(self, base):
        self.base, self.n = base, 0

    def next(self):
        self.n += 1
        return self.base + (self.n + 1)


def load_constants(nc, T, B):
    with stage(nc, "init") as st:
        loaded, zeroed, stored = st.sem("loaded"), st.sem("zeroed"), st.sem("stored")
        with st.block() as block:
            @block.vector
            def _(dve):
                dve.memset(B.zero[:], 0.0).then_inc(zeroed, 1)
                dve.memset(B.ones[:], 1.0).then_inc(zeroed, 1)
                dve.memset(B.eps[:], EPS).then_inc(zeroed, 1)

            @block.sync
            def _(sp):
                n = 0
                for dst, src in ((B.masks[:], T["masks"]), (B.rope[:], T["rope"]), (B.ids[:], T["ids"]),
                                 (B.x[:, 0, :], T["x_prompt"][0]),
                                 (B.x[:, 1:TILES, :], T["x_sample"][0].rearrange("(t p) d -> p t d", p=P))):
                    sp.dma_start(dst, src).then_inc(loaded, 16)
                    n += 16
                sp.wait_ge(zeroed, 4)
                for row in (0, 1 + SEQ, 2 + ROWS):
                    sp.dma_start(T["proj"][row, :].rearrange("(p c) -> p c", c=32), B.zero[0:IN_DIM // 32, :]).then_inc(stored, 16)
                sp.wait_ge(loaded, n + 1)
                sp.wait_ge(stored, 49)


def modulation(nc, T, B, l):
    NB = 512
    with stage(nc, "mod") as st:
        cond = st.sb("cond", [P, 2, KD])
        e = st.sb("e", [P, 2, KD])
        w = st.sb("w", [P, 2, KD, NB])
        row = st.sb("row", [2, 6 * D])
        bias = st.sb("bias", [2, 6 * D])
        colT = st.sb("colT", [P, 2, 4, KD])
        gainT = st.sb("gainT", [P, 2, KD])
        gain = st.sb("gain", [P, 2, D])
        acc = st.ps("acc", [P, 2, 512])
        cond_in, w_in = st.sem("cond_in"), [st.sem("w_in0"), st.sem("w_in1")]
        exp_done, silu_done, prod_done = (st.sem(x) for x in ("exp_done", "silu_done", "prod_done"))
        row_done = [st.sem("row_done0"), st.sem("row_done1")]
        row_out, table_in, step_sem = st.sem("row_out"), st.sem("table_in"), st.sem("dve_steps")
        with st.block() as block:
            @block.sync
            def _(sp):
                sp.dma_start(cond[:, 0, :], T["c_ctx"].rearrange("(k p) -> p k", p=P)).then_inc(cond_in, 16)
                sp.dma_start(cond[:, 1, :], T["c"][0].rearrange("(k p) -> p k", p=P)).then_inc(cond_in, 16)
                sp.dma_start(bias[:], T["b_mod"][l].partition_broadcast(2)).then_inc(cond_in, 16)
                wsrc = T["w_mod"].rearrange("l (k p) n -> l p k n", p=P)
                with sp.Fori(0, 6) as n:
                    col = sp.snap(n * (2 * NB))
                    for s in range(2):
                        sp.wait_ge(row_done[s], n + 1)
                        sp.dma_start(w[:, s], wsrc[l, :, :, bass.ds(col + s * NB, NB)]).then_inc(w_in[s], 16)
                for s in range(2):
                    sp.wait_ge(row_done[s], 7)
                sp.dma_start(T["mod"], row[:]).then_inc(row_out, 16)
                sp.wait_ge(row_out, 17)
                n = 0
                for c in range(2):
                    for i, j in enumerate((0, 1, 3, 4)):
                        sp.dma_start(colT[:, c, i, :], T["mod"][c, j * D:(j + 1) * D].rearrange("(k p) -> p k", p=P)).then_inc(table_in, 16)
                    for i, j in enumerate((2, 5)):
                        sp.dma_start(B.gate[:, i, c, :], T["mod"][c, j * D:(j + 1) * D].partition_broadcast(P)).then_inc(table_in, 16)
                for i in range(2):
                    sp.dma_start(gainT[:, i, :], T["sandwich_norms"][l, 2 * i].rearrange("(k p) -> p k", p=P)).then_inc(table_in, 16)
                    sp.dma_start(gain[:, i, :], T["sandwich_norms"][l, 2 * i + 1].partition_broadcast(P)).then_inc(table_in, 16)

            @block.scalar
            def _(act):
                act.wait_ge(cond_in, 49)
                act.activation(e[:], cond[:], ACT.Exp, scale=-1.0).then_inc(exp_done, 1)

            @block.tensor
            def _(pe):
                pe.wait_ge(silu_done, 2)
                with pe.Fori(0, 6) as n:
                    for s in range(2):
                        pe.wait_ge(w_in[s], n * 16 + 17)
                        pe.wait_ge(row_done[s], n + 1)
                        for k in range(KD):
                            mm = pe.matmul(acc[0:2, s, :], e[:, :, k], w[:, s, k, :], start=k == 0, stop=k == KD - 1)
                        mm.then_inc(prod_done, 1)

            @block.vector
            def _(dve):
                own, step = step_sem, Steps()
                dve.wait_ge(exp_done, 2)
                dve.tensor_scalar(e[:], e[:], 1.0, None, ALU.add).then_inc(own, step())
                dve.wait_ge(own, step.n)
                dve.reciprocal(e[:], e[:]).then_inc(own, step())
                dve.wait_ge(own, step.n)
                dve.tensor_tensor(e[:], e[:], cond[:], ALU.mult).then_inc(silu_done, 1)
                for n in range(12):
                    dve.wait_ge(prod_done, n + 2)
                    c = slice(n * NB, (n + 1) * NB)
                    dve.tensor_tensor(row[:, c], acc[0:2, n % 2, :], bias[:, c], ALU.add).then_inc(row_done[n % 2], 1)
                dve.wait_ge(table_in, 16 * 16 + 1)
                for c in range(2):
                    for i in range(2):
                        dve.scalar_tensor_tensor(B.scale[:, c, i, :], colT[:, c, 2 * i + 1, :], 1.0, gainT[:, i, :], ALU.add, ALU.mult).then_inc(own, step())
                        dve.tensor_copy(B.shift[:, c, i, :], colT[:, c, 2 * i, :]).then_inc(own, step())
                        dve.tensor_tensor(B.gate[:, i, c, :], B.gate[:, i, c, :], gain[:, i, :], ALU.mult).then_inc(own, step())
                dve.wait_ge(own, step.n)


def input_norm(nc, T, B, l, xmT):
    with stage(nc, "norm") as st:
        sq = st.sb("sq", [P, D])
        ss = st.sb("ss", [P, 1])
        xhat = st.sb("xhat", [P, D])
        tr = st.ps("tr", [P, KD, P])
        rs_done, xhat_done, tr_done, ev_done = (st.sem(x) for x in ("rs_done", "xhat_done", "tr_done", "ev_done"))
        act_steps, dve_steps = st.sem("act_steps"), st.sem("dve_steps")
        with st.block() as block:
            @block.scalar
            def _(act):
                own, step = act_steps, Steps()

                def body(t):
                    act.wait_ge(xhat_done, t + 1)
                    act.activation(sq[:], B.x[:, t, :], ACT.Square, accum_out=ss[:]).then_inc(own, step())
                    act.wait_ge(own, step.n)
                    act.activation(ss[:], ss[:], ACT.Ln, bias=B.eps[:, 0:1], scale=1.0 / D).then_inc(own, step())
                    act.wait_ge(own, step.n)
                    act.activation(ss[:], ss[:], ACT.Exp, scale=-0.5).then_inc(rs_done, 1)
                    act.wait_ge(own, step.n)
                    act.sem_clear(own)
                    step.restart()
                with act.Fori(0, TILES) as t:
                    body(t)

            @block.vector
            def _(dve):
                own, step = dve_steps, Steps()

                def body(t, c):
                    dve.wait_ge(rs_done, t + 2)
                    dve.tensor_scalar(xhat[:], B.x[:, t, :], ss[:, 0:1], None, ALU.mult).then_inc(xhat_done, 1)
                    dve.wait_ge(tr_done, t + 2)
                    for k in range(KD):
                        dve.tensor_scalar(xmT[:, k, bass.ds(t * P, P)], tr[:, k, :], B.scale[:, c, 0, k:k + 1],
                                               B.shift[:, c, 0, k:k + 1], ALU.mult, ALU.add).then_inc(own, step())
                    dve.wait_ge(own, step.n)
                    dve.sem_clear(own)
                    step.restart()
                body(0, 0)
                with dve.Fori(1, TILES) as t:
                    body(t, 1)

            @block.tensor
            def _(pe):
                with pe.Fori(0, TILES) as t:
                    pe.wait_ge(xhat_done, t + 2)
                    for k in range(KD):
                        mm = pe.transpose(tr[:, k, :], xhat[:, k * P:(k + 1) * P], B.ident)
                    mm.then_inc(tr_done, 1)


def proj_row(t):
    return 1 if isinstance(t, int) and t == 0 else t * P + 2


def input_projection(nc, T, B, l, xmT):
    NB = IN_DIM // 8
    BANKS = 3
    with stage(nc, "proj") as st:
        w = st.sb("w", [P, 2, KD, NB])
        out = st.sb("out", [P, BANKS, NB])
        acc = st.ps("acc", [P, BANKS, 512])
        w_in = [st.sem("w_in0"), st.sem("w_in1")]
        w_used = [st.sem("w_used0"), st.sem("w_used1")]
        prod_done, copied = st.sem("prod_done"), st.sem("copied")
        stored = [st.sem(f"stored{i}") for i in range(BANKS)]
        with st.block() as block:
            @block.sync
            def _(sp):
                wsrc = T["w_in"].rearrange("l (k p) n -> l p k n", p=P)
                with sp.Fori(0, 4) as n:
                    for s in range(2):
                        col = sp.snap(n * (2 * NB) + s * NB)
                        sp.wait_ge(w_used[s], n + 1)
                        sp.dma_start(w[:, s], wsrc[l, :, :, bass.ds(col, NB)]).then_inc(w_in[s], 16)

            @block.tensor
            def _(pe):
                with pe.Fori(0, 4) as n:
                    for s in range(2):
                        pe.wait_ge(w_in[s], n * 16 + 17)
                        for t in range(TILES):
                            i = s * TILES + t
                            b = i % BANKS
                            if i >= BANKS:
                                pe.wait_ge(copied, n * (2 * TILES) + (i - BANKS + 1) + 1)
                            else:
                                pe.wait_ge(copied, n * (2 * TILES) + 1)
                            for k in range(KD):
                                mm = pe.matmul(acc[:, b, 0:NB], xmT[:, k, t * P:(t + 1) * P], w[:, s, k, :],
                                               start=k == 0, stop=k == KD - 1)
                            mm.then_inc(prod_done, 1)

            @block.vector
            def _(dve):
                with dve.Fori(0, 4) as n:
                    for i in range(2 * TILES):
                        b = i % BANKS
                        dve.wait_ge(prod_done, n * (2 * TILES) + (i + 1) + 1)
                        dve.wait_ge(stored[b], n * (16 * 2 * TILES // BANKS) + 16 * (i // BANKS) + 1)
                        if i % TILES == TILES - 1:
                            dve.sem_inc(w_used[i // TILES], 1)
                        dve.tensor_copy(out[:, b, :], acc[:, b, 0:NB]).then_inc(copied, 1)

            @block.scalar
            def _(act):
                with act.Fori(0, 4) as n:
                    for i in range(2 * TILES):
                        b, s, t = i % BANKS, i // TILES, i % TILES
                        r = proj_row(t)
                        col = act.snap(n * (2 * NB) + s * NB)
                        act.wait_ge(copied, n * (2 * TILES) + (i + 1) + 1)
                        act.dma_start(T["proj"][r:r + P, bass.ds(col, NB)], out[:, b, :]).then_inc(stored[b], 16)
                for b in range(BANKS):
                    act.wait_ge(stored[b], 4 * 16 * 2 * TILES // BANKS + 1)


def rotate(own, step, dve, out, x, cos, sin, tmp):
    x1, x2 = x[..., 0::2], x[..., 1::2]
    dve.tensor_tensor(tmp[0], x1, cos, ALU.mult).then_inc(own, step())
    dve.tensor_tensor(tmp[1], x2, sin, ALU.mult).then_inc(own, step())
    dve.tensor_tensor(tmp[2], x1, sin, ALU.mult).then_inc(own, step())
    dve.tensor_tensor(tmp[3], x2, cos, ALU.mult).then_inc(own, step())
    dve.wait_ge(own, step.n)
    dve.tensor_tensor(out[..., 0::2], tmp[0], tmp[1], ALU.subtract).then_inc(own, step())
    dve.tensor_tensor(out[..., 1::2], tmp[2], tmp[3], ALU.add).then_inc(own, step())


def latent_attention(nc, T, B, l):
    with nc.sbuf_tensor("keysT", [P, H_MLA, 10 * P], F32) as keysT, nc.sbuf_tensor("values", [P, 10, H_MLA, VD], F32) as values:
        latent_keys(nc, T, B, l, keysT, values)
        attend(nc, T, B, l, keysT, values, True)
        attend(nc, T, B, l, keysT, values, False)


def latent_keys(nc, T, B, l, keysT, values):
    with stage(nc, "keys") as st:
        kin = st.sb("kin", [P, KVL + ROPE])
        ckv = st.sb("ckv", [P, KVL])
        ckvT = st.sb("ckvT", [P, P])
        ka = st.sb("ka", [P, H_MLA, P])
        kr = st.sb("kr", [P, ROPE])
        tmp = st.sb("tmp", [P, 4, ROPE // 2])
        sq = st.sb("sq", [P, KVL])
        rs = st.sb("rs", [P, 1])
        gain = st.sb("gain", [P, KVL])
        wkv = st.sb("wkv", [P, 512])
        tr, kv, trk = st.ps("tr", [P, 512]), st.ps("kv", [P, 512]), st.ps("trk", [P, H_MLA, P])
        w_in, k_in, rs_done, to_pe, from_pe, turn_done, stored = (
            st.sem(x) for x in ("w_in", "k_in", "rs_done", "to_pe", "from_pe", "turn_done", "stored"))
        asem, dsem = st.sem("act_steps"), st.sem("dve_steps")

        def turns(eng, body):
            body(0, "prompt")
            body(1, "context")
            with eng.Fori(2, 10) as s:
                body(s, "sample")

        with st.block() as block:
            @block.sync
            def _(sp):
                sp.dma_start(wkv[:], T["mla_wkv_b"][l]).then_inc(w_in, 16)
                sp.dma_start(gain[:], T["mla_kv_norm"][l].partition_broadcast(P)).then_inc(w_in, 16)

                def body(s, kind):
                    if kind == "sample":
                        r = sp.snap(s * P - (P - 2))
                    sp.wait_ge(turn_done, s + 1)
                    if kind == "context":
                        sp.dma_start(kin[:, 0:KVL], T["cache_ckv"][0, l]).then_inc(k_in, 16)
                        sp.dma_start(kin[:, KVL:], T["cache_krope"][0, l]).then_inc(k_in, 16)
                    else:
                        src = T["proj"][1:1 + P] if kind == "prompt" else T["proj"][bass.ds(r, P)]
                        sp.dma_start(kin[:, 0:KVL], src[:, C_KVLAT:C_KROPE]).then_inc(k_in, 16)
                        sp.dma_start(kin[:, KVL:], src[:, C_KROPE:C_GQ]).then_inc(k_in, 16)
                    if kind == "prompt":
                        sp.wait_ge(to_pe, 2)
                        sp.dma_start(T["new_ckv"][0, l], ckv[:]).then_inc(stored, 16)
                        sp.dma_start(T["new_krope"][0, l], kin[:, KVL:]).then_inc(stored, 16)
                        sp.wait_ge(stored, 33)
                turns(sp, body)

            @block.scalar
            def _(act):
                own, step = asem, Steps()

                def body(s, kind):
                    act.wait_ge(k_in, s * 32 + 33)
                    act.activation(sq[:], kin[:, 0:KVL], ACT.Square, accum_out=rs[:]).then_inc(own, step())
                    act.wait_ge(own, step.n)
                    act.activation(rs[:], rs[:], ACT.Ln, bias=B.eps[:, 0:1], scale=1.0 / KVL).then_inc(own, step())
                    act.wait_ge(own, step.n)
                    act.activation(rs[:], rs[:], ACT.Exp, scale=-0.5).then_inc(rs_done, 1)
                    act.wait_ge(own, step.n)
                    act.sem_clear(own)
                    step.restart()
                    act.wait_ge(turn_done, s + 2)
                turns(act, body)

            @block.tensor
            def _(pe):
                pe.wait_ge(w_in, 33)

                def body(s, kind):
                    op = Turns(s * 3)
                    pe.wait_ge(to_pe, op.next())
                    pe.transpose(tr[:, 0:P], ckv[:], B.ident).then_inc(from_pe, 1)
                    pe.wait_ge(to_pe, op.next())
                    pe.matmul(kv[:], ckvT[:], wkv[:], start=True, stop=True).then_inc(from_pe, 1)
                    pe.wait_ge(to_pe, op.next())
                    for h in range(H_MLA):
                        mm = pe.transpose(trk[:, h, :], ka[:, h, :], B.ident)
                    mm.then_inc(from_pe, 1)
                turns(pe, body)

            @block.vector
            def _(dve):
                own, step = dsem, Steps()
                dve.memset(ka[:], 0.0).then_inc(own, step())
                dve.wait_ge(own, step.n)
                dve.wait_ge(own, step.n)
                dve.sem_clear(own)
                step.restart()
                dve.wait_ge(w_in, 33)

                def body(s, kind):
                    pr = Turns(s * 3)
                    dve.wait_ge(rs_done, s + 2)
                    if kind == "prompt":
                        pass
                    if kind == "context":
                        dve.wait_ge(stored, 33)
                        dve.tensor_copy(ckv[:], kin[:, 0:KVL]).then_inc(to_pe, 1)
                    else:
                        dve.scalar_tensor_tensor(ckv[:], kin[:, 0:KVL], rs[:, 0:1], gain[:], ALU.mult, ALU.mult).then_inc(to_pe, 1)
                    dve.wait_ge(from_pe, pr.next())
                    dve.tensor_copy(ckvT[:], tr[:, 0:P]).then_inc(to_pe, 1)
                    raw = kin[:, KVL:]
                    if kind == "sample":
                        rotate(own, step, dve, kr[:], raw, B.rope[:, s - 1, 0, :], B.rope[:, s - 1, 1, :], [tmp[:, i, :] for i in range(4)])
                        dve.wait_ge(own, step.n)
                        if True:
                            dve.tensor_copy(ka[:, :, NOPE:QD], kr[:].unsqueeze(1).to_broadcast([P, H_MLA, ROPE])).then_inc(own, step())
                            dve.memset(ka[:, :, QD:P], 0.0).then_inc(own, step())
                    else:
                        dve.tensor_copy(ka[:, :, QD:P], raw.unsqueeze(1).to_broadcast([P, H_MLA, ROPE])).then_inc(own, step())
                    dve.wait_ge(from_pe, pr.next())
                    kvh = kv[:].rearrange("p (h e) -> p h e", h=H_MLA)
                    dve.tensor_copy(ka[:, :, 0:NOPE], kvh[:, :, 0:NOPE]).then_inc(own, step())
                    dve.tensor_copy(values[:, s, :, :], kvh[:, :, NOPE:]).then_inc(own, step())
                    dve.wait_ge(own, step.n)
                    dve.sem_inc(to_pe, 1)
                    dve.wait_ge(from_pe, pr.next())
                    dve.tensor_copy(keysT[:, :, bass.ds(s * P, P)], trk[:]).then_inc(own, step())
                    dve.wait_ge(own, step.n)
                    dve.wait_ge(own, step.n)
                    dve.sem_clear(own)
                    step.restart()
                    dve.sem_inc(turn_done, 1)
                turns(dve, body)


def attend(nc, T, B, l, keysT, values, prompt):
    NK = 1 if prompt else 9
    K0 = 0 if prompt else 1
    W = NK * P
    with stage(nc, "attp" if prompt else "atts") as st:
        qin = st.sb("qin", [P, QL])
        sq = st.sb("sq", [P, QL])
        rs = st.sb("rs", [P, 1])
        qlT = st.sb("qlT", [P, 2, P])
        q = st.sb("q", [P, H_MLA, QD])
        qa = st.sb("qa", [P, H_MLA, P])
        qaT = st.sb("qaT", [P, 2, H_MLA, P])
        tmp = st.sb("tmp", [P, 4, H_MLA, ROPE // 2])
        gainT = st.sb("gainT", [P, 2])
        wq = st.sb("wq", [P, 2, H_MLA * QD])
        prob = st.sb("prob", [P, 2, W])
        probT = st.sb("probT", [P, 2, W])
        mx = st.sb("mx", [P, H_MLA])
        den = st.sb("den", [P, H_MLA])
        out = st.sb("out", [P, 2, H_MLA, VD])
        score, turned = st.ps("score", [P, 1536]), st.ps("turned", [P, 1536])
        misc, acc = st.ps("misc", [P, 512]), st.ps("acc", [P, 512])
        w_in, q_in, rs_done, q_ready, q_prod = (st.sem(x) for x in ("w_in", "q_in", "rs_done", "q_ready", "q_prod"))
        score_done, max_done, exp_done, turn_done, probT_done, pv_done, out_done = (st.sem(x) for x in (
            "score_done", "max_done", "exp_done", "turn_done", "probT_done", "pv_done", "out_done"))
        stored = [st.sem("stored0"), st.sem("stored1")]
        asem, dsem = st.sem("act_steps"), st.sem("dve_steps")
        N = 1 if prompt else TILES - 1

        def turns(eng, body):
            if prompt:
                body(0, 0)
            else:
                with eng.Fori(0, N // 2 - 1) as j:
                    for s in range(2):
                        body(j * 2 + s, s)
                body(N - 2, 0)
                body(N - 1, 1)

        def more(i):
            return not isinstance(i, int) or i + 1 < N

        with st.block() as block:
            @block.sync
            def _(sp):
                sp.dma_start(wq[:], T["mla_wq_b"][l].rearrange("(k p) n -> p k n", p=P)).then_inc(w_in, 16)
                sp.dma_start(gainT[:], T["mla_q_norm"][l].rearrange("(k p) -> p k", p=P)).then_inc(w_in, 16)

                def load(r, queries_before):
                    sp.wait_ge(q_prod, queries_before)
                    sp.dma_start(qin[:], T["proj"][bass.ds(r, P), 0:QL]).then_inc(q_in, 16)
                load(proj_row(0 if prompt else 1), 1)

                def body(i, s):
                    fixed = (lambda x: x) if isinstance(i, int) else sp.snap
                    row = 0 if prompt else fixed(i * P + P)
                    tile_written = fixed(i + 2)
                    if more(i):
                        load(fixed(i * P + (2 * P + 2)), fixed(i * 3 + 4))
                    sp.wait_ge(out_done, tile_written)
                    sp.dma_start(T["mla_out"][bass.ds(row, P), :], out[:, s].rearrange("p h e -> p (h e)")).then_inc(stored[s], 16)
                turns(sp, body)
                for s in range(1 if prompt else 2):
                    sp.wait_ge(stored[s], 16 * (1 if prompt else N // 2) + 1)

            @block.scalar
            def _(act):
                own, step = asem, Steps()

                def norm(i):
                    act.wait_ge(q_in, i * 16 + 17)
                    act.activation(sq[:], qin[:], ACT.Square, accum_out=rs[:]).then_inc(own, step())
                    act.wait_ge(own, step.n)
                    act.activation(rs[:], rs[:], ACT.Ln, bias=B.eps[:, 0:1], scale=1.0 / QL).then_inc(own, step())
                    act.wait_ge(own, step.n)
                    act.activation(rs[:], rs[:], ACT.Exp, scale=-0.5).then_inc(rs_done, 1)
                norm(0)
                act.sem_clear(own)
                step.restart()

                def body(i, s):
                    for h in range(H_MLA):
                        act.wait_ge(max_done, i * H_MLA + h + 2)
                        act.activation(prob[:, h % 2, :], score[:, 0:W], ACT.Exp, bias=mx[:, h:h + 1], scale=MLA_SCALE,
                                       accum_out=den[:, h:h + 1]).then_inc(exp_done, 1)
                        if h == 0 and more(i):
                            norm(i + 1)
                            act.sem_clear(own)
                            step.restart()
                turns(act, body)

            @block.tensor
            def _(pe):
                pe.wait_ge(w_in, 33)

                def turn_latent(i):
                    pe.wait_ge(q_in, i * 16 + 17)
                    pe.wait_ge(q_ready, i * 3 + 1)
                    for k in range(2):
                        mm = pe.transpose(misc[:, k * P:(k + 1) * P], qin[:, k * P:(k + 1) * P], B.ident)
                    mm.then_inc(q_prod, 1)

                def project(i):
                    pe.wait_ge(q_ready, i * 3 + 2)
                    for k in range(2):
                        mm = pe.matmul(misc[:, 0:H_MLA * QD], qlT[:, k, :], wq[:, k, :], start=k == 0, stop=k == 1)
                    mm.then_inc(q_prod, 1)

                def turn_queries(i):
                    pe.wait_ge(q_ready, i * 3 + 3)
                    for h in range(H_MLA):
                        mm = pe.transpose(misc[:, h * P:(h + 1) * P], qa[:, h, :], B.ident)
                    mm.then_inc(q_prod, 1)
                turn_latent(0)
                project(0)
                turn_queries(0)

                def body(i, s):
                    def scores(h):
                        pe.wait_ge(exp_done, i * H_MLA + h + 1)
                        for c in range(0, W, 512):
                            n = min(512, W - c)
                            mm = pe.matmul(score[:, c:c + n], qaT[:, s, h, :], keysT[:, h, K0 * P + c:K0 * P + c + n], start=True, stop=True)
                        mm.then_inc(score_done, 1)
                    pe.wait_ge(q_ready, i * 3 + 4)
                    scores(0)
                    for h in range(H_MLA):
                        if h + 1 < H_MLA:
                            scores(h + 1)
                        if more(i) and h < 3:
                            (turn_latent, project, turn_queries)[h](i + 1)
                        pe.wait_ge(exp_done, i * H_MLA + h + 2)
                        pe.wait_ge(probT_done, i * H_MLA + h + 1)
                        for k in range(NK):
                            mm = pe.transpose(turned[:, k * P:(k + 1) * P], prob[:, h % 2, k * P:(k + 1) * P], B.ident)
                        mm.then_inc(turn_done, 1)
                        pe.wait_ge(probT_done, i * H_MLA + h + 2)
                        for k in range(NK):
                            mm = pe.matmul(acc[:, 0:VD], probT[:, h % 2, k * P:(k + 1) * P], values[:, K0 + k, h, :],
                                           start=k == 0, stop=k == NK - 1)
                        mm.then_inc(pv_done, 1)
                turns(pe, body)

            @block.vector
            def _(dve):
                own, step = dsem, Steps()
                dve.wait_ge(w_in, 33)

                def latent(i):
                    dve.wait_ge(q_prod, i * 3 + 2)
                    for k in range(2):
                        dve.tensor_scalar(qlT[:, k, :], misc[:, k * P:(k + 1) * P], gainT[:, k:k + 1], None, ALU.mult).then_inc(own, step())
                    dve.wait_ge(own, step.n)
                    dve.sem_inc(q_ready, 1)

                def queries(i):
                    dve.wait_ge(q_prod, i * 3 + 3)
                    dve.wait_ge(rs_done, i + 2)
                    dve.tensor_scalar(q[:].rearrange("p h e -> p (h e)"), misc[:, 0:H_MLA * QD], rs[:, 0:1], None, ALU.mult).then_inc(own, step())
                    dve.wait_ge(own, step.n)
                    dve.tensor_copy(qa[:, :, 0:NOPE], q[:, :, 0:NOPE]).then_inc(own, step())
                    dve.tensor_copy(qa[:, :, QD:P], q[:, :, NOPE:QD]).then_inc(own, step())
                    t = 0 if prompt else i + 1
                    cos, sin = (B.rope[:, t, j, :].unsqueeze(1).to_broadcast([P, H_MLA, ROPE // 2]) for j in range(2))
                    rotate(own, step, dve, qa[:, :, NOPE:QD], q[:, :, NOPE:QD], cos, sin, [tmp[:, j] for j in range(4)])
                    dve.wait_ge(own, step.n)
                    dve.sem_inc(q_ready, 1)

                def queries_turned(i, s):
                    dve.wait_ge(q_prod, i * 3 + 4)
                    dve.tensor_copy(qaT[:, s].rearrange("p h e -> p (h e)"), misc[:]).then_inc(q_ready, 1)
                latent(0)
                queries(0)
                queries_turned(0, 0)
                dve.sem_clear(own)
                step.restart()

                def body(i, s):
                    def softmax_max(h):
                        dve.wait_ge(score_done, i * H_MLA + h + 2)
                        dve.tensor_reduce(mx[:, h:h + 1], score[:, 0:W], AX.X, ALU.max).then_inc(own, step())
                        dve.wait_ge(own, step.n)
                        dve.tensor_scalar(mx[:, h:h + 1], mx[:, h:h + 1], -MLA_SCALE, None, ALU.mult).then_inc(max_done, 1)

                    def output(h):
                        dve.wait_ge(pv_done, i * H_MLA + h + 2)
                        dve.reciprocal(den[:, h:h + 1], den[:, h:h + 1]).then_inc(own, step())
                        dve.wait_ge(own, step.n)
                        dve.tensor_scalar(out[:, s, h, :], acc[:, 0:VD], den[:, h:h + 1], None, ALU.mult).then_inc(own, step())
                    dve.wait_ge(stored[s], 1 if prompt else (i // 2) * 16 + 1 if isinstance(i, int) else i * 8 + (1 - 8 * s))
                    softmax_max(0)
                    for h in range(H_MLA):
                        if h + 1 < H_MLA:
                            softmax_max(h + 1)
                        if h:
                            output(h - 1)
                        dve.wait_ge(turn_done, i * H_MLA + h + 2)
                        dve.tensor_copy(probT[:, h % 2, :], turned[:, 0:W]).then_inc(probT_done, 1)
                        if more(i) and h < 2:
                            (latent, queries)[h](i + 1)
                        if more(i) and h == 2:
                            queries_turned(i + 1, 1 - s)
                    output(H_MLA - 1)
                    dve.wait_ge(own, step.n)
                    dve.sem_clear(own)
                    step.restart()
                    dve.sem_inc(out_done, 1)
                turns(dve, body)


def scan_inputs(nc, T, B, l):
    CW = 3 * DQ
    GB, GL = 2 * H_GDN, 2 * GQ
    with stage(nc, "gate") as st:
        taps = st.sb("taps", [P, 2, 3, CW])
        wc = st.sb("wc", [P, 3, CW])
        y, tmp, sq = st.sb("y", [P, 2, CW]), st.sb("tmp", [P, 2, CW]), st.sb("sq", [P, 2 * DQ])
        ss = st.sb("ss", [P, 2 * H_GDN])
        ba = st.sb("ba", [P, 2, 2 * GB])
        eb = st.sb("eb", [P, 2, GB])
        ab = st.sb("ab", [P, GB])
        gates = st.sb("gates", [P, 2, 2 * GB])
        alog, dt = st.sb("alog", [P, GB]), st.sb("dt", [P, GB])
        lr = st.sb("lr", [P, 2, 2, RANK])
        lrT = st.sb("lrT", [RANK, 2, P])
        wg = st.sb("wg", [RANK, 2, GQ])
        bg = st.sb("bg", [P, GL])
        logit, absl, la = st.sb("logit", [P, GL]), st.sb("absl", [P, GL]), st.sb("la", [P, 2, GL])
        ptr, pl = st.ps("ptr", [P, 2, P]), st.ps("pl", [P, GL])
        w_in, t_in, conv_done, silu_done, sq_done, rs_done, a_done, ln_done, logit_done, lnl_done = (st.sem(x) for x in (
            "w_in", "t_in", "conv_done", "silu_done", "sq_done", "rs_done", "a_done", "ln_done", "logit_done", "lnl_done"))
        lr_turned, lrT_done, pl_done, ready, gates_ready, mixed, ss_done = (
            st.sem(x) for x in ("lr_turned", "lrT_done", "pl_done", "ready", "gates_ready", "mixed", "ss_done"))
        stored = [st.sem("stored0"), st.sem("stored1")]
        asem, dsem, psem = st.sem("act_steps"), st.sem("dve_steps"), st.sem("pool_steps")

        def turns(eng, body):
            with eng.Fori(0, (TILES - 1) // 2) as i:
                for s in range(2):
                    body(i * 2 + s, s, i)
            body(TILES - 1, 0, (TILES - 1) // 2)

        with st.block() as block:
            @block.sync
            def _(sp):
                for dst, src in ((wc[:].rearrange("p a c -> p (a c)"), T["gdn_conv"][l].rearrange("a c -> (a c)").partition_broadcast(P)),
                                 (alog[:], T["gdn_a_log"][l].rearrange("a c -> (a c)").partition_broadcast(P)),
                                 (dt[:], T["gdn_dt_bias"][l].rearrange("a c -> (a c)").partition_broadcast(P)),
                                 (bg[:], T["gla_bg"][l].rearrange("a c -> (a c)").partition_broadcast(P)),
                                 (wg[:], T["gla_wg"][l].rearrange("a r c -> r a c"))):
                    sp.dma_start(dst, src).then_inc(w_in, 16)

                def load(t):
                    s, r = t % 2, proj_row(t)
                    for j in range(3):
                        sp.dma_start(taps[:, s, j, :], T["proj"][r + j - 1:r + j - 1 + P, C_DQ:C_DZ]).then_inc(t_in, 16)
                    sp.dma_start(ba[:, s, :], T["proj"][r:r + P, C_DB:IN_DIM]).then_inc(t_in, 16)
                    sp.dma_start(lr[:, s].rearrange("p a r -> p (a r)"), T["proj"][r:r + P, C_GLR:C_GZ]).then_inc(t_in, 16)
                load(0)
                sp.wait_ge(t_in, 81)
                load(1)
                for t in range(TILES):
                    s, R = t % 2, slice(t * P, (t + 1) * P)
                    sp.wait_ge(gates_ready, t + 2)
                    sp.dma_start(T["gates"][R, :], gates[:, s, :]).then_inc(stored[s], 16)
                    sp.dma_start(T["gla_la"][R, :], la[:, s, :]).then_inc(stored[s], 16)
                    sp.wait_ge(ready, t + 2)
                    sp.dma_start(T["qkv"][R, :], y[:, s, :]).then_inc(stored[s], 16)
                    if t + 2 < TILES:
                        sp.wait_ge(t_in, (t + 2) * 80 + 1)
                        load(t + 2)
                for s in range(2):
                    sp.wait_ge(stored[s], 48 * ((TILES + 1 - s) // 2) + 1)

            @block.tensor
            def _(pe):
                pe.wait_ge(w_in, 81)

                def body(t, s, i):
                    pe.wait_ge(t_in, t * 80 + 81)
                    for d in range(2):
                        mm = pe.transpose(ptr[0:RANK, d, :], lr[:, s, d, :], B.ident)
                    mm.then_inc(lr_turned, 1)
                    pe.wait_ge(lrT_done, t + 2)
                    for d in range(2):
                        mm = pe.matmul(pl[:, d * GQ:(d + 1) * GQ], lrT[:, d, :], wg[:, d, :], start=True, stop=True)
                    mm.then_inc(pl_done, 1)
                turns(pe, body)

            @block.gpsimd
            def _(pool):
                own, step = psem, Steps()
                pool.wait_ge(w_in, 81)

                def body(t, s, i):
                    pool.wait_ge(t_in, t * 80 + 81)
                    pool.tensor_tensor(taps[:, s, 0, :], taps[:, s, 0, :], wc[:, 0, :], ALU.mult).then_inc(own, step())
                    pool.tensor_tensor(taps[:, s, 2, :], taps[:, s, 2, :], wc[:, 2, :], ALU.mult).then_inc(own, step())
                    pool.wait_ge(own, step.n)
                    pool.wait_ge(conv_done, t + 1)
                    pool.tensor_tensor(tmp[:, s], taps[:, s, 0, :], taps[:, s, 2, :], ALU.add).then_inc(mixed, 1)
                    pool.sem_clear(own)
                    step.restart()
                turns(pool, body)

            @block.scalar
            def _(act):
                own, step = asem, Steps()
                act.wait_ge(w_in, 81)
                act.activation(alog[:], alog[:], ACT.Exp).then_inc(own, step())
                act.wait_ge(own, step.n)
                act.sem_clear(own)
                step.restart()

                def body(t, s, i):
                    act.wait_ge(a_done, t + 2)
                    act.activation(eb[:, 0, :], ba[:, s, 0:GB], ACT.Exp, scale=-1.0).then_inc(own, step())
                    act.activation(eb[:, 1, :], ab[:], ACT.Exp, scale=-1.0).then_inc(own, step())
                    act.wait_ge(own, step.n)
                    act.activation(eb[:, 1, :], eb[:, 1, :], ACT.Ln, bias=B.ones[:, 0:1]).then_inc(ln_done, 1)
                    act.wait_ge(logit_done, t + 2)
                    act.activation(absl[:], absl[:], ACT.Exp, scale=-1.0).then_inc(own, step())
                    act.wait_ge(own, step.n)
                    act.activation(absl[:], absl[:], ACT.Ln, bias=B.ones[:, 0:1]).then_inc(lnl_done, 1)
                    act.wait_ge(conv_done, t + 2)
                    act.activation(y[:, s], y[:, s], ACT.Silu).then_inc(own, step())
                    act.wait_ge(own, step.n)
                    act.activation(sq[:], y[:, s, 0:2 * DQ], ACT.Square).then_inc(sq_done, 1)
                    act.wait_ge(ss_done, t + 2)
                    act.activation(ss[:], ss[:], ACT.Ln, bias=B.eps[:, 0:1]).then_inc(own, step())
                    act.wait_ge(own, step.n)
                    act.activation(ss[:], ss[:], ACT.Exp, scale=-0.5).then_inc(rs_done, 1)
                    act.sem_clear(own)
                    step.restart()
                turns(act, body)

            @block.vector
            def _(dve):
                own, step = dsem, Steps()
                dve.wait_ge(w_in, 81)

                def gate_logits(t, s):
                    dve.wait_ge(t_in, t * 80 + 81)
                    x = ba[:, s, GB:]
                    dve.tensor_tensor(x, x, dt[:], ALU.add).then_inc(own, step())
                    dve.wait_ge(own, step.n)
                    dve.scalar_tensor_tensor(ab[:], x, -1.0, x, ALU.mult, ALU.max).then_inc(a_done, 1)
                    dve.wait_ge(lr_turned, t + 2)
                    dve.tensor_copy(lrT[:], ptr[0:RANK, :, :]).then_inc(lrT_done, 1)
                    dve.tensor_tensor(y[:, s], taps[:, s, 1, :], wc[:, 1, :], ALU.mult).then_inc(own, step())
                    dve.wait_ge(pl_done, t + 2)
                    dve.tensor_tensor(logit[:], pl[:], bg[:], ALU.add).then_inc(own, step())
                    dve.wait_ge(own, step.n)
                    dve.scalar_tensor_tensor(absl[:], logit[:], -1.0, logit[:], ALU.mult, ALU.max).then_inc(logit_done, 1)
                    dve.wait_ge(mixed, t + 2)
                    dve.tensor_tensor(y[:, s], y[:, s], tmp[:, s], ALU.add).then_inc(conv_done, 1)

                def gate_values(t, s):
                    dve.wait_ge(ln_done, t + 2)
                    x = ba[:, s, GB:]
                    dve.scalar_tensor_tensor(eb[:, 1, :], x, 0.0, eb[:, 1, :], ALU.max, ALU.add).then_inc(own, step())
                    dve.tensor_scalar(eb[:, 0, :], eb[:, 0, :], 1.0, None, ALU.add).then_inc(own, step())
                    dve.wait_ge(own, step.n)
                    dve.scalar_tensor_tensor(gates[:, s, GB:], eb[:, 1, :], -1.0, alog[:], ALU.mult, ALU.mult).then_inc(own, step())
                    dve.reciprocal(gates[:, s, 0:GB], eb[:, 0, :]).then_inc(own, step())
                    dve.wait_ge(lnl_done, t + 2)
                    dve.scalar_tensor_tensor(la[:, s], logit[:], 0.0, absl[:], ALU.min, ALU.subtract).then_inc(own, step())
                    dve.wait_ge(own, step.n)
                    dve.tensor_scalar(la[:, s], la[:, s], 1.0 / TAU, None, ALU.mult).then_inc(gates_ready, 1)

                def head_norms(t, s):
                    dve.wait_ge(sq_done, t + 2)
                    dve.tensor_reduce(ss[:], sq[:].rearrange("p (h e) -> p h e", e=GK), AX.X, ALU.add).then_inc(ss_done, 1)
                    dve.wait_ge(rs_done, t + 2)
                    dve.tensor_scalar(ss[:, 0:H_GDN], ss[:, 0:H_GDN], float(GK) ** -0.5, None, ALU.mult).then_inc(own, step())
                    dve.wait_ge(own, step.n)
                    qk = y[:, s, 0:2 * DQ].rearrange("p (h e) -> p h e", e=GK)
                    dve.tensor_tensor(qk, qk, ss[:].unsqueeze(2).to_broadcast([P, 2 * H_GDN, GK]), ALU.mult).then_inc(own, step())
                    dve.wait_ge(own, step.n)
                    dve.sem_inc(ready, 1)

                def body(t, s, i):
                    dve.wait_ge(stored[s], i * 48 + 1)
                    gate_logits(t, s)
                    gate_values(t, s)
                    head_norms(t, s)
                    dve.sem_clear(own)
                    step.restart()
                turns(dve, body)


LEVELS = 7
PE_N, DVE_N, ACT_N, POOL_N = 25, 22, 8, 2 + LEVELS


def scan(nc, T, B, l, prompt):
    N = 1 if prompt else TILES - 1
    H, G = H_GDN, H_GLA
    with stage(nc, "scanp" if prompt else "scans") as st:
        both = lambda name, shape: [st.sb(f"{name}{d}", shape) for d in range(2)]
        qkv, gla, gla_la, gate = both("qkv", [P, 3, H, GK]), both("gla", [P, 3, G, GK]), both("gla_la", [P, GQ]), both("gate", [P, 16])
        decay = both("decay", [P, H, P])
        S, ST = both("S", [P, H, P]), [both("Sa", [P, H, P]), both("Sb", [P, H, P])]
        A, Ti, TT, Y = both("A", [P, H, P]), both("Ti", [P, H, P]), both("TT", [P, H, P]), both("Y", [P, H, P])
        kT, qT = both("kT", [GK, H, P]), both("qT", [GK, H, P])
        nwT = kT
        Rk, Rv, kend, VN = both("Rk", [P, H, GK]), both("Rv", [P, H, GK]), both("kend", [P, H, GK]), both("VN", [P, H, GK])
        s_d, s_g, s_m = both("s_d", [GK, H, GK]), both("s_g", [GK, G, GK]), both("s_m", [GK, G, GK])
        gg, eg = both("gg", [P, 3, H]), both("eg", [P, 3, H])
        mid, emid = both("mid", [GK, G, 3]), both("emid", [GK, G, 3])
        E, Ei = both("E", [P, G, GK]), both("Ei", [P, G, GK])
        gkv = both("gkv", [GK, G, GK])
        out = both("out", [P, 768])
        gT = [TT[d][0:GK] for d in range(2)]
        gA = both("gA", [P, G, P])
        qd, ki = E, Ei
        pX, pY = [st.ps(f"pX{d}", [P, H, P]) for d in range(2)], [st.ps(f"pY{d}", [P, H, P]) for d in range(2)]
        fpe, fdve, fact, fpool = ([st.sem(f"{x}_done{d}") for d in range(2)] for x in ("pe", "dve", "act", "pool"))
        arrived, stored, s_in = ([st.sem(f"{x}{d}") for d in range(2)] for x in ("arrived", "stored", "state_in"))
        asem, dsem, passed = st.sem("act_steps"), st.sem("dve_steps"), st.sem("passed")
        cum = [B.masks[:, 1, :], B.masks[:, 2, :]]
        anchored = [B.masks[:, 3, :], B.masks[:, 4, :]]
        mid_col = [B.midcols[:, 0:2], B.midcols[:, 2:4]]
        kd, qdl, vd = [qkv[d][:, 1] for d in range(2)], [qkv[d][:, 0] for d in range(2)], [qkv[d][:, 2] for d in range(2)]
        last = {}

        def heads(ap, n, w):
            return ap.unsqueeze(2).to_broadcast([ap.shape[0], n, w])

        def over(ap, n):
            return ap.unsqueeze(1).to_broadcast([ap.shape[0], n, ap.shape[1]])

        bank = lambda p, b: p[:].rearrange("p (b h) c -> p b (h c)", b=2)[:, b, :].rearrange("p (h e) -> p h e", e=GK)

        def turns(eng, body):
            if prompt:
                body(0)
            else:
                with eng.Fori(0, N) as t:
                    body(t)

        with st.block() as block:
            @block.sync
            def _(sp):
                if not prompt:
                    for d in range(2):
                        sp.dma_start(s_d[d][:], T["state_gdn"][0, l, d].rearrange("h k v -> k h v")).then_inc(s_in[d], 16)
                        sp.dma_start(s_g[d][:], T["state_gla"][0, l, d].rearrange("h k v -> k h v")).then_inc(s_in[d], 16)

                def body(t):
                    if prompt:
                        row, prow = [0, 0], [1, 1]
                    else:
                        row = [sp.snap(t * P + P), sp.snap(t * -P + N * P)]
                        prow = [sp.snap(t * P + P + 2), sp.snap(t * -P + (N * P + 2))]
                    for d in range(2):
                        sp.wait_ge(fdve[d], t * DVE_N + 1)
                        R, Q = bass.ds(row[d], P), bass.ds(prow[d], P)
                        for dst, src in ((gla_la[d][:], T["gla_la"][R, d * GQ:(d + 1) * GQ]),
                                         (gla[d][:].rearrange("p a h e -> p (a h e)"), T["proj"][Q, C_GQ:C_GLR]),
                                         (qkv[d][:].rearrange("p a h e -> p (a h e)"), T["qkv"][R, :]),
                                         (gate[d][:, 0:H], T["gates"][R, d * H:(d + 1) * H]),
                                         (gate[d][:, H:], T["gates"][R, 2 * H + d * H:2 * H + (d + 1) * H])):
                            sp.dma_start(dst, src).then_inc(arrived[d], 16)
                    for d in range(2):
                        sp.wait_ge(fdve[d], t * DVE_N + DVE_N + 1)
                        sp.dma_start(T["scan_b" if d else "scan_f"][bass.ds(row[d], P), :], out[d][:]).then_inc(stored[d], 16)
                turns(sp, body)
                n = N
                if prompt:
                    for d in range(2):
                        sp.dma_start(T["new_gdn"][0, l, d].rearrange("h k v -> k h v"), s_d[d][:]).then_inc(stored[d], 16)
                        sp.dma_start(T["new_gla"][0, l, d].rearrange("h k v -> k h v"), s_g[d][:]).then_inc(stored[d], 16)
                    n = 3
                for d in range(2):
                    sp.wait_ge(stored[d], 16 * n + 1)

            @block.tensor
            def _(pe):
                def body(t):
                    for d in range(2):
                        pe.wait_ge(arrived[d], t * 80 + 81)
                        pe.wait_ge(fdve[d], t * DVE_N + 1)
                        pe.matmul(pY[d][:, 0:2, :], anchored[d], gla_la[d][:], start=True, stop=True)
                        for h in range(G):
                            mm = pe.matmul(pX[d][0:GK, 0, 2 * h:2 * h + 2], gla_la[d][:, h * GK:(h + 1) * GK], mid_col[d], start=True, stop=True)
                        mm.then_inc(fpe[d], 1)
                    for d in range(2):
                        pe.wait_ge(fdve[d], t * DVE_N + 3)
                        pe.sem_inc(passed, 1)
                        for h in range(G):
                            pe.transpose(pX[d][0:GK, h, :], qd[d][:, h, :], B.ident)
                            mm = pe.transpose(pX[d][0:GK, G + h, :], ki[d][:, h, :], B.ident)
                        mm.then_inc(fpe[d], 1)
                    for d in range(2):
                        pe.wait_ge(fact[d], t * ACT_N + 4)
                        for h in range(G):
                            mm = pe.matmul(pY[d][:, h, :], gT[d][:, G + h, :], gT[d][:, h, :], start=True, stop=True)
                        mm.then_inc(fpe[d], 1)
                    for d in range(2):
                        pe.wait_ge(fdve[d], t * DVE_N + 4)
                        for h in range(G):
                            pe.matmul(bank(pX[d], 0)[:, h, :], gA[d][:, h, :], gla[d][:, 2, h, :], start=True, stop=False)
                            pe.matmul(bank(pX[d], 0)[:, h, :], gT[d][:, h, :], s_m[d][:, h, :], start=False, stop=True)
                        for h in range(G):
                            mm = pe.matmul(bank(pX[d], 1)[0:GK, h, :], ki[d][:, h, :], gla[d][:, 2, h, :], start=True, stop=True)
                        mm.then_inc(fpe[d], 1)
                    for d in range(2):
                        pe.wait_ge(fdve[d], t * DVE_N + 5)
                        la = gate[d][:, H:]
                        pe.matmul(pY[d][:, 0, 0:H], cum[d], la, start=True, stop=True)
                        pe.matmul(pY[d][:, 0, H:2 * H], B.ones[:], la, start=True, stop=True)
                        for h in range(H):
                            mm = pe.matmul(pX[d][:, h, :], la[:, h:h + 1].to_broadcast([P, P]), cum[d], start=True, stop=True)
                        mm.then_inc(fpe[d], 1)
                    for d in range(2):
                        pe.wait_ge(fdve[d], t * DVE_N + 6)
                        pe.sem_inc(passed, 1)
                        for h in range(H):
                            mm = pe.transpose(pY[d][0:GK, h, :], kd[d][:, h, :], B.ident)
                        mm.then_inc(fpe[d], 1)
                        for h in range(H):
                            mm = pe.transpose(pX[d][0:GK, h, :], qdl[d][:, h, :], B.ident)
                        mm.then_inc(fpe[d], 1)
                    for d in range(2):
                        pe.wait_ge(fact[d], t * ACT_N + 8)
                        for h in range(H):
                            pe.matmul(pX[d][:, h, :], kT[d][:, h, :], kT[d][:, h, :], start=True, stop=True)
                            mm = pe.matmul(pY[d][:, h, :], kT[d][:, h, :], qT[d][:, h, :], start=True, stop=True)
                        mm.then_inc(fpe[d], 1)
                    for v in range(LEVELS):
                        for d in range(2):
                            pe.wait_ge(fdve[d], t * DVE_N + (6 + 2 * v) + 1)
                            pe.wait_ge(fpool[d], t * POOL_N + (2 + v) + 1)
                            for h in range(H):
                                mm = pe.matmul(pX[d][:, h, :], ST[v % 2][d][:, h, :], Ti[d][:, h, :] if v else B.ident, start=True, stop=True)
                            mm.then_inc(fpe[d], 1)
                        for d in range(2):
                            pe.wait_ge(fdve[d], t * DVE_N + (7 + 2 * v) + 1)
                            for h in range(H):
                                if 0 < v < LEVELS - 1:
                                    pe.matmul(pY[d][:, h, :], TT[d][:, h, :], Y[d][:, h, :], start=True, stop=True)
                                mm = pe.matmul(pX[d][:, h, :], Y[d][:, h, :], TT[d][:, h, :] if v else B.ident, start=True, stop=True)
                            mm.then_inc(fpe[d], 1)
                    for d in range(2):
                        pe.wait_ge(fdve[d], t * DVE_N + 21)
                        pe.wait_ge(fpool[d], t * POOL_N + 10)
                        for h in range(H):
                            mm = pe.matmul(pX[d][0:GK, h, :], Rk[d][:, h, :], TT[d][:, h, :], start=True, stop=True)
                        mm.then_inc(fpe[d], 1)
                    for d in range(2):
                        pe.wait_ge(fact[d], t * ACT_N + 9)
                        for h in range(H):
                            pe.matmul(bank(pY[d], 0)[:, h, :], TT[d][:, h, :], Rv[d][:, h, :], start=True, stop=False)
                            mm = pe.matmul(bank(pY[d], 0)[:, h, :], nwT[d][:, h, :], s_d[d][:, h, :], start=False, stop=True)
                        mm.then_inc(fpe[d], 1)
                    for d in range(2):
                        pe.wait_ge(fdve[d], t * DVE_N + 22)
                        for h in range(H):
                            pe.matmul(bank(pX[d], 0)[:, h, :], qT[d][:, h, :], s_d[d][:, h, :], start=True, stop=True)
                            pe.matmul(bank(pX[d], 1)[:, h, :], A[d][:, h, :], VN[d][:, h, :], start=True, stop=True)
                            mm = pe.matmul(bank(pY[d], 1)[0:GK, h, :], kend[d][:, h, :], VN[d][:, h, :], start=True, stop=True)
                        mm.then_inc(fpe[d], 1)
                turns(pe, body)

            @block.scalar
            def _(act):
                own, step = asem, Steps()

                def body(t):
                    for d in range(2):
                        act.wait_ge(fpe[d], t * PE_N + 2)
                        y = pY[d][:, 0:2, :].rearrange("p a c -> p (a c)")
                        act.activation(E[d][:].rearrange("p h e -> p (h e)"), y, ACT.Exp).then_inc(own, step())
                        act.activation(Ei[d][:].rearrange("p h e -> p (h e)"), y, ACT.Exp, scale=-1.0).then_inc(fact[d], 1)
                        act.wait_ge(fdve[d], t * DVE_N + 2)
                        act.activation(emid[d][:], mid[d][:], ACT.Exp).then_inc(fact[d], 1)
                    for d in range(2):
                        act.wait_ge(fpe[d], t * PE_N + 3)
                        act.activation(gT[d], pX[d][0:GK], ACT.Copy).then_inc(fact[d], 1)
                    for d in range(2):
                        act.wait_ge(fdve[d], t * DVE_N + 6)
                        act.activation(eg[d][:], gg[d][:], ACT.Exp).then_inc(fact[d], 1)
                        act.activation(decay[d][:], decay[d][:], ACT.Exp).then_inc(fact[d], 1)
                        act.wait_ge(fpe[d], t * PE_N + 7)
                        act.activation(kT[d][:], pY[d][0:GK], ACT.Copy).then_inc(fact[d], 1)
                        act.wait_ge(fpe[d], t * PE_N + 8)
                        act.activation(qT[d][:], pX[d][0:GK], ACT.Copy).then_inc(fact[d], 1)
                    for d in range(2):
                        act.wait_ge(fpe[d], t * PE_N + 24)
                        act.activation(nwT[d][:], pX[d][0:GK], ACT.Copy, scale=-1.0).then_inc(fact[d], 1)
                    act.wait_ge(own, step.n)
                    act.sem_clear(own)
                    step.restart()
                turns(act, body)

            @block.gpsimd
            def _(pool):
                def body(t):
                    for d in range(2):
                        pool.wait_ge(fact[d], t * ACT_N + 6)
                        pool.tensor_tensor(decay[d][:], decay[d][:], over(cum[d], H), ALU.mult).then_inc(fpool[d], 1)
                    for v in range(LEVELS):
                        for d in range(2):
                            if v == 0:
                                pool.wait_ge(fdve[d], t * DVE_N + 7)
                            if v >= 2:
                                pool.wait_ge(fpe[d], t * PE_N + (9 + 2 * (v - 2)) + 1)
                            pool.tensor_tensor(ST[v % 2][d][:], S[d][:], over(B.masks[:, 5 + 7 * d + v, :], H), ALU.mult).then_inc(fpool[d], 1)
                    for d in range(2):
                        pool.tensor_tensor(kend[d][:], kd[d], heads(eg[d][:, 2, :], H, GK), ALU.mult)
                        pool.tensor_tensor(Rv[d][:], vd[d], heads(gate[d][:, 0:H], H, GK), ALU.mult)
                        pool.tensor_tensor(Rk[d][:], kd[d], heads(gg[d][:, 1, :], H, GK), ALU.mult).then_inc(fpool[d], 1)
                turns(pool, body)

            @block.vector
            def _(dve):
                own, step = dsem, Steps()
                for d in range(2):
                    dve.memset(gA[d][:], 0.0).then_inc(own, step())
                    if prompt:
                        dve.memset(s_d[d][:], 0.0).then_inc(own, step())
                        dve.memset(s_g[d][:], 0.0).then_inc(own, step())
                    else:
                        dve.wait_ge(s_in[d], 33)
                dve.wait_ge(own, step.n)
                dve.sem_clear(own)
                step.restart()

                def body(t):
                    for d in range(2):
                        dve.wait_ge(fpe[d], t * PE_N + 2)
                        mg = pX[d][0:GK, 0, 0:2 * G].rearrange("p (h a) -> p h a", a=2)
                        dve.tensor_copy(mid[d][:, :, 0:2], mg).then_inc(own, step())
                        dve.wait_ge(own, step.n)
                        dve.tensor_tensor(mid[d][:, :, 2], mid[d][:, :, 1], mid[d][:, :, 0], ALU.subtract).then_inc(fdve[d], 1)
                    for d in range(2):
                        dve.wait_ge(fact[d], t * ACT_N + 2)
                        dve.scalar_tensor_tensor(qd[d][:], gla[d][:, 0], float(GK) ** -0.5, E[d][:], ALU.mult, ALU.mult).then_inc(own, step())
                        dve.tensor_tensor(ki[d][:], gla[d][:, 1], Ei[d][:], ALU.mult).then_inc(fdve[d], 1)
                    for d in range(2):
                        dve.wait_ge(fact[d], t * ACT_N + 3)
                        dve.wait_ge(fpe[d], t * PE_N + 4)
                        dve.tensor_tensor(s_m[d][:], s_g[d][:], heads(emid[d][:, :, 0], G, GK), ALU.mult).then_inc(own, step())
                        dve.copy_predicated(gA[d][:], over(cum[d], G).bitcast(U32), pY[d][:, 0:G, :]).then_inc(fdve[d], 1)
                    for d in range(2):
                        dve.wait_ge(fpe[d], t * PE_N + 5)
                        dve.wait_ge(stored[d], t * 16 + 1)
                        dve.tensor_copy(out[d][:, 0:GQ].rearrange("p (h e) -> p h e", e=GK), bank(pX[d], 0)[:, 0:G, :]).then_inc(own, step())
                        dve.tensor_tensor(gkv[d][:], bank(pX[d], 1)[0:GK, 0:G, :], heads(emid[d][:, :, 2], G, GK), ALU.mult).then_inc(own, step())
                        dve.tensor_tensor(s_g[d][:], s_g[d][:], heads(emid[d][:, :, 1], G, GK), ALU.mult).then_inc(own, step())
                        dve.wait_ge(own, step.n)
                        dve.tensor_tensor(s_g[d][:], s_g[d][:], gkv[d][:], ALU.add).then_inc(fdve[d], 1)
                    for d in range(2):
                        dve.wait_ge(fpe[d], t * PE_N + 6)
                        dve.tensor_copy(gg[d][:, 0:2, :], pY[d][:, 0, 0:2 * H].rearrange("p (a h) -> p a h", h=H)).then_inc(own, step())
                        dve.wait_ge(own, step.n)
                        dve.tensor_tensor(gg[d][:, 2, :], gg[d][:, 1, :], gg[d][:, 0, :], ALU.subtract).then_inc(own, step())
                        for h in range(H):
                            dve.tensor_scalar(decay[d][:, h, :], pX[d][:, h, :], gg[d][:, 0, h:h + 1], 0.0, ALU.subtract, ALU.min).then_inc(own, step())
                        dve.wait_ge(own, step.n)
                        dve.sem_inc(fdve[d], 1)
                    for d in range(2):
                        dve.wait_ge(fact[d], t * ACT_N + 5)
                        dve.tensor_tensor(gg[d][:, 1, :], eg[d][:, 0, :], gate[d][:, 0:H], ALU.mult).then_inc(own, step())
                        dve.wait_ge(own, step.n)
                    for d in range(2):
                        dve.wait_ge(fpe[d], t * PE_N + 9)
                        dve.wait_ge(fpool[d], t * POOL_N + 2)
                        dve.tensor_tensor(S[d][:], pX[d][:], decay[d][:], ALU.mult).then_inc(own, step())
                        dve.tensor_tensor(A[d][:], pY[d][:], decay[d][:], ALU.mult).then_inc(own, step())
                        dve.wait_ge(own, step.n)
                        dve.sem_inc(fdve[d], 1)
                    for v in range(LEVELS):
                        for d in range(2):
                            dve.wait_ge(fpe[d], t * PE_N + (9 + 2 * v) + 1)
                            dve.tensor_tensor(Y[d][:], pX[d][:], heads(gate[d][:, 0:H], H, P), ALU.mult).then_inc(fdve[d], 1)
                        for d in range(2):
                            dve.wait_ge(fpe[d], t * PE_N + (10 + 2 * v) + 1)
                            if v == 0:
                                dve.wait_ge(fdve[d], t * DVE_N + 8)
                                dve.tensor_tensor(Ti[d][:], over(B.ident, H), Y[d][:], ALU.subtract).then_inc(own, step())
                                dve.tensor_tensor(TT[d][:], over(B.ident, H), pX[d][:], ALU.subtract).then_inc(own, step())
                            else:
                                if v < LEVELS - 1:
                                    dve.tensor_tensor(Ti[d][:], Ti[d][:], pY[d][:], ALU.subtract).then_inc(own, step())
                                dve.tensor_tensor(TT[d][:], TT[d][:], pX[d][:], ALU.subtract).then_inc(own, step())
                            dve.wait_ge(own, step.n)
                            dve.sem_inc(fdve[d], 1)
                    for d in range(2):
                        dve.wait_ge(fpe[d], t * PE_N + 25)
                        dve.tensor_copy(VN[d][:], bank(pY[d], 0)).then_inc(fdve[d], 1)
                    for d in range(2):
                        dve.wait_ge(fpe[d], t * PE_N + 26)
                        o = out[d][:, GQ:].rearrange("p (h e) -> p h e", e=GK)
                        dve.tensor_tensor(o, bank(pX[d], 0), heads(eg[d][:, 0, :], H, GK), ALU.mult).then_inc(own, step())
                        dve.tensor_tensor(s_d[d][:], s_d[d][:], heads(eg[d][0:GK, 1, :], H, GK), ALU.mult).then_inc(own, step())
                        dve.wait_ge(own, step.n)
                        dve.tensor_tensor(o, o, bank(pX[d], 1), ALU.add).then_inc(own, step())
                        dve.tensor_tensor(s_d[d][:], s_d[d][:], bank(pY[d], 1)[0:GK], ALU.add).then_inc(own, step())
                        dve.wait_ge(own, step.n)
                        dve.sem_inc(fdve[d], 1)
                    dve.wait_ge(own, step.n)
                    dve.sem_clear(own)
                    step.restart()
                turns(dve, body)


def mixer_output(nc, T, B, l):
    W3 = 768
    NH = W3 // GK
    with stage(nc, "mixer") as st:
        wout = st.sb("wout", [P, KD, D])
        wr = st.sb("wr", [P, KD, E_N])
        gain = st.sb("gain", [P, 2, GK])
        o = st.sb("o", [P, D])
        ob, z = st.sb("ob", [P, W3]), st.sb("z", [P, W3])
        ss = st.sb("ss", [P, NH])
        rs = st.sb("rs", [P, 2])
        oT = st.sb("oT", [P, KD, P])
        sq = st.sb("sq", [P, D])
        branch = st.sb("branch", [P, D])
        xhat = st.sb("xhat", [P, 2, D])
        xT = st.sb("xT", [P, KD, P])
        mx, den = st.sb("mx", [P, 1]), st.sb("den", [P, 1])
        ex = st.sb("ex", [P, E_N])
        af = st.sb("af", [P, E_N + 2])
        affT = st.sb("affT", [E_N + 2, ROWS])
        tr, acc, xtr = st.ps("tr", [P, KD, P]), st.ps("acc", [P, D]), st.ps("xtr", [P, KD, P])
        lg, at = st.ps("lg", [P, 512]), st.ps("at", [P, 512])
        w_in, t_in, zsilu_done, ss_done, rs_done, o_done, o_turned, oT_done, y_prod = (st.sem(x) for x in (
            "w_in", "t_in", "zsilu_done", "ss_done", "rs_done", "o_done", "o_turned", "oT_done", "y_prod"))
        yrs_done, branch_done, x_done, xrs_done, xhat_done, x_turned, xT_done, logits = (st.sem(x) for x in (
            "yrs_done", "branch_done", "x_done", "xrs_done", "xhat_done", "x_turned", "xT_done", "logits"))
        max_done, exp_done, aff_done, aff_turned, affT_done, all_stored = (st.sem(x) for x in (
            "max_done", "exp_done", "aff_done", "aff_turned", "affT_done", "all_stored"))
        stored = [st.sem("stored0"), st.sem("stored1")]
        asem, dsem = st.sem("act_steps"), st.sem("dve_steps")

        def turns(eng, body):
            body(0, 0)
            with eng.Fori(0, (TILES - 3) // 2) as i:
                for s in range(2):
                    body(i * 2 + (s + 1), 1 - s)
            body(TILES - 2, 1)
            body(TILES - 1, 0)

        def ahead(t, n):
            return not isinstance(t, int) or t + n < TILES

        with st.block() as block:
            @block.sync
            def _(sp):
                for dst, src in ((wout[:], T["w_out"][l].rearrange("(k p) n -> p k n", p=P)),
                                 (wr[:], T["w_router"][l].rearrange("(k p) n -> p k n", p=P)),
                                 (gain[:, 0, :], T["gla_out_norm"][l].partition_broadcast(P)),
                                 (gain[:, 1, :], T["gdn_out_norm"][l].partition_broadcast(P))):
                    sp.dma_start(dst, src).then_inc(w_in, 16)

                def load(t):
                    row = t * P if isinstance(t, int) else sp.snap(t * P)
                    prow = proj_row(t) if isinstance(t, int) else sp.snap(t * P + 2)
                    R, Q = bass.ds(row, P), bass.ds(prow, P)
                    sp.wait_ge(o_turned, t + 1)
                    for dst, src in ((o[:, 0:256], T["mla_out"][R, :]), (o[:, 256:], T["scan_f"][R, :]), (ob[:], T["scan_b"][R, :]),
                                     (z[:, 0:GQ], T["proj"][Q, C_GZ:C_DQ]), (z[:, GQ:], T["proj"][Q, C_DZ:C_DB])):
                        sp.dma_start(dst, src).then_inc(t_in, 16)

                load(0)
                load(1)

                def body(t, s):
                    row = t * P if isinstance(t, int) else sp.snap(t * P)
                    if ahead(t, 2):
                        load(t + 2)
                    sp.wait_ge(xhat_done, t + 2)
                    sp.dma_start(T["xhat"][bass.ds(row, P), :], xhat[:, s]).then_inc(stored[s], 16)
                turns(sp, body)
                sp.wait_ge(affT_done, TILES + 1)
                sp.dma_start(T["affT"], affT[:]).then_inc(all_stored, 16)
                sp.wait_ge(all_stored, 17)
                for s in range(2):
                    sp.wait_ge(stored[s], 16 * ((TILES + 1 - s) // 2) + 1)

            @block.scalar
            def _(act):
                own, step = asem, Steps()

                def rows(t):
                    act.wait_ge(t_in, t * 80 + 81)
                    act.activation(z[:], z[:], ACT.Silu).then_inc(zsilu_done, 1)
                    act.wait_ge(ss_done, t + 2)
                    act.activation(ss[:], ss[:], ACT.Ln, bias=B.eps[:, 0:1], scale=1.0 / GK).then_inc(own, step())
                    act.wait_ge(own, step.n)
                    act.activation(ss[:], ss[:], ACT.Exp, scale=-0.5).then_inc(rs_done, 1)

                def turned(t):
                    act.wait_ge(o_turned, t + 2)
                    act.wait_ge(y_prod, t + 1)
                    act.activation(oT[:], tr[:], ACT.Copy).then_inc(oT_done, 1)

                for t in range(2):
                    rows(t)
                    turned(t)
                act.wait_ge(own, step.n)
                act.sem_clear(own)
                step.restart()

                def body(t, s):
                    act.wait_ge(y_prod, t + 2)
                    act.activation(sq[:], acc[:], ACT.Square, accum_out=rs[:, 0:1]).then_inc(own, step())
                    act.wait_ge(own, step.n)
                    act.activation(rs[:, 0:1], rs[:, 0:1], ACT.Ln, bias=B.eps[:, 0:1], scale=1.0 / D).then_inc(own, step())
                    act.wait_ge(own, step.n)
                    act.activation(rs[:, 0:1], rs[:, 0:1], ACT.Exp, scale=-0.5).then_inc(yrs_done, 1)
                    act.wait_ge(x_done, t + 2)
                    act.activation(sq[:], B.x[:, t, :], ACT.Square, accum_out=rs[:, 1:2]).then_inc(own, step())
                    act.wait_ge(own, step.n)
                    act.activation(rs[:, 1:2], rs[:, 1:2], ACT.Ln, bias=B.eps[:, 0:1], scale=1.0 / D).then_inc(own, step())
                    act.wait_ge(own, step.n)
                    act.activation(rs[:, 1:2], rs[:, 1:2], ACT.Exp, scale=-0.5).then_inc(xrs_done, 1)
                    if ahead(t, 2):
                        rows(t + 2)
                    act.wait_ge(max_done, t + 2)
                    act.activation(ex[:], lg[:, 0:E_N], ACT.Exp, bias=mx[:, 0:1], accum_out=den[:]).then_inc(exp_done, 1)
                    if ahead(t, 2):
                        turned(t + 2)
                    act.sem_clear(own)
                    step.restart()
                turns(act, body)

            @block.tensor
            def _(pe):
                pe.wait_ge(w_in, 65)

                def turn(t):
                    pe.wait_ge(o_done, t + 2)
                    pe.wait_ge(oT_done, t + 1)
                    for k in range(KD):
                        mm = pe.transpose(tr[:, k, :], o[:, k * P:(k + 1) * P], B.ident)
                    mm.then_inc(o_turned, 1)

                def project(t):
                    pe.wait_ge(oT_done, t + 2)
                    pe.wait_ge(branch_done, t + 1)
                    for n in range(2):
                        for k in range(KD):
                            mm = pe.matmul(acc[:, n * 512:(n + 1) * 512], oT[:, k, :], wout[:, k, n * 512:(n + 1) * 512], start=k == 0, stop=k == KD - 1)
                    mm.then_inc(y_prod, 1)

                turn(0)
                project(0)
                turn(1)

                def body(t, s):
                    if ahead(t, 1):
                        project(t + 1)
                    pe.wait_ge(xhat_done, t + 2)
                    for k in range(KD):
                        mm = pe.transpose(xtr[:, k, :], xhat[:, s, k * P:(k + 1) * P], B.ident)
                    mm.then_inc(x_turned, 1)
                    if ahead(t, 2):
                        turn(t + 2)
                    pe.wait_ge(xT_done, t + 2)
                    for k in range(KD):
                        mm = pe.matmul(lg[:, 0:E_N], xT[:, k, :], wr[:, k, :], start=k == 0, stop=k == KD - 1)
                    mm.then_inc(logits, 1)
                    pe.wait_ge(aff_done, t + 2)
                    pe.transpose(at[0:E_N + 2, 0:P], af[:], B.ident).then_inc(aff_turned, 1)
                turns(pe, body)

            @block.vector
            def _(dve):
                own, step = dsem, Steps()
                dve.memset(af[:], 0.0).then_inc(own, step())
                dve.wait_ge(w_in, 65)

                def rows(t):
                    m = o[:, 256:]
                    mh = m.rearrange("p (h e) -> p h e", e=GK)
                    dve.wait_ge(t_in, t * 80 + 81)
                    dve.tensor_tensor(m, m, ob[:], ALU.add).then_inc(own, step())
                    dve.wait_ge(own, step.n)
                    dve.tensor_tensor(ob[:], m, m, ALU.mult).then_inc(own, step())
                    dve.wait_ge(own, step.n)
                    dve.tensor_reduce(ss[:], ob[:].rearrange("p (h e) -> p h e", e=GK), AX.X, ALU.add).then_inc(ss_done, 1)
                    dve.wait_ge(zsilu_done, t + 2)
                    dve.tensor_tensor(m, m, z[:], ALU.mult).then_inc(own, step())
                    dve.wait_ge(own, step.n)
                    dve.tensor_tensor(mh[:, 0:H_GLA], mh[:, 0:H_GLA], gain[:, 0:1, :].to_broadcast([P, H_GLA, GK]), ALU.mult).then_inc(own, step())
                    dve.tensor_tensor(mh[:, H_GLA:], mh[:, H_GLA:], gain[:, 1:2, :].to_broadcast([P, H_GDN, GK]), ALU.mult).then_inc(own, step())
                    dve.wait_ge(own, step.n)
                    dve.wait_ge(rs_done, t + 2)
                    dve.tensor_tensor(mh, mh, ss[:].unsqueeze(2).to_broadcast([P, NH, GK]), ALU.mult).then_inc(o_done, 1)

                rows(0)
                rows(1)
                dve.wait_ge(own, step.n)
                dve.sem_clear(own)
                step.restart()

                def body(t, s):
                    c = 0 if isinstance(t, int) and t == 0 else 1
                    dve.wait_ge(yrs_done, t + 2)
                    dve.scalar_tensor_tensor(branch[:], acc[:], rs[:, 0:1], B.gate[:, 0, c, :], ALU.mult, ALU.mult).then_inc(branch_done, 1)
                    dve.wait_ge(branch_done, t + 2)
                    dve.tensor_tensor(B.x[:, t, :], B.x[:, t, :], branch[:], ALU.add).then_inc(x_done, 1)
                    dve.wait_ge(xrs_done, t + 2)
                    dve.wait_ge(stored[s], (t // 2) * 16 + 1 if isinstance(t, int) else t * 8 + (1 - 8 * s))
                    dve.tensor_scalar(xhat[:, s], B.x[:, t, :], rs[:, 1:2], None, ALU.mult).then_inc(xhat_done, 1)
                    if ahead(t, 2):
                        rows(t + 2)
                    dve.wait_ge(x_turned, t + 2)
                    for k in range(KD):
                        dve.tensor_scalar(xT[:, k, :], xtr[:, k, :], B.scale[:, c, 1, k:k + 1], B.shift[:, c, 1, k:k + 1], ALU.mult, ALU.add).then_inc(own, step())
                    dve.wait_ge(own, step.n)
                    dve.sem_inc(xT_done, 1)
                    dve.wait_ge(logits, t + 2)
                    dve.tensor_reduce(mx[:], lg[:, 0:E_N], AX.X, ALU.max).then_inc(own, step())
                    dve.wait_ge(own, step.n)
                    dve.tensor_scalar(mx[:], mx[:], -1.0, None, ALU.mult).then_inc(max_done, 1)
                    dve.wait_ge(exp_done, t + 2)
                    dve.reciprocal(den[:], den[:]).then_inc(own, step())
                    dve.wait_ge(own, step.n)
                    dve.tensor_scalar(af[:, 0:E_N], ex[:], den[:, 0:1], None, ALU.mult).then_inc(own, step())
                    dve.wait_ge(own, step.n)
                    dve.sem_inc(aff_done, 1)
                    dve.tensor_copy(B.aff[:, t, :], af[:]).then_inc(own, step())
                    dve.wait_ge(aff_turned, t + 2)
                    dve.tensor_copy(affT[:, bass.ds(t * P, P)], at[0:E_N + 2, 0:P]).then_inc(own, step())
                    dve.wait_ge(own, step.n)
                    dve.sem_clear(own)
                    step.restart()
                    dve.sem_inc(affT_done, 1)
                turns(dve, body)


def experts(nc, T, B, l):
    RING = 4
    PER = KF // RING
    PER_BANK = 512 // CAP
    with stage(nc, "ffn") as st:
        w1, w3, w2 = (st.sb(x, [P, RING, KD, P]) for x in ("w1", "w3", "w2"))
        xe, xp = st.sb("xe", [P, D]), st.sb("xp", [CAP_P, D])
        g_idx, s_idx = st.sb("g_idx", [P, 2], I32), st.sb("s_idx", [P, 2], I32)
        xT = st.sb("xT", [P, 2, KD, CAP])
        en = st.sb("en", [P, 2, CAP])
        hT = st.sb("hT", [P, 2, CAP])
        yT = st.sb("yT", [P, KD, CAP])
        ye, yp = st.sb("ye", [P, D]), st.sb("yp", [CAP_P, D])
        row = st.sb("row", [P, ROWS])
        junk = st.sb("junk", [P, DEC])
        counts = st.sb("counts", [P, TILES, 3])
        rank = st.sb("rank", [P, TILES])
        sel = st.sb("sel", [P, TILES, P])
        pair = st.sb("pair", [P, TILES, 2])
        later = st.sb("later", [P, P])
        token, gate = st.sb("token", [P, 2, E_N + 2]), st.sb("gate", [P, 2, E_N + 2])
        acc, hb = st.ps("acc", [P, 3, 512]), st.ps("hb", [P, 2, 512])
        tr, trp = st.ps("tr", [P, D]), st.ps("trp", [P, 512])
        slot_s, slot_p = trp[:, 0:2], trp[0:CAP_P, 2:4]
        w_in = [st.sem(f"w_in{i}") for i in range(RING)]
        w_used = [st.sem(f"w_used{i}") for i in range(RING)]
        idx_done, turned, xT_done, h_prod, silu_done, h_done, yT_done = (
            st.sem(x) for x in ("idx_done", "turned", "xT_done", "h_prod", "silu_done", "h_done", "yT_done"))
        y_turned, y_done, rows_added, passed = (st.sem(x) for x in ("y_turned", "y_done", "rows_added", "passed"))
        half_done = st.sem("half_done")
        row_in, ranked, sel_done, picked = (st.sem(x) for x in ("row_in", "ranked", "sel_done", "picked"))
        zeroed, cleared, dsem = st.sem("zeroed"), st.sem("cleared"), st.sem("dve_steps")
        gathered, scattered = B.gathered, B.scattered
        part = lambda c: acc[:, c // PER_BANK, (c % PER_BANK) * CAP:(c % PER_BANK + 1) * CAP]

        def turns(eng, body):
            body(0, 0, True)
            body(1, 1, False)
            with eng.Fori(1, E_N // 2) as i:
                for s in range(2):
                    body(i * 2 + s, s, False)

        with st.block() as block:
            @block.sync
            def _(sp):
                for e in range(2):
                    sp.wait_ge(ranked, e + 1)
                    sp.dma_start(row[:], T["affT"][e:e + 1, :].to_broadcast([P, ROWS])).then_inc(row_in, 16)

                def body(e, s, first):
                    for j in range(KF):
                        r = j % RING
                        c = slice(j * P, (j + 1) * P)
                        sp.wait_ge(w_used[r], e * PER + j // RING + 1)
                        sp.dma_start(w1[:, r], T["w_e1"][l, bass.ds(e, 1), :, c].rearrange("a (k p) n -> p (a k) n", p=P)).then_inc(w_in[r], 16)
                        sp.dma_start(w3[:, r], T["w_e3"][l, bass.ds(e, 1), :, c].rearrange("a (k p) n -> p (a k) n", p=P)).then_inc(w_in[r], 16)
                        sp.dma_start(w2[:, r].rearrange("p k n -> p (k n)"), T["w_e2"][l, bass.ds(e, 1), c, :].rearrange("a p n -> p (a n)")).then_inc(w_in[r], 16)
                        if j == 1:
                            sp.wait_ge(ranked, e + 3)
                            sp.dma_start(row[:], T["affT"][bass.ds(e + 2, 1), :].to_broadcast([P, ROWS])).then_inc(row_in, 16)
                turns(sp, body)
                sp.wait_ge(row_in, 16 * (E_N + 2) + 1)

            @block.gpsimd
            def _(pool):
                pool.memset(ye[:], 0.0).then_inc(zeroed, 1)

                def gather():
                    for dst, n, k in ((xe, P, 0), (xp, CAP_P, 1)):
                        at = bass.IndirectOffsetOnAxis(ap=g_idx[0:n, k:k + 1].bitcast(U32), axis=0)
                        pool.indirect_dma_start(dst[:], None, T["xhat"], at).then_inc(gathered, 16)

                def scatter(e):
                    pool.wait_ge(y_done, e + 2)
                    pool.sem_inc(passed, 1)
                    for src, n, k in ((ye, P, 0), (yp, CAP_P, 1)):
                        at = bass.IndirectOffsetOnAxis(ap=s_idx[0:n, k:k + 1].bitcast(U32), axis=0)
                        pool.indirect_dma_start(T["moe"], at, src[:], None, compute_op=ALU.add).then_inc(scattered, 16)
                    pool.wait_ge(scattered, l * (E_N * 32) + (e * 32 + 32))
                    pool.sem_inc(rows_added, 1)

                pool.wait_ge(idx_done, 2)
                gather()
                pool.wait_ge(cleared, 16 * TILES + 1)

                def body(e, s, first):
                    pool.wait_ge(turned, e + 2)
                    pool.wait_ge(idx_done, e + 3)
                    pool.sem_inc(passed, 1)
                    gather()
                    if not first:
                        scatter(e - 1)
                turns(pool, body)
                scatter(E_N - 1)
                pool.wait_ge(gathered, l * ((E_N + 1) * 32) + (E_N + 1) * 32)

            @block.tensor
            def _(pe):
                def turn_x(e):
                    pe.wait_ge(gathered, l * ((E_N + 1) * 32) + (e * 32 + 32))
                    for k in range(KD):
                        pe.transpose(tr[:, k * P:(k + 1) * P], xe[:, k * P:(k + 1) * P], B.ident)
                    for k in range(KD):
                        mm = pe.transpose(trp[:, k * CAP_P:(k + 1) * CAP_P], xp[:, k * P:(k + 1) * P], B.ident[0:CAP_P, 0:CAP_P])
                    mm.then_inc(turned, 1)

                def turn_y(e, half):
                    if half == 0:
                        pe.wait_ge(yT_done, e * 2 + 3)
                        for k in range(KD):
                            pe.transpose(tr[:, k * P:(k + 1) * P], yT[:, k, 0:CAP_S], B.ident)
                    else:
                        pe.wait_ge(half_done, e + 2)
                    for k in range(4):
                        mm = pe.transpose(trp[0:CAP_P, k * P:(k + 1) * P], yT[:, 4 * half + k, CAP_S:], B.ident)
                    mm.then_inc(y_turned, 1)

                def pick(e):
                    pe.wait_ge(sel_done, e + 2)
                    for t in range(1, TILES):
                        pe.matmul(slot_s, sel[:, t, :], pair[:, t, :], start=t == 1, stop=t == TILES - 1)
                    pe.matmul(slot_p, sel[:, 0, 0:CAP_P], pair[:, 0, :], start=True, stop=True).then_inc(picked, 1)

                pick(0)
                pick(1)
                turn_x(0)

                def body(e, s, first):
                    def up_products(j):
                        r, b = j % RING, j % 2
                        pe.wait_ge(w_in[r], (e * PER + j // RING) * 48 + 49)
                        if j >= 2:
                            pe.wait_ge(h_done, e * KF + j)
                        for i, w in enumerate((w1, w3)):
                            for k in range(KD):
                                mm = pe.matmul(hb[:, b, i * CAP:(i + 1) * CAP], w[:, r, k, :], xT[:, s, k, :], start=k == 0, stop=k == KD - 1)
                        mm.then_inc(h_prod, 1)

                    def down_products(j):
                        r, b = j % RING, j % 2
                        pe.wait_ge(h_done, e * KF + j + 2)
                        for c in range(KD):
                            mm = pe.matmul(part(c), w2[:, r, c, :], hT[:, b, :], start=j == 0 and c % PER_BANK == 0,
                                           stop=j == KF - 1, skip_group_check=True)
                        mm.then_inc(w_used[r], 1)

                    pe.wait_ge(xT_done, e + 2)
                    up_products(0)
                    if not first:
                        turn_y(e - 1, 0)
                    up_products(1)
                    if not first:
                        pe.wait_ge(yT_done, e * 2 + 1)
                    down_products(0)
                    if not first:
                        turn_y(e - 1, 1)
                    for j in range(2, KF):
                        if j == 6:
                            pe.wait_ge(y_done, e + 1)
                            turn_x(e + 1)
                        up_products(j)
                        down_products(j - 1)
                    pe.wait_ge(xT_done, e + 3)
                    pick(e + 2)
                    down_products(KF - 1)
                turns(pe, body)
                turn_y(E_N - 1, 0)
                turn_y(E_N - 1, 1)

            @block.scalar
            def _(act):
                act.wait_ge(zeroed, 2)
                for t in range(TILES):
                    act.dma_start(T["moe"][t * P:(t + 1) * P, :], ye[:]).then_inc(cleared, 16)

                def body(e, s, first):
                    for j in range(KF):
                        act.wait_ge(h_prod, e * KF + j + 2)
                        if not (first and j < 2):
                            act.wait_ge(h_done, e * KF + j)
                        act.activation(en[:, j % 2], hb[:, j % 2, 0:CAP], ACT.Silu).then_inc(silu_done, 1)
                    act.wait_ge(w_used[RING - 1], e * PER + PER + 1)
                    for b in (1, 2):
                        n = min(PER_BANK, KD - b * PER_BANK)
                        ins = act.activation(yT[:, b * PER_BANK:b * PER_BANK + n, :].rearrange("p k n -> p (k n)"), acc[:, b, 0:n * CAP], ACT.Copy)
                    ins.then_inc(yT_done, 1)
                turns(act, body)

            @block.vector
            def _(dve):
                own, step = dsem, Steps()
                dve.memset(counts[:], 0.0).then_inc(own, step())
                dve.tensor_tensor(later[:], B.masks[:, 2, :], B.ident, ALU.subtract).then_inc(own, step())
                dve.tensor_copy(pair[:, :, 0], B.ids[:, 0:TILES]).then_inc(own, step())

                def rank_tile(t):
                    mine = pair[:, t, 1:2]
                    lo, hi = (0, SEQ) if t == 0 else (SEQ, ROWS)
                    a, b = t * P, (t + 1) * P
                    dve.wait_ge(own, step.n)
                    if a > lo:
                        dve.tensor_scalar(junk[:, 0:a - lo], row[:, lo:a], mine, 0.0, ALU.is_ge, ALU.add, accum_out=counts[:, t, 0:1]).then_inc(own, step())
                    dve.tensor_scalar(junk[:, a - lo:hi - lo], row[:, a:hi], mine, 0.0, ALU.is_gt, ALU.add, accum_out=counts[:, t, 1:2]).then_inc(own, step())
                    dve.wait_ge(own, step.n)
                    dve.scalar_tensor_tensor(junk[:, 0:P], row[:, a:b], mine, later[:], ALU.is_equal, ALU.mult, accum_out=counts[:, t, 2:3]).then_inc(own, step())

                def rank_start(e):
                    dve.wait_ge(row_in, e * 16 + 17)
                    dve.tensor_copy(pair[:, :, 1], B.aff[:, :, e]).then_inc(own, step())

                def rank_end():
                    dve.wait_ge(own, step.n)
                    dve.tensor_reduce(rank[:], counts[:], AX.X, ALU.add).then_inc(own, step())
                    dve.wait_ge(own, step.n)
                    dve.sem_inc(ranked, 1)
                    slots = B.ids[:, TILES:TILES + P].unsqueeze(1).to_broadcast([P, TILES, P])
                    dve.tensor_tensor(sel[:], slots, rank[:].unsqueeze(2).to_broadcast([P, TILES, P]), ALU.is_equal).then_inc(sel_done, 1)

                def rank_picked(e):
                    dve.wait_ge(picked, e + 2)
                    for src, n, k in ((slot_s, P, 0), (slot_p, CAP_P, 1)):
                        dve.tensor_copy(token[0:n, k, bass.ds(e, 1)], src[:, 0:1]).then_inc(own, step())
                        dve.tensor_copy(gate[0:n, k, bass.ds(e, 1)], src[:, 1:2]).then_inc(own, step())

                def index(idx, e, signal):
                    if step.count:
                        dve.wait_ge(own, step.n)
                    dve.tensor_copy(idx[:, 0:1], token[:, 0, bass.ds(e, 1)]).then_inc(own, step())
                    dve.tensor_copy(idx[0:CAP_P, 1:2], token[0:CAP_P, 1, bass.ds(e, 1)]).then_inc(own, step())
                    dve.wait_ge(own, step.n)
                    if signal:
                        dve.sem_inc(signal, 1)

                def modulate(e, s):
                    dve.wait_ge(turned, e + 2)
                    for k in range(KD):
                        dve.tensor_scalar(xT[:, s, k, 0:CAP_S], tr[:, k * P:(k + 1) * P], B.scale[:, 1, 1, k:k + 1], B.shift[:, 1, 1, k:k + 1], ALU.mult, ALU.add).then_inc(own, step())
                    tp = trp[:, 0:KD * CAP_P].rearrange("p (k n) -> p k n", n=CAP_P)
                    sc, sh = (a[:, 0, 1, :].unsqueeze(2).to_broadcast([P, KD, CAP_P]) for a in (B.scale, B.shift))
                    dve.tensor_tensor(xT[:, s, :, CAP_S:], tp, sc, ALU.mult).then_inc(own, step())
                    dve.wait_ge(own, step.n)
                    dve.tensor_tensor(xT[:, s, :, CAP_S:], xT[:, s, :, CAP_S:], sh, ALU.add).then_inc(xT_done, 1)

                def output(e, half):
                    dve.wait_ge(y_turned, e * 2 + half + 2)
                    if half == 0:
                        dve.tensor_scalar(ye[:], tr[:], gate[:, 0, bass.ds(e, 1)], None, ALU.mult).then_inc(own, step())
                    dve.tensor_scalar(yp[:, half * 512:(half + 1) * 512], trp[0:CAP_P, :], gate[0:CAP_P, 1, bass.ds(e, 1)], None, ALU.mult).then_inc(own, step())
                    dve.wait_ge(own, step.n)
                    dve.sem_inc(half_done if half == 0 else y_done, 1)

                for e in range(2):
                    rank_start(e)
                    for t in range(TILES):
                        rank_tile(t)
                    rank_end()
                    rank_picked(e)
                index(g_idx, 0, idx_done)
                modulate(0, 0)
                dve.wait_ge(cleared, 16 * TILES + 1)
                dve.wait_ge(own, step.n)
                dve.sem_clear(own)
                step.restart()

                def body(e, s, first):
                    for j in range(KF):
                        b = j % 2
                        dve.wait_ge(silu_done, e * KF + j + 2)
                        dve.tensor_tensor(hT[:, b, :], en[:, b], hb[:, b, CAP:2 * CAP], ALU.mult).then_inc(h_done, 1)
                        if j == 0:
                            dve.tensor_copy(pair[:, :, 1], B.aff[:, :, e + 2]).then_inc(own, step())
                            index(g_idx, e + 1, idx_done)
                            if not first:
                                dve.wait_ge(rows_added, e)
                                index(s_idx, e - 1, None)
                                output(e - 1, 0)
                            dve.wait_ge(row_in, e * 16 + 49)
                        if j == 1 and not first:
                            output(e - 1, 1)
                        if j == 5:
                            modulate(e + 1, 1 - s)
                        if j == 6:
                            rank_end()
                        for t in ((), (0, 1), (2, 3), (4, 5), (6, 7), (8,), (), ())[j]:
                            rank_tile(t)
                    rank_picked(e + 2)
                    dve.wait_ge(w_used[RING - 1], e * PER + PER + 1)
                    dve.tensor_copy(yT[:, 0:PER_BANK, :].rearrange("p k n -> p (k n)"), acc[:, 0, 0:PER_BANK * CAP]).then_inc(own, step())
                    dve.wait_ge(own, step.n)
                    dve.sem_clear(own)
                    step.restart()
                    dve.sem_inc(yT_done, 1)
                turns(dve, body)
                dve.wait_ge(rows_added, E_N)
                index(s_idx, E_N - 1, None)
                output(E_N - 1, 0)
                output(E_N - 1, 1)


def expert_residual(nc, T, B, l):
    with stage(nc, "resid") as st:
        y = st.sb("y", [P, 2, D])
        sq = st.sb("sq", [P, D])
        rs = st.sb("rs", [P, 2])
        y_in, rs_done, added = [st.sem("y_in0"), st.sem("y_in1")], st.sem("rs_done"), st.sem("added")
        asem, dsem = st.sem("act_steps"), st.sem("dve_steps")
        with st.block() as block:
            @block.sync
            def _(sp):
                for t in range(TILES):
                    sp.wait_ge(added, t - 1 + 1)
                    sp.dma_start(y[:, t % 2], T["moe"][t * P:(t + 1) * P, :]).then_inc(y_in[t % 2], 16)

            @block.scalar
            def _(act):
                own, step = asem, Steps()
                for t in range(TILES):
                    r = rs[:, t % 2:t % 2 + 1]
                    act.wait_ge(y_in[t % 2], 16 * (t // 2 + 1) + 1)
                    act.activation(sq[:], y[:, t % 2], ACT.Square, accum_out=r).then_inc(own, step())
                    act.wait_ge(own, step.n)
                    act.activation(r, r, ACT.Ln, bias=B.eps[:, 0:1], scale=1.0 / D).then_inc(own, step())
                    act.wait_ge(own, step.n)
                    act.activation(r, r, ACT.Exp, scale=-0.5).then_inc(rs_done, 1)

            @block.vector
            def _(dve):
                own, step = dsem, Steps()
                for t in range(TILES):
                    dve.wait_ge(rs_done, t + 2)
                    yt = y[:, t % 2]
                    dve.scalar_tensor_tensor(yt, yt, rs[:, t % 2:t % 2 + 1], B.gate[:, 1, 1 if t else 0, :], ALU.mult, ALU.mult).then_inc(own, step())
                    dve.wait_ge(own, step.n)
                    dve.tensor_tensor(B.x[:, t, :], B.x[:, t, :], yt, ALU.add).then_inc(added, 1)


def store_outputs(nc, T, B):
    with stage(nc, "store") as st:
        stored = st.sem("stored")
        with st.block() as block:
            @block.sync
            def _(sp):
                sp.dma_start(T["y_prompt"][0], B.x[:, 0, :]).then_inc(stored, 16)
                sp.dma_start(T["y_sample"][0].rearrange("(t p) d -> p t d", p=P), B.x[:, 1:TILES, :]).then_inc(stored, 16)
                sp.wait_ge(stored, 33)


class Buffers:
    pass


def host_constants():
    j, i = np.arange(P)[:, None], np.arange(P)[None, :]
    up_f = (j <= i).astype(np.float32)
    up_b = (j >= i).astype(np.float32)
    m = [np.eye(P, dtype=np.float32), up_f, up_b,
         up_f - up_f[:, P // 2 - 1:P // 2], up_b - up_b[:, P // 2:P // 2 + 1]]
    for back in (0, 1):
        b = 1
        while b < P:
            lev = (j // (2 * b) == i // (2 * b)) & (i % (2 * b) >= b) & (j % (2 * b) < b)
            m.append((lev.T if back else lev).astype(np.float32))
            b *= 2
    masks = np.stack(m, 1)
    half = ROPE // 2
    freqs = (ROPE_BASE ** (-np.arange(0, half, 2, dtype=np.float32) / half)).astype(np.float32)
    t = np.arange(DEC)
    row, col = (t // GRID_W).astype(np.float32), (t % GRID_W).astype(np.float32)
    ang = np.concatenate([row[:, None] * freqs, col[:, None] * freqs], -1)
    rope = np.stack([np.cos(ang), np.sin(ang)], 1).astype(np.float32)
    rope = np.concatenate([np.stack([np.ones((P, half)), np.zeros((P, half))], 1).astype(np.float32), rope])
    rope = np.ascontiguousarray(rope.reshape(TILES, P, 2, half).transpose(1, 0, 2, 3))
    ids = np.zeros((P, TILES + P + 4), np.float32)
    ids[:, :TILES] = np.arange(ROWS).reshape(TILES, P).T
    ids[:, TILES:TILES + P] = np.arange(P)[None, :]
    ids[:, TILES + P:] = np.stack([up_f[:, P // 2 - 1], np.ones(P), up_b[:, P // 2], np.ones(P)], 1)
    return {"masks": masks, "rope": rope, "ids": ids}


OUTS = [("y_prompt", (1, SEQ, D)), ("y_sample", (1, DEC, D)), ("new_ckv", (1, DEPTH, SEQ, KVL)),
        ("new_krope", (1, DEPTH, SEQ, ROPE)), ("new_gla", (1, DEPTH, 2, H_GLA, GK, GK)),
        ("new_gdn", (1, DEPTH, 2, H_GDN, GK, GK))]
SCRATCH = [("mod", (2, 6 * D)), ("proj", (ROWS + 3, IN_DIM)), ("qkv", (ROWS, 3 * DQ)), ("gates", (ROWS, 32)),
           ("gla_la", (ROWS, 2 * GQ)), ("mla_out", (ROWS, 256)), ("scan_f", (ROWS, 768)), ("scan_b", (ROWS, 768)),
           ("xhat", (ROWS, D)), ("affT", (E_N + 2, ROWS)), ("moe", (ROWS, D))]


def build(nc, T, last_stage=99):
    with ExitStack() as ctx:
        B = Buffers()
        sb = lambda n, s: ctx.enter_context(nc.sbuf_tensor(n, s, F32))
        B.gathered = ctx.enter_context(nc.semaphore("gathered"))
        B.scattered = ctx.enter_context(nc.semaphore("scattered"))
        B.x = sb("x_res", [P, TILES, D])
        B.masks = sb("masks_sb", [P, 19, P])
        B.ident = B.masks[:, 0, :]
        B.rope = sb("rope_sb", [P, TILES, 2, ROPE // 2])
        B.ids = sb("ids_sb", [P, TILES + P + 4])
        B.midcols = B.ids[:, TILES + P:]
        B.zero = sb("zero", [P, 32])
        B.ones = sb("ones", [P, P])
        B.eps = sb("eps", [P, 1])
        B.scale = sb("scale", [P, 2, 2, KD])
        B.shift = sb("shift", [P, 2, 2, KD])
        B.gate = sb("gate", [P, 2, 2, D])
        B.aff = sb("aff", [P, TILES, E_N + 2])
        ctx.enter_context(nc.allow_non_contiguous_dma(reason="small tables are turned on the way in"))
        load_constants(nc, T, B)
        with nc.Fori(0, DEPTH if last_stage > 8 else 1) as l:
            modulation(nc, T, B, l)
            with nc.sbuf_tensor("xmT", [P, KD, ROWS], F32) as xmT:
                if last_stage > 0:
                    input_norm(nc, T, B, l, xmT)
                if last_stage > 1:
                    input_projection(nc, T, B, l, xmT)
            if last_stage > 2:
                latent_attention(nc, T, B, l)
            if last_stage > 3:
                scan_inputs(nc, T, B, l)
            if last_stage > 4:
                scan(nc, T, B, l, True)
                scan(nc, T, B, l, False)
            if last_stage > 5:
                mixer_output(nc, T, B, l)
            if last_stage > 6:
                experts(nc, T, B, l)
            if last_stage > 7:
                expert_residual(nc, T, B, l)
        store_outputs(nc, T, B)


def kernel(**inputs):
    import concourse.bacc as bacc
    from concourse.bass_utils import run_bass_kernel_spmd

    nc = bacc.Bacc("TRN2", target_bir_lowering=False, num_devices=1)
    arrays, T = {}, {}
    for name, a in {**inputs, **host_constants()}.items():
        arrays[f"in_{name}"] = np.ascontiguousarray(a)
        T[name] = nc.dram_tensor(f"in_{name}", arrays[f"in_{name}"].shape, F32, kind="ExternalInput").ap()
    for name, shape in OUTS:
        T[name] = nc.dram_tensor(f"out_{name}", shape, F32, kind="ExternalOutput").ap()
    for name, shape in SCRATCH:
        T[name] = nc.dram_tensor(f"scratch_{name}", shape, F32, kind="Internal").ap()
    build(nc, T)
    r = run_bass_kernel_spmd(nc, [arrays], core_ids=[0])
    return tuple(r.results[0][f"out_{name}"] for name, _ in OUTS)
```

```python
from contextlib import ExitStack, contextmanager

import numpy as np
import concourse.bass as bass
from concourse import mybir

F32 = mybir.dt.float32
I32 = mybir.dt.int32
U32 = mybir.dt.uint32
ALU = mybir.AluOpType
ACT = mybir.ActivationFunctionType
AX = mybir.AxisListType

P = 128
D = 1024
KD = D // P
DEPTH = 2
SEQ = 128
DEC = 1024
PAST = 128
ROWS = SEQ + DEC
TILES = ROWS // P
EPS = 1e-6
GRID_W = 64
H_MLA, NOPE, ROPE, VD = 4, 64, 32, 64
QL, KVL = 256, 128
QD = NOPE + ROPE
MLA_SCALE = float(NOPE + ROPE) ** -0.5
ROPE_BASE = 10000.0
H_GLA, GK = 4, 64
RANK = 16
TAU = 16.0
H_GDN = 8
GQ = H_GLA * GK
DQ = H_GDN * GK
IN_DIM = 3552
C_QLAT, C_KVLAT, C_KROPE = 0, 256, 384
C_GQ, C_GK, C_GV, C_GLR, C_GZ = 416, 672, 928, 1184, 1216
C_DQ, C_DK, C_DV, C_DZ, C_DB, C_DA = 1472, 1984, 2496, 3008, 3520, 3536
E_N = 16
FF = 1024
KF = FF // P
CAP_S = 2 * DEC // E_N
CAP_P = 2 * SEQ // E_N
CAP = CAP_S + CAP_P
NEG = -1e30


class Steps:

    def __init__(self):
        self.count = 0

    def __call__(self):
        self.count += 1
        return 1

    @property
    def n(self):
        assert self.count > 0
        return self.count

    def restart(self):
        self.count = 0


class Stage:
    def __init__(self, nc, name, ctx):
        self.nc, self.name, self.ctx, self.sems = nc, name, ctx, []

    def sb(self, name, shape, dt=F32):
        return self.ctx.enter_context(self.nc.sbuf_tensor(f"{self.name}_{name}", shape, dt))

    def ps(self, name, shape, dt=F32):
        return self.ctx.enter_context(self.nc.psum_tensor(f"{self.name}_{name}", shape, dt))

    def sem(self, name):
        s = self.ctx.enter_context(self.nc.semaphore(f"{self.name}_{name}"))
        self.sems.append(s)
        if not name.endswith("_steps"):
            self.shared(len(self.sems)).sem_inc(s, 1)
        return s

    def shared(self, n):
        return (self.nc.gpsimd, self.nc.vector, self.nc.scalar)[n % 3]

    def block(self):
        self.nc.all_engine_barrier()
        return self.nc.Block()


@contextmanager
def stage(nc, name):
    with ExitStack() as ctx:
        st = Stage(nc, name, ctx)
        yield st
        for n, s in enumerate(st.sems):
            st.shared(n + 1).sem_clear(s)
        nc.all_engine_barrier()


def bc(ap, shape):
    return ap.to_broadcast(shape)


class Turns:

    def __init__(self, base):
        self.base, self.n = base, 0

    def next(self):
        self.n += 1
        return self.base + (self.n + 1)


def load_constants(nc, T, B):
    with stage(nc, "init") as st:
        loaded, zeroed, stored = st.sem("loaded"), st.sem("zeroed"), st.sem("stored")
        with st.block() as block:
            @block.vector
            def _(dve):
                dve.memset(B.zero[:], 0.0).then_inc(zeroed, 1)
                dve.memset(B.ones[:], 1.0).then_inc(zeroed, 1)
                dve.memset(B.eps[:], EPS).then_inc(zeroed, 1)

            @block.sync
            def _(sp):
                n = 0
                for dst, src in ((B.masks[:], T["masks"]), (B.rope[:], T["rope"]), (B.ids[:], T["ids"]),
                                 (B.x[:, 0, :], T["x_prompt"][0]),
                                 (B.x[:, 1:TILES, :], T["x_sample"][0].rearrange("(t p) d -> p t d", p=P))):
                    sp.dma_start(dst, src).then_inc(loaded, 16)
                    n += 16
                sp.wait_ge(zeroed, 4)
                for row in (0, 1 + SEQ, 2 + ROWS):
                    sp.dma_start(T["proj"][row, :].rearrange("(p c) -> p c", c=32), B.zero[0:IN_DIM // 32, :]).then_inc(stored, 16)
                sp.wait_ge(loaded, n + 1)
                sp.wait_ge(stored, 49)


def modulation(nc, T, B, l):
    NB = 512
    with stage(nc, "mod") as st:
        cond = st.sb("cond", [P, 2, KD])
        e = st.sb("e", [P, 2, KD])
        w = st.sb("w", [P, 2, KD, NB])
        row = st.sb("row", [2, 6 * D])
        bias = st.sb("bias", [2, 6 * D])
        colT = st.sb("colT", [P, 2, 4, KD])
        gainT = st.sb("gainT", [P, 2, KD])
        gain = st.sb("gain", [P, 2, D])
        acc = st.ps("acc", [P, 2, 512])
        cond_in, w_in = st.sem("cond_in"), [st.sem("w_in0"), st.sem("w_in1")]
        exp_done, silu_done, prod_done = (st.sem(x) for x in ("exp_done", "silu_done", "prod_done"))
        row_done = [st.sem("row_done0"), st.sem("row_done1")]
        row_out, table_in, step_sem = st.sem("row_out"), st.sem("table_in"), st.sem("dve_steps")
        with st.block() as block:
            @block.sync
            def _(sp):
                sp.dma_start(cond[:, 0, :], T["c_ctx"].rearrange("(k p) -> p k", p=P)).then_inc(cond_in, 16)
                sp.dma_start(cond[:, 1, :], T["c"][0].rearrange("(k p) -> p k", p=P)).then_inc(cond_in, 16)
                sp.dma_start(bias[:], T["b_mod"][l].partition_broadcast(2)).then_inc(cond_in, 16)
                wsrc = T["w_mod"].rearrange("l (k p) n -> l p k n", p=P)
                with sp.Fori(0, 6) as n:
                    col = sp.snap(n * (2 * NB))
                    for s in range(2):
                        sp.wait_ge(row_done[s], n + 1)
                        sp.dma_start(w[:, s], wsrc[l, :, :, bass.ds(col + s * NB, NB)]).then_inc(w_in[s], 16)
                for s in range(2):
                    sp.wait_ge(row_done[s], 7)
                sp.dma_start(T["mod"], row[:]).then_inc(row_out, 16)
                sp.wait_ge(row_out, 17)
                n = 0
                for c in range(2):
                    for i, j in enumerate((0, 1, 3, 4)):
                        sp.dma_start(colT[:, c, i, :], T["mod"][c, j * D:(j + 1) * D].rearrange("(k p) -> p k", p=P)).then_inc(table_in, 16)
                    for i, j in enumerate((2, 5)):
                        sp.dma_start(B.gate[:, i, c, :], T["mod"][c, j * D:(j + 1) * D].partition_broadcast(P)).then_inc(table_in, 16)
                for i in range(2):
                    sp.dma_start(gainT[:, i, :], T["sandwich_norms"][l, 2 * i].rearrange("(k p) -> p k", p=P)).then_inc(table_in, 16)
                    sp.dma_start(gain[:, i, :], T["sandwich_norms"][l, 2 * i + 1].partition_broadcast(P)).then_inc(table_in, 16)

            @block.scalar
            def _(act):
                act.wait_ge(cond_in, 49)
                act.activation(e[:], cond[:], ACT.Exp, scale=-1.0).then_inc(exp_done, 1)

            @block.tensor
            def _(pe):
                pe.wait_ge(silu_done, 2)
                with pe.Fori(0, 6) as n:
                    for s in range(2):
                        pe.wait_ge(w_in[s], n * 16 + 17)
                        pe.wait_ge(row_done[s], n + 1)
                        for k in range(KD):
                            mm = pe.matmul(acc[0:2, s, :], e[:, :, k], w[:, s, k, :], start=k == 0, stop=k == KD - 1)
                        mm.then_inc(prod_done, 1)

            @block.vector
            def _(dve):
                own, step = step_sem, Steps()
                dve.wait_ge(exp_done, 2)
                dve.tensor_scalar(e[:], e[:], 1.0, None, ALU.add).then_inc(own, step())
                dve.wait_ge(own, step.n)
                dve.reciprocal(e[:], e[:]).then_inc(own, step())
                dve.wait_ge(own, step.n)
                dve.tensor_tensor(e[:], e[:], cond[:], ALU.mult).then_inc(silu_done, 1)
                for n in range(12):
                    dve.wait_ge(prod_done, n + 2)
                    c = slice(n * NB, (n + 1) * NB)
                    dve.tensor_tensor(row[:, c], acc[0:2, n % 2, :], bias[:, c], ALU.add).then_inc(row_done[n % 2], 1)
                dve.wait_ge(table_in, 16 * 16 + 1)
                for c in range(2):
                    for i in range(2):
                        dve.scalar_tensor_tensor(B.scale[:, c, i, :], colT[:, c, 2 * i + 1, :], 1.0, gainT[:, i, :], ALU.add, ALU.mult).then_inc(own, step())
                        dve.tensor_copy(B.shift[:, c, i, :], colT[:, c, 2 * i, :]).then_inc(own, step())
                        dve.tensor_tensor(B.gate[:, i, c, :], B.gate[:, i, c, :], gain[:, i, :], ALU.mult).then_inc(own, step())
                dve.wait_ge(own, step.n)


def input_norm(nc, T, B, l, xmT):
    G = 3
    with stage(nc, "norm") as st:
        sq = st.sb("sq", [P, G, D])
        ss = st.sb("ss", [P, G])
        xhat = st.sb("xhat", [P, G, D])
        tr = st.ps("tr", [P, G, KD, P])
        rs_done, xhat_done, tr_done = (st.sem(x) for x in ("rs_done", "xhat_done", "tr_done"))
        act_steps, dve_steps = st.sem("act_steps"), st.sem("dve_steps")
        with st.block() as block:
            @block.scalar
            def _(act):
                own, step = act_steps, Steps()
                with act.Fori(0, TILES // G) as g:
                    act.wait_ge(xhat_done, g * G + 1)
                    for j in range(G):
                        act.activation(sq[:, j], B.x[:, g * G + j, :], ACT.Square, accum_out=ss[:, j:j + 1]).then_inc(own, step())
                    act.wait_ge(own, step.n)
                    act.activation(ss[:], ss[:], ACT.Ln, bias=B.eps[:, 0:1], scale=1.0 / D).then_inc(own, step())
                    act.wait_ge(own, step.n)
                    act.activation(ss[:], ss[:], ACT.Exp, scale=-0.5).then_inc(rs_done, 1)
                    act.sem_clear(own)
                    step.restart()

            @block.vector
            def _(dve):
                own, step = dve_steps, Steps()

                def body(g):
                    dve.wait_ge(rs_done, g + 2)
                    for j in range(G):
                        dve.tensor_scalar(xhat[:, j], B.x[:, g * G + j, :], ss[:, j:j + 1], None, ALU.mult).then_inc(xhat_done, 1)
                    for j in range(G):
                        c = 0 if isinstance(g, int) and j == 0 else 1
                        dve.wait_ge(tr_done, g * G + (j + 2))
                        for k in range(KD):
                            dve.tensor_scalar(xmT[:, k, bass.ds(g * (G * P) + j * P, P)], tr[:, j, k, :], B.scale[:, c, 0, k:k + 1],
                                              B.shift[:, c, 0, k:k + 1], ALU.mult, ALU.add).then_inc(own, step())
                    dve.wait_ge(own, step.n)
                    dve.sem_clear(own)
                    step.restart()
                body(0)
                with dve.Fori(1, TILES // G) as g:
                    body(g)

            @block.tensor
            def _(pe):
                with pe.Fori(0, TILES // G) as g:
                    for j in range(G):
                        pe.wait_ge(xhat_done, g * G + (j + 2))
                        for k in range(KD):
                            mm = pe.transpose(tr[:, j, k, :], xhat[:, j, k * P:(k + 1) * P], B.ident)
                        mm.then_inc(tr_done, 1)


def proj_row(t):
    return 1 if isinstance(t, int) and t == 0 else t * P + 2


def input_projection(nc, T, B, l, xmT):
    NB = IN_DIM // 8
    BANKS = 3
    with stage(nc, "proj") as st:
        w = st.sb("w", [P, 2, KD, NB])
        out = st.sb("out", [P, BANKS, NB])
        acc = st.ps("acc", [P, BANKS, 512])
        w_in = [st.sem("w_in0"), st.sem("w_in1")]
        w_used = [st.sem("w_used0"), st.sem("w_used1")]
        prod_done, copied = st.sem("prod_done"), st.sem("copied")
        stored = [st.sem(f"stored{i}") for i in range(BANKS)]
        with st.block() as block:
            @block.sync
            def _(sp):
                wsrc = T["w_in"].rearrange("l (k p) n -> l p k n", p=P)
                with sp.Fori(0, 4) as n:
                    for s in range(2):
                        col = sp.snap(n * (2 * NB) + s * NB)
                        sp.wait_ge(w_used[s], n + 1)
                        sp.dma_start(w[:, s], wsrc[l, :, :, bass.ds(col, NB)]).then_inc(w_in[s], 16)

            @block.tensor
            def _(pe):
                with pe.Fori(0, 4) as n:
                    for s in range(2):
                        pe.wait_ge(w_in[s], n * 16 + 17)
                        for t in range(TILES):
                            i = s * TILES + t
                            b = i % BANKS
                            if i >= BANKS:
                                pe.wait_ge(copied, n * (2 * TILES) + (i - BANKS + 1) + 1)
                            else:
                                pe.wait_ge(copied, n * (2 * TILES) + 1)
                            for k in range(KD):
                                mm = pe.matmul(acc[:, b, 0:NB], xmT[:, k, t * P:(t + 1) * P], w[:, s, k, :],
                                               start=k == 0, stop=k == KD - 1)
                            mm.then_inc(prod_done, 1)

            @block.vector
            def _(dve):
                with dve.Fori(0, 4) as n:
                    for i in range(2 * TILES):
                        b = i % BANKS
                        dve.wait_ge(prod_done, n * (2 * TILES) + (i + 1) + 1)
                        dve.wait_ge(stored[b], n * (16 * 2 * TILES // BANKS) + 16 * (i // BANKS) + 1)
                        if i % TILES == TILES - 1:
                            dve.sem_inc(w_used[i // TILES], 1)
                        dve.tensor_copy(out[:, b, :], acc[:, b, 0:NB]).then_inc(copied, 1)

            @block.scalar
            def _(act):
                with act.Fori(0, 4) as n:
                    for i in range(2 * TILES):
                        b, s, t = i % BANKS, i // TILES, i % TILES
                        r = proj_row(t)
                        col = act.snap(n * (2 * NB) + s * NB)
                        act.wait_ge(copied, n * (2 * TILES) + (i + 1) + 1)
                        act.dma_start(T["proj"][r:r + P, bass.ds(col, NB)], out[:, b, :]).then_inc(stored[b], 16)
                for b in range(BANKS):
                    act.wait_ge(stored[b], 4 * 16 * 2 * TILES // BANKS + 1)


def rotate(own, step, dve, out, x, cos, sin, tmp):
    x1, x2 = x[..., 0::2], x[..., 1::2]
    dve.tensor_tensor(tmp[0], x1, cos, ALU.mult).then_inc(own, step())
    dve.tensor_tensor(tmp[1], x2, sin, ALU.mult).then_inc(own, step())
    dve.tensor_tensor(tmp[2], x1, sin, ALU.mult).then_inc(own, step())
    dve.tensor_tensor(tmp[3], x2, cos, ALU.mult).then_inc(own, step())
    dve.wait_ge(own, step.n)
    dve.tensor_tensor(out[..., 0::2], tmp[0], tmp[1], ALU.subtract).then_inc(own, step())
    dve.tensor_tensor(out[..., 1::2], tmp[2], tmp[3], ALU.add).then_inc(own, step())


def latent_attention(nc, T, B, l):
    with nc.sbuf_tensor("keysT", [P, H_MLA, 10 * P], F32) as keysT, nc.sbuf_tensor("values", [P, 10, H_MLA, VD], F32) as values:
        mixer_inputs(nc, T, B, l, keysT, values)
        attend(nc, T, B, l, keysT, values, True)
        attend(nc, T, B, l, keysT, values, False)


def attend(nc, T, B, l, keysT, values, prompt):
    NK = 1 if prompt else 9
    K0 = 0 if prompt else 1
    W = NK * P
    N = 1 if prompt else TILES - 1
    with stage(nc, "attp" if prompt else "atts") as st:
        qin = st.sb("qin", [P, QL])
        rs = st.sb("rs", [P, N])
        latents = st.sb("latents", [P, N, QL])
        qlT = st.sb("qlT", [P, 2, P])
        q = st.sb("q", [P, H_MLA, QD])
        qa = st.sb("qa", [P, H_MLA, P])
        qaT = st.sb("qaT", [P, 2, H_MLA, P])
        tmp = st.sb("tmp", [P, 4, H_MLA, ROPE // 2])
        gainT = st.sb("gainT", [P, 2])
        wq = st.sb("wq", [P, 2, H_MLA * QD])
        prob = st.sb("prob", [P, 2, W])
        probT = st.sb("probT", [P, 2, W])
        mx = st.sb("mx", [P, H_MLA])
        den = st.sb("den", [P, H_MLA])
        out = st.sb("out", [P, 2, H_MLA, VD])
        score, turned = st.ps("score", [P, 1536]), st.ps("turned", [P, 1536])
        misc, acc = st.ps("misc", [P, 512]), st.ps("acc", [P, 512])
        w_in, all_in, q_in, rs_done, q_ready, q_prod = (st.sem(x) for x in ("w_in", "all_in", "q_in", "rs_done", "q_ready", "q_prod"))
        score_done, max_done, exp_done, turn_done, probT_done, pv_done, head_out = (st.sem(x) for x in (
            "score_done", "max_done", "exp_done", "turn_done", "probT_done", "pv_done", "head_out"))
        stored = [st.sem("stored0"), st.sem("stored1")]
        asem, dsem = st.sem("act_steps"), st.sem("dve_steps")

        def turns(eng, body):
            if prompt:
                body(0, 0)
            else:
                with eng.Fori(0, N // 2 - 1) as j:
                    for s in range(2):
                        body(j * 2 + s, s)
                body(N - 2, 0)
                body(N - 1, 1)

        def more(i):
            return not isinstance(i, int) or i + 1 < N

        with st.block() as block:
            @block.sync
            def _(sp):
                first = proj_row(0 if prompt else 1)
                sp.dma_start(latents[:], T["proj"][first:first + N * P, 0:QL].rearrange("(t p) c -> p t c", p=P)).then_inc(all_in, 16)
                sp.dma_start(wq[:], T["mla_wq_b"][l].rearrange("(k p) n -> p k n", p=P)).then_inc(w_in, 16)
                sp.dma_start(gainT[:], T["mla_q_norm"][l].rearrange("(k p) -> p k", p=P)).then_inc(w_in, 16)

                def load(r, queries_before):
                    sp.wait_ge(q_prod, queries_before)
                    sp.dma_start(qin[:], T["proj"][bass.ds(r, P), 0:QL]).then_inc(q_in, 16)
                load(first, 1)

                def body(i, s):
                    fixed = (lambda x: x) if isinstance(i, int) else sp.snap
                    row = 0 if prompt else fixed(i * P + P)
                    tile_written = fixed(i * H_MLA + (H_MLA + 1))
                    if more(i):
                        load(fixed(i * P + (2 * P + 2)), fixed(i * 3 + 4))
                    sp.wait_ge(head_out, tile_written)
                    sp.dma_start(T["mla_out"][bass.ds(row, P), :], out[:, s].rearrange("p h e -> p (h e)")).then_inc(stored[s], 16)
                turns(sp, body)
                for s in range(1 if prompt else 2):
                    sp.wait_ge(stored[s], 16 * (1 if prompt else N // 2) + 1)

            @block.scalar
            def _(act):
                own, step = asem, Steps()

                act.wait_ge(all_in, 17)
                for t in range(N):
                    act.activation(latents[:, t, :], latents[:, t, :], ACT.Square, accum_out=rs[:, t:t + 1]).then_inc(own, step())
                act.wait_ge(own, step.n)
                act.activation(rs[:], rs[:], ACT.Ln, bias=B.eps[:, 0:1], scale=1.0 / QL).then_inc(own, step())
                act.wait_ge(own, step.n)
                act.activation(rs[:], rs[:], ACT.Exp, scale=-0.5).then_inc(rs_done, 1)

                def body(i, s):
                    for h in range(H_MLA):
                        act.wait_ge(max_done, i * H_MLA + h + 2)
                        act.activation(prob[:, h % 2, :], score[:, 0:W], ACT.Exp, bias=mx[:, h:h + 1], scale=MLA_SCALE,
                                       accum_out=den[:, h:h + 1]).then_inc(exp_done, 1)
                turns(act, body)

            @block.tensor
            def _(pe):
                pe.wait_ge(w_in, 33)

                def turn_latent(i):
                    pe.wait_ge(q_in, i * 16 + 17)
                    pe.wait_ge(q_ready, i * 3 + 1)
                    for k in range(2):
                        mm = pe.transpose(misc[:, k * P:(k + 1) * P], qin[:, k * P:(k + 1) * P], B.ident)
                    mm.then_inc(q_prod, 1)

                def project(i):
                    pe.wait_ge(q_ready, i * 3 + 2)
                    for k in range(2):
                        mm = pe.matmul(misc[:, 0:H_MLA * QD], qlT[:, k, :], wq[:, k, :], start=k == 0, stop=k == 1)
                    mm.then_inc(q_prod, 1)

                def turn_queries(i):
                    pe.wait_ge(q_ready, i * 3 + 3)
                    for h in range(H_MLA):
                        mm = pe.transpose(misc[:, h * P:(h + 1) * P], qa[:, h, :], B.ident)
                    mm.then_inc(q_prod, 1)

                def scores(i, s, h):
                    pe.wait_ge(q_ready, i * 3 + 4)
                    pe.wait_ge(exp_done, i * H_MLA + h + 1)
                    for c in range(0, W, 512):
                        n = min(512, W - c)
                        mm = pe.matmul(score[:, c:c + n], qaT[:, s, h, :], keysT[:, h, K0 * P + c:K0 * P + c + n], start=True, stop=True)
                    mm.then_inc(score_done, 1)

                def weigh_values(i, h):
                    pe.wait_ge(probT_done, i * H_MLA + h + 2)
                    pe.wait_ge(head_out, i * H_MLA + h + 1)
                    for k in range(NK):
                        mm = pe.matmul(acc[:, 0:VD], probT[:, h % 2, k * P:(k + 1) * P], values[:, K0 + k, h, :],
                                       start=k == 0, stop=k == NK - 1)
                    mm.then_inc(pv_done, 1)
                turn_latent(0)
                project(0)
                turn_queries(0)
                scores(0, 0, 0)

                def body(i, s):
                    for h in range(H_MLA):
                        if h + 1 < H_MLA:
                            scores(i, s, h + 1)
                        if more(i) and h < 3:
                            (turn_latent, project, turn_queries)[h](i + 1)
                        pe.wait_ge(exp_done, i * H_MLA + h + 2)
                        pe.wait_ge(probT_done, i * H_MLA + h + 1)
                        for k in range(NK):
                            mm = pe.transpose(turned[:, k * P:(k + 1) * P], prob[:, h % 2, k * P:(k + 1) * P], B.ident)
                        mm.then_inc(turn_done, 1)
                        if h:
                            weigh_values(i, h - 1)
                    if more(i):
                        scores(i + 1, 1 - s, 0)
                    weigh_values(i, H_MLA - 1)
                turns(pe, body)

            @block.vector
            def _(dve):
                own, step = dsem, Steps()
                dve.wait_ge(w_in, 33)

                def latent(i):
                    dve.wait_ge(q_prod, i * 3 + 2)
                    for k in range(2):
                        dve.tensor_scalar(qlT[:, k, :], misc[:, k * P:(k + 1) * P], gainT[:, k:k + 1], None, ALU.mult).then_inc(own, step())
                    dve.wait_ge(own, step.n)
                    dve.sem_inc(q_ready, 1)

                def queries(i):
                    dve.wait_ge(q_prod, i * 3 + 3)
                    dve.wait_ge(rs_done, 2)
                    dve.tensor_scalar(q[:].rearrange("p h e -> p (h e)"), misc[:, 0:H_MLA * QD], rs[:, i:i + 1] if isinstance(i, int) else rs[:, bass.ds(i, 1)], None, ALU.mult).then_inc(own, step())
                    dve.wait_ge(own, step.n)
                    dve.tensor_copy(qa[:, :, 0:NOPE], q[:, :, 0:NOPE]).then_inc(own, step())
                    dve.tensor_copy(qa[:, :, QD:P], q[:, :, NOPE:QD]).then_inc(own, step())
                    t = 0 if prompt else i + 1
                    cos, sin = (B.rope[:, t, j, :].unsqueeze(1).to_broadcast([P, H_MLA, ROPE // 2]) for j in range(2))
                    rotate(own, step, dve, qa[:, :, NOPE:QD], q[:, :, NOPE:QD], cos, sin, [tmp[:, j] for j in range(4)])
                    dve.wait_ge(own, step.n)
                    dve.sem_inc(q_ready, 1)

                def queries_turned(i, s):
                    dve.wait_ge(q_prod, i * 3 + 4)
                    dve.tensor_copy(qaT[:, s].rearrange("p h e -> p (h e)"), misc[:]).then_inc(q_ready, 1)
                latent(0)
                queries(0)
                queries_turned(0, 0)

                def softmax_max(i, h):
                    dve.wait_ge(score_done, i * H_MLA + h + 2)
                    dve.tensor_reduce(mx[:, h:h + 1], score[:, 0:W], AX.X, ALU.max).then_inc(own, step())
                    dve.wait_ge(own, step.n)
                    dve.tensor_scalar(mx[:, h:h + 1], mx[:, h:h + 1], -MLA_SCALE, None, ALU.mult).then_inc(max_done, 1)

                def output(i, s, h):
                    dve.wait_ge(pv_done, i * H_MLA + h + 2)
                    dve.reciprocal(den[:, h:h + 1], den[:, h:h + 1]).then_inc(own, step())
                    dve.wait_ge(own, step.n)
                    dve.tensor_scalar(out[:, s, h, :], acc[:, 0:VD], den[:, h:h + 1], None, ALU.mult).then_inc(head_out, 1)
                softmax_max(0, 0)
                dve.sem_clear(own)
                step.restart()

                def body(i, s):
                    dve.wait_ge(stored[s], 1 if prompt else (i // 2) * 16 + 1 if isinstance(i, int) else i * 8 + (1 - 8 * s))
                    for h in range(H_MLA):
                        if h > 1:
                            output(i, s, h - 2)
                        if h + 1 < H_MLA:
                            softmax_max(i, h + 1)
                        dve.wait_ge(turn_done, i * H_MLA + h + 2)
                        dve.tensor_copy(probT[:, h % 2, :], turned[:, 0:W]).then_inc(probT_done, 1)
                        if more(i) and h < 2:
                            (latent, queries)[h](i + 1)
                        if more(i) and h == 2:
                            queries_turned(i + 1, 1 - s)
                    output(i, s, H_MLA - 2)
                    if more(i):
                        softmax_max(i + 1, 0)
                    output(i, s, H_MLA - 1)
                    dve.sem_clear(own)
                    step.restart()
                turns(dve, body)


def mixer_inputs(nc, T, B, l, keysT, values):
    CW = 3 * DQ
    GB, GL = 2 * H_GDN, 2 * GQ
    with stage(nc, "inputs") as st:
        taps = st.sb("taps", [P, 2, 3, CW])
        wc = st.sb("wc", [P, 3, CW])
        y, tmp, sq = st.sb("y", [P, 2, CW]), st.sb("tmp", [P, 2, CW]), st.sb("sq", [P, 2 * DQ])
        ss = st.sb("ss", [P, 2 * H_GDN])
        ba = st.sb("ba", [P, 2, 2 * GB])
        eb = st.sb("eb", [P, 2, GB])
        ab = st.sb("ab", [P, GB])
        gates = st.sb("gates", [P, 2, 2 * GB])
        alog, dt = st.sb("alog", [P, GB]), st.sb("dt", [P, GB])
        lr = st.sb("lr", [P, 2, 2, RANK])
        lrT = st.sb("lrT", [RANK, 2, P])
        wg = st.sb("wg", [RANK, 2, GQ])
        bg = st.sb("bg", [P, GL])
        logit, absl, la = st.sb("logit", [P, GL]), st.sb("absl", [P, GL]), st.sb("la", [P, 2, GL])
        ptr, pl = st.ps("ptr", [P, 2, P]), st.ps("pl", [P, GL])
        w_in, t_in0, conv_done, silu_done, sq_done, rs_done, a_done, ln_done, logit_done, lnl_done = (st.sem(x) for x in (
            "w_in", "t_in0", "conv_done", "silu_done", "sq_done", "rs_done", "a_done", "ln_done", "logit_done", "lnl_done"))
        lr_turned, lrT_done, pl_done, ready, gates_ready, mixed, ss_done = (
            st.sem(x) for x in ("lr_turned", "lrT_done", "pl_done", "ready", "gates_ready", "mixed", "ss_done"))
        t_in = [t_in0, st.sem("t_in1")]
        stored = [st.sem("stored0"), st.sem("stored1")]
        asem, dsem, psem = st.sem("act_steps"), st.sem("dve_steps"), st.sem("pool_steps")
        kin = st.sb("kin", [P, KVL + ROPE])
        ckv = st.sb("ckv", [P, KVL])
        ckvT = st.sb("ckvT", [P, P])
        ka = st.sb("ka", [P, H_MLA, P])
        kr = st.sb("kr", [P, ROPE])
        ktmp = st.sb("ktmp", [P, 4, ROPE // 2])
        ksq = st.sb("ksq", [P, KVL])
        rs = st.sb("rs", [P, 1])
        gain = st.sb("gain", [P, KVL])
        wkv = st.sb("wkv", [P, 512])
        tr, kv, trk = st.ps("tr", [P, 512]), st.ps("kv", [P, 512]), st.ps("trk", [P, H_MLA, P])
        kw_in, k_in, krs_done, to_pe, from_pe, turn_done, kstored = (
            st.sem(x) for x in ("kw_in", "k_in", "krs_done", "to_pe", "from_pe", "turn_done", "kstored"))

        def turns(eng, keys, start, tile, settle):
            keys(0, "prompt")
            keys(1, "context")
            start(0, 0, 0)
            settle()
            pairs = (TILES - 1) // 2
            with eng.Fori(0, pairs - 1) as i:
                for s in range(2):
                    tile(i * 2 + s, s, i)
                settle()
            for t in range(TILES - 3, TILES):
                tile(t, t % 2, t // 2)
            settle()

        def more(t):
            return not isinstance(t, int) or t + 1 < TILES

        with st.block() as block:
            @block.sync
            def _(sp):
                for dst, src in ((wc[:].rearrange("p a c -> p (a c)"), T["gdn_conv"][l].rearrange("a c -> (a c)").partition_broadcast(P)),
                                 (alog[:], T["gdn_a_log"][l].rearrange("a c -> (a c)").partition_broadcast(P)),
                                 (dt[:], T["gdn_dt_bias"][l].rearrange("a c -> (a c)").partition_broadcast(P)),
                                 (bg[:], T["gla_bg"][l].rearrange("a c -> (a c)").partition_broadcast(P)),
                                 (wg[:], T["gla_wg"][l].rearrange("a r c -> r a c"))):
                    sp.dma_start(dst, src).then_inc(w_in, 16)
                sp.dma_start(wkv[:], T["mla_wkv_b"][l]).then_inc(kw_in, 16)
                sp.dma_start(gain[:], T["mla_kv_norm"][l].partition_broadcast(P)).then_inc(kw_in, 16)

                def load_keys(kind, row):
                    if kind == "context":
                        sp.dma_start(kin[:, 0:KVL], T["cache_ckv"][0, l]).then_inc(k_in, 16)
                        sp.dma_start(kin[:, KVL:], T["cache_krope"][0, l]).then_inc(k_in, 16)
                    else:
                        src = T["proj"][bass.ds(row, P)]
                        sp.dma_start(kin[:, 0:KVL], src[:, C_KVLAT:C_KROPE]).then_inc(k_in, 16)
                        sp.dma_start(kin[:, KVL:], src[:, C_KROPE:C_GQ]).then_inc(k_in, 16)

                def load(s, r, above, below):
                    for j, first in enumerate((above, r, below)):
                        sp.dma_start(taps[:, s, j, :], T["proj"][bass.ds(first, P), C_DQ:C_DZ]).then_inc(t_in[s], 16)
                    sp.dma_start(ba[:, s, :], T["proj"][bass.ds(r, P), C_DB:IN_DIM]).then_inc(t_in[s], 16)
                    sp.dma_start(lr[:, s].rearrange("p a r -> p (a r)"), T["proj"][bass.ds(r, P), C_GLR:C_GZ]).then_inc(t_in[s], 16)

                load_keys("prompt", 1)
                load(0, 1, 0, 2)
                sp.wait_ge(to_pe, 2)
                sp.dma_start(T["new_ckv"][0, l], ckv[:]).then_inc(kstored, 16)
                sp.dma_start(T["new_krope"][0, l], kin[:, KVL:]).then_inc(kstored, 16)
                sp.wait_ge(kstored, 33)
                sp.wait_ge(turn_done, 2)
                load_keys("context", 0)

                load(1, P + 2, P + 1, P + 3)

                def tile(t, s):
                    fixed = (lambda x: x) if isinstance(t, int) else sp.snap
                    row, key_row = fixed(t * P), fixed(t * P + (P + 2))
                    count, keys_before = fixed(t + 2), fixed(t + 3)
                    ahead = not isinstance(t, int) or t + 2 < TILES
                    r, above, below = (fixed(t * P + (2 * P + x)) for x in (2, 1, 3)) if ahead else (0, 0, 0)
                    if not isinstance(t, int) or t < TILES - 1:
                        sp.wait_ge(turn_done, keys_before)
                        load_keys("sample", key_row)
                    sp.wait_ge(gates_ready, count)
                    sp.dma_start(T["gates"][bass.ds(row, P), :], gates[:, s, :]).then_inc(stored[s], 16)
                    sp.dma_start(T["gla_la"][bass.ds(row, P), :], la[:, s, :]).then_inc(stored[s], 16)
                    if ahead:
                        load(s, r, above, below)
                    sp.wait_ge(ready, count)
                    sp.dma_start(T["qkv"][bass.ds(row, P), :], y[:, s, :]).then_inc(stored[s], 16)

                with sp.Fori(0, (TILES - 1) // 2 - 1) as i:
                    for s in range(2):
                        tile(i * 2 + s, s)
                for t in range(TILES - 3, TILES):
                    tile(t, t % 2)
                for s in range(2):
                    sp.wait_ge(stored[s], 48 * ((TILES + 1 - s) // 2) + 1)

            @block.tensor
            def _(pe):
                pe.wait_ge(w_in, 81)
                pe.wait_ge(kw_in, 33)

                def start(t, s, i):
                    pe.wait_ge(t_in[s], i * 80 + 81)
                    for d in range(2):
                        mm = pe.transpose(ptr[0:RANK, d, :], lr[:, s, d, :], B.ident)
                    mm.then_inc(lr_turned, 1)
                    pe.wait_ge(lrT_done, t + 2)
                    for d in range(2):
                        mm = pe.matmul(pl[:, d * GQ:(d + 1) * GQ], lrT[:, d, :], wg[:, d, :], start=True, stop=True)
                    mm.then_inc(pl_done, 1)

                def key_part(k, kind, part):
                    pe.wait_ge(to_pe, k * 3 + (part + 2))
                    if part == 0:
                        pe.transpose(tr[:, 0:P], ckv[:], B.ident).then_inc(from_pe, 1)
                    if part == 1:
                        pe.matmul(kv[:], ckvT[:], wkv[:], start=True, stop=True).then_inc(from_pe, 1)
                    if part == 2:
                        for h in range(H_MLA):
                            mm = pe.transpose(trk[:, h, :], ka[:, h, :], B.ident)
                        mm.then_inc(from_pe, 1)
                def keys(k, kind):
                    for part in range(3):
                        key_part(k, kind, part)

                def tile(t, s, i):
                    if more(t):
                        start(t + 1, 1 - s, i + s)
                        keys(t + 2, "sample")
                turns(pe, keys, start, tile, lambda: None)

            @block.gpsimd
            def _(pool):
                own, step = psem, Steps()
                pool.wait_ge(w_in, 81)

                def start(t, s, i):
                    pool.wait_ge(t_in[s], i * 80 + 81)
                    pool.tensor_tensor(taps[:, s, 0, :], taps[:, s, 0, :], wc[:, 0, :], ALU.mult).then_inc(own, step())
                    pool.tensor_tensor(taps[:, s, 2, :], taps[:, s, 2, :], wc[:, 2, :], ALU.mult).then_inc(own, step())
                    pool.wait_ge(own, step.n)
                    pool.wait_ge(conv_done, t + 1)
                    pool.tensor_tensor(tmp[:, s], taps[:, s, 0, :], taps[:, s, 2, :], ALU.add).then_inc(mixed, 1)

                def tile(t, s, i):
                    if more(t):
                        start(t + 1, 1 - s, i + s)

                def settle():
                    pool.sem_clear(own)
                    step.restart()
                turns(pool, lambda k, kind: None, start, tile, settle)

            @block.scalar
            def _(act):
                own, step = asem, Steps()
                act.wait_ge(w_in, 81)
                act.activation(alog[:], alog[:], ACT.Exp).then_inc(own, step())

                def start(t, s, i):
                    act.wait_ge(a_done, t + 2)
                    act.activation(eb[:, 0, :], ba[:, s, 0:GB], ACT.Exp, scale=-1.0).then_inc(own, step())
                    act.activation(eb[:, 1, :], ab[:], ACT.Exp, scale=-1.0).then_inc(own, step())
                    act.wait_ge(logit_done, t + 2)
                    act.activation(absl[:], absl[:], ACT.Exp, scale=-1.0).then_inc(own, step())
                    act.wait_ge(conv_done, t + 2)
                    act.activation(y[:, s], y[:, s], ACT.Silu).then_inc(own, step())
                    act.wait_ge(own, step.n)
                    act.activation(sq[:], y[:, s, 0:2 * DQ], ACT.Square).then_inc(sq_done, 1)

                def key_square(k):
                    act.wait_ge(k_in, k * 32 + 33)
                    act.wait_ge(turn_done, k + 1)
                    act.activation(ksq[:], kin[:, 0:KVL], ACT.Square, accum_out=rs[:]).then_inc(own, step())
                    act.wait_ge(own, step.n)

                def keys(k, kind):
                    key_square(k)
                    act.activation(rs[:], rs[:], ACT.Ln, bias=B.eps[:, 0:1], scale=1.0 / KVL).then_inc(own, step())
                    act.wait_ge(own, step.n)
                    act.activation(rs[:], rs[:], ACT.Exp, scale=-0.5).then_inc(krs_done, 1)

                def tile(t, s, i):
                    act.activation(eb[:, 1, :], eb[:, 1, :], ACT.Ln, bias=B.ones[:, 0:1]).then_inc(ln_done, 1)
                    act.activation(absl[:], absl[:], ACT.Ln, bias=B.ones[:, 0:1]).then_inc(lnl_done, 1)
                    if more(t):
                        key_square(t + 2)
                        act.activation(rs[:], rs[:], ACT.Ln, bias=B.eps[:, 0:1], scale=1.0 / KVL).then_inc(own, step())
                    act.wait_ge(ss_done, t + 2)
                    act.activation(ss[:], ss[:], ACT.Ln, bias=B.eps[:, 0:1]).then_inc(own, step())
                    act.wait_ge(own, step.n)
                    if more(t):
                        act.activation(rs[:], rs[:], ACT.Exp, scale=-0.5).then_inc(krs_done, 1)
                    act.activation(ss[:], ss[:], ACT.Exp, scale=-0.5).then_inc(rs_done, 1)
                    if more(t):
                        start(t + 1, 1 - s, i + s)

                def settle():
                    act.wait_ge(own, step.n)
                    act.sem_clear(own)
                    step.restart()
                turns(act, keys, start, tile, settle)

            @block.vector
            def _(dve):
                own, step = dsem, Steps()
                dve.memset(ka[:], 0.0).then_inc(own, step())
                dve.wait_ge(own, step.n)
                dve.wait_ge(w_in, 81)
                dve.wait_ge(kw_in, 33)

                def gate_logits(t, s, i):
                    dve.wait_ge(t_in[s], i * 80 + 81)
                    x = ba[:, s, GB:]
                    dve.tensor_tensor(x, x, dt[:], ALU.add).then_inc(own, step())
                    dve.wait_ge(own, step.n)
                    dve.scalar_tensor_tensor(ab[:], x, -1.0, x, ALU.mult, ALU.max).then_inc(a_done, 1)
                    dve.wait_ge(lr_turned, t + 2)
                    dve.tensor_copy(lrT[:], ptr[0:RANK, :, :]).then_inc(lrT_done, 1)
                    dve.tensor_tensor(y[:, s], taps[:, s, 1, :], wc[:, 1, :], ALU.mult).then_inc(own, step())
                    dve.wait_ge(pl_done, t + 2)
                    dve.tensor_tensor(logit[:], pl[:], bg[:], ALU.add).then_inc(own, step())
                    dve.wait_ge(own, step.n)
                    dve.scalar_tensor_tensor(absl[:], logit[:], -1.0, logit[:], ALU.mult, ALU.max).then_inc(logit_done, 1)
                    dve.wait_ge(mixed, t + 2)
                    dve.tensor_tensor(y[:, s], y[:, s], tmp[:, s], ALU.add).then_inc(conv_done, 1)

                def gate_values(t, s):
                    dve.wait_ge(ln_done, t + 2)
                    x = ba[:, s, GB:]
                    dve.scalar_tensor_tensor(eb[:, 1, :], x, 0.0, eb[:, 1, :], ALU.max, ALU.add).then_inc(own, step())
                    dve.tensor_scalar(eb[:, 0, :], eb[:, 0, :], 1.0, None, ALU.add).then_inc(own, step())
                    dve.wait_ge(own, step.n)
                    dve.scalar_tensor_tensor(gates[:, s, GB:], eb[:, 1, :], -1.0, alog[:], ALU.mult, ALU.mult).then_inc(own, step())
                    dve.reciprocal(gates[:, s, 0:GB], eb[:, 0, :]).then_inc(own, step())
                    dve.wait_ge(lnl_done, t + 2)
                    dve.scalar_tensor_tensor(la[:, s], logit[:], 0.0, absl[:], ALU.min, ALU.subtract).then_inc(own, step())
                    dve.wait_ge(own, step.n)
                    dve.tensor_scalar(la[:, s], la[:, s], 1.0 / TAU, None, ALU.mult).then_inc(gates_ready, 1)

                def head_norms(t, s):
                    dve.wait_ge(rs_done, t + 2)
                    dve.tensor_scalar(ss[:, 0:H_GDN], ss[:, 0:H_GDN], float(GK) ** -0.5, None, ALU.mult).then_inc(own, step())
                    dve.wait_ge(own, step.n)
                    qk = y[:, s, 0:2 * DQ].rearrange("p (h e) -> p h e", e=GK)
                    dve.tensor_tensor(qk, qk, ss[:].unsqueeze(2).to_broadcast([P, 2 * H_GDN, GK]), ALU.mult).then_inc(own, step())
                    dve.wait_ge(own, step.n)
                    dve.sem_inc(ready, 1)

                def start(t, s, i):
                    dve.wait_ge(stored[s], i * 48 + 1)
                    gate_logits(t, s, i)

                def key_part(k, kind, part):
                    if part == 0:
                        dve.wait_ge(krs_done, k + 2)
                        if kind == "context":
                            dve.wait_ge(kstored, 33)
                            dve.tensor_copy(ckv[:], kin[:, 0:KVL]).then_inc(to_pe, 1)
                        else:
                            dve.scalar_tensor_tensor(ckv[:], kin[:, 0:KVL], rs[:, 0:1], gain[:], ALU.mult, ALU.mult).then_inc(to_pe, 1)
                        raw = kin[:, KVL:]
                        if kind == "sample":
                            rotate(own, step, dve, kr[:], raw, B.rope[:, k - 1, 0, :], B.rope[:, k - 1, 1, :], [ktmp[:, j, :] for j in range(4)])
                            dve.wait_ge(own, step.n)
                            dve.tensor_copy(ka[:, :, NOPE:QD], kr[:].unsqueeze(1).to_broadcast([P, H_MLA, ROPE])).then_inc(own, step())
                            dve.memset(ka[:, :, QD:P], 0.0).then_inc(own, step())
                        else:
                            dve.tensor_copy(ka[:, :, QD:P], raw.unsqueeze(1).to_broadcast([P, H_MLA, ROPE])).then_inc(own, step())
                        dve.wait_ge(from_pe, k * 3 + 2)
                        dve.tensor_copy(ckvT[:], tr[:, 0:P]).then_inc(to_pe, 1)
                    if part == 1:
                        dve.wait_ge(from_pe, k * 3 + 3)
                        kvh = kv[:].rearrange("p (h e) -> p h e", h=H_MLA)
                        dve.tensor_copy(ka[:, :, 0:NOPE], kvh[:, :, 0:NOPE]).then_inc(own, step())
                        dve.tensor_copy(values[:, k, :, :], kvh[:, :, NOPE:]).then_inc(own, step())
                        dve.wait_ge(own, step.n)
                        dve.sem_inc(to_pe, 1)
                    if part == 2:
                        dve.wait_ge(from_pe, k * 3 + 4)
                        dve.tensor_copy(keysT[:, :, bass.ds(k * P, P)], trk[:]).then_inc(turn_done, 1)

                def settle():
                    dve.wait_ge(own, step.n)
                    dve.sem_clear(own)
                    step.restart()
                def keys(k, kind):
                    for part in range(3):
                        key_part(k, kind, part)

                def tile(t, s, i):
                    dve.wait_ge(sq_done, t + 2)
                    dve.tensor_reduce(ss[:], sq[:].rearrange("p (h e) -> p h e", e=GK), AX.X, ALU.add).then_inc(ss_done, 1)
                    gate_values(t, s)
                    if more(t):
                        start(t + 1, 1 - s, i + s)
                        key_part(t + 2, "sample", 0)
                    head_norms(t, s)
                    if more(t):
                        key_part(t + 2, "sample", 1)
                        key_part(t + 2, "sample", 2)
                turns(dve, keys, start, tile, settle)


LEVELS = 7
PE_N, DVE_N, ACT_N, POOL_N = 11, 8, 8, 1 + LEVELS
TAIL, SLOTS = 3, 2 * LEVELS


def scan(nc, T, B, l, prompt):
    N = 1 if prompt else TILES - 1
    H, G = H_GDN, H_GLA
    with stage(nc, "scanp" if prompt else "scans") as st:
        both = lambda name, shape: [st.sb(f"{name}{d}", shape) for d in range(2)]
        qkv, gla, gla_la, gate = both("qkv", [P, 3, H, GK]), both("gla", [P, 3, G, GK]), both("gla_la", [P, GQ]), both("gate", [P, 16])
        decay = both("decay", [P, H, P])
        S, ST = both("S", [P, H, P]), [both("Sa", [P, H, P]), both("Sb", [P, H, P])]
        A, Ti, TT, Y = both("A", [P, H, P]), both("Ti", [P, H, P]), both("TT", [P, H, P]), both("Y", [P, H, P])
        kT, qT = both("kT", [GK, H, P]), both("qT", [GK, H, P])
        nwT = kT
        Rk, Rv, kend, VN = both("Rk", [P, H, GK]), both("Rv", [P, H, GK]), both("kend", [P, H, GK]), both("VN", [P, H, GK])
        s_d, s_g, s_m = both("s_d", [GK, H, GK]), both("s_g", [GK, G, GK]), both("s_m", [GK, G, GK])
        gg, eg = both("gg", [P, 3, H]), both("eg", [P, 3, H])
        mid, emid = both("mid", [GK, G, 3]), both("emid", [GK, G, 3])
        E, Ei = both("E", [P, G, GK]), both("Ei", [P, G, GK])
        gkv = both("gkv", [GK, G, GK])
        out = both("out", [P, 768])
        gT = [TT[d][0:GK] for d in range(2)]
        gA = both("gA", [P, G, P])
        qd, ki = E, Ei
        pX, pY = [st.ps(f"pX{d}", [P, H, P]) for d in range(2)], [st.ps(f"pY{d}", [P, H, P]) for d in range(2)]
        fpe, fdve, fact, fpool = ([st.sem(f"{x}_done{d}") for d in range(2)] for x in ("pe", "dve", "act", "pool"))
        gla_in, gdn_in, stored, s_in = ([st.sem(f"{x}{d}") for d in range(2)] for x in ("gla_in", "gdn_in", "stored", "state_in"))
        z_made, y_made, u_made, t_made = ([[st.sem(f"{x}{d}{g}") for g in range(2)] for d in range(2)] for x in ("z", "y", "u", "t"))
        asem, dsem, passed = st.sem("act_steps"), st.sem("dve_steps"), st.sem("passed")
        cum = [B.masks[:, 1, :], B.masks[:, 2, :]]
        anchored = [B.masks[:, 3, :], B.masks[:, 4, :]]
        mid_col = [B.midcols[:, 0:2], B.midcols[:, 2:4]]
        kd, qdl, vd = [qkv[d][:, 1] for d in range(2)], [qkv[d][:, 0] for d in range(2)], [qkv[d][:, 2] for d in range(2)]

        def heads(ap, n, w):
            return ap.unsqueeze(2).to_broadcast([ap.shape[0], n, w])

        def over(ap, n):
            return ap.unsqueeze(1).to_broadcast([ap.shape[0], n, ap.shape[1]])

        bank = lambda p, b: p[:].rearrange("p (b h) c -> p b (h c)", b=2)[:, b, :].rearrange("p (h e) -> p h e", e=GK)

        half = [slice(0, H // 2), slice(H // 2, H)]

        def chunks(eng, levels, others, settle):
            if prompt:
                for part, slots in ((others, range(TAIL, SLOTS)), (levels, range(SLOTS)), (others, range(TAIL))):
                    for slot in slots:
                        for d in range(2):
                            part(d, 0, slot)
                settle()
                return

            def side(d, t, tail, head):
                for slot in range(SLOTS):
                    levels(d, t, slot)
                    other = tail if slot < TAIL else head
                    if other is not None:
                        others(1 - d, other, slot)

            for slot in range(TAIL, SLOTS):
                others(0, 0, slot)
            side(0, 0, None, 0)
            side(1, 0, 0, 1)
            settle()
            with eng.Fori(1, N - 1) as t:
                side(0, t, t - 1, t)
                side(1, t, t, t + 1)
                settle()
            side(0, N - 1, N - 2, N - 1)
            side(1, N - 1, N - 1, None)
            for slot in range(TAIL):
                others(1, N - 1, slot)
            settle()

        with st.block() as block:
            @block.sync
            def _(sp):
                if not prompt:
                    for d in range(2):
                        sp.dma_start(s_d[d][:], T["state_gdn"][0, l, d].rearrange("h k v -> k h v")).then_inc(s_in[d], 16)
                        sp.dma_start(s_g[d][:], T["state_gla"][0, l, d].rearrange("h k v -> k h v")).then_inc(s_in[d], 16)

                def rows(d, t):
                    if prompt:
                        return 0, 1
                    if isinstance(t, int):
                        at = (N - t if d else t + 1) * P
                        return at, at + 2
                    return ((sp.snap(t * -P + N * P), sp.snap(t * -P + (N * P + 2))) if d else
                            (sp.snap(t * P + P), sp.snap(t * P + (P + 2))))

                def load_gla(d, at):
                    R, Q = bass.ds(at[0], P), bass.ds(at[1], P)
                    for dst, src in ((gla_la[d][:], T["gla_la"][R, d * GQ:(d + 1) * GQ]),
                                     (gla[d][:].rearrange("p a h e -> p (a h e)"), T["proj"][Q, C_GQ:C_GLR])):
                        sp.dma_start(dst, src).then_inc(gla_in[d], 16)

                def load_gdn(d, at):
                    R = bass.ds(at[0], P)
                    for dst, src in ((qkv[d][:].rearrange("p a h e -> p (a h e)"), T["qkv"][R, :]),
                                     (gate[d][:, 0:H], T["gates"][R, d * H:(d + 1) * H]),
                                     (gate[d][:, H:], T["gates"][R, 2 * H + d * H:2 * H + (d + 1) * H])):
                        sp.dma_start(dst, src).then_inc(gdn_in[d], 16)

                def store(d, at):
                    sp.dma_start(T["scan_b" if d else "scan_f"][bass.ds(at[0], P), :], out[d][:]).then_inc(stored[d], 16)

                for d in range(2):
                    load_gla(d, rows(d, 0))
                    load_gdn(d, rows(d, 0))
                if prompt:
                    for d in range(2):
                        sp.wait_ge(fdve[d], DVE_N + 1)
                        store(d, (0, 1))
                        sp.dma_start(T["new_gdn"][0, l, d].rearrange("h k v -> k h v"), s_d[d][:]).then_inc(stored[d], 16)
                        sp.dma_start(T["new_gla"][0, l, d].rearrange("h k v -> k h v"), s_g[d][:]).then_inc(stored[d], 16)
                        sp.wait_ge(stored[d], 49)
                else:
                    for d in range(2):
                        sp.wait_ge(fdve[d], 5)
                        load_gla(d, rows(d, 1))

                    def body(t, last):
                        now = [rows(d, t) for d in range(2)]
                        after = [None if last else rows(d, t + 1) for d in range(2)]
                        second = [None if last or isinstance(t, int) and t + 2 >= N else rows(d, t + 2) for d in range(2)]
                        for d in range(2):
                            sp.wait_ge(fdve[d], t * DVE_N + DVE_N + 1)
                            store(d, now[d])
                            if after[d]:
                                load_gdn(d, after[d])
                            if second[d]:
                                sp.wait_ge(fdve[d], t * DVE_N + DVE_N + 5)
                                load_gla(d, second[d])
                    with sp.Fori(0, N - 2) as t:
                        body(t, False)
                    body(N - 2, False)
                    body(N - 1, True)
                    for d in range(2):
                        sp.wait_ge(stored[d], 16 * N + 1)

            @block.tensor
            def _(pe):
                def levels(d, t, slot):
                    v = slot // 2
                    for g in range(2):
                        if slot % 2 == 0:
                            if v == 0:
                                pe.wait_ge(fdve[d], t * DVE_N + 7)
                            else:
                                pe.wait_ge(t_made[d][g], t * LEVELS + v + 1)
                            pe.wait_ge(fpool[d], t * POOL_N + (1 + v) + 1)
                            for h in range(H)[half[g]]:
                                mm = pe.matmul(pX[d][:, h, :], ST[v % 2][d][:, h, :], Ti[d][:, h, :] if v else B.ident, start=True, stop=True)
                            mm.then_inc(z_made[d][g], 1)
                        else:
                            pe.wait_ge(y_made[d][g], t * LEVELS + v + 2)
                            for h in range(H)[half[g]]:
                                if 0 < v < LEVELS - 1:
                                    pe.matmul(pY[d][:, h, :], TT[d][:, h, :], Y[d][:, h, :], start=True, stop=True)
                                mm = pe.matmul(pX[d][:, h, :], Y[d][:, h, :], TT[d][:, h, :] if v else B.ident, start=True, stop=True)
                            mm.then_inc(u_made[d][g], 1)

                def others(d, t, slot):
                    if slot == 3:
                        pe.wait_ge(gla_in[d], t * 32 + 33)
                        pe.wait_ge(fdve[d], t * DVE_N + 1)
                        pe.matmul(pY[d][:, 0:2, :], anchored[d], gla_la[d][:], start=True, stop=True)
                        for h in range(G):
                            mm = pe.matmul(pX[d][0:GK, 0, 2 * h:2 * h + 2], gla_la[d][:, h * GK:(h + 1) * GK], mid_col[d], start=True, stop=True)
                        mm.then_inc(fpe[d], 1)
                    if slot == 5:
                        pe.wait_ge(fdve[d], t * DVE_N + 3)
                        pe.sem_inc(passed, 1)
                        for h in range(G):
                            pe.transpose(pX[d][0:GK, h, :], qd[d][:, h, :], B.ident)
                            mm = pe.transpose(pX[d][0:GK, G + h, :], ki[d][:, h, :], B.ident)
                        mm.then_inc(fpe[d], 1)
                    if slot == 6:
                        pe.wait_ge(fact[d], t * ACT_N + 4)
                        for h in range(G):
                            mm = pe.matmul(pY[d][:, h, :], gT[d][:, G + h, :], gT[d][:, h, :], start=True, stop=True)
                        mm.then_inc(fpe[d], 1)
                    if slot == 7:
                        pe.wait_ge(fdve[d], t * DVE_N + 4)
                        for h in range(G):
                            pe.matmul(bank(pX[d], 0)[:, h, :], gA[d][:, h, :], gla[d][:, 2, h, :], start=True, stop=False)
                            pe.matmul(bank(pX[d], 0)[:, h, :], gT[d][:, h, :], s_m[d][:, h, :], start=False, stop=True)
                        for h in range(G):
                            mm = pe.matmul(bank(pX[d], 1)[0:GK, h, :], ki[d][:, h, :], gla[d][:, 2, h, :], start=True, stop=True)
                        mm.then_inc(fpe[d], 1)
                    if slot == 8:
                        pe.wait_ge(gdn_in[d], t * 48 + 49)
                        pe.wait_ge(fdve[d], t * DVE_N + 5)
                        la = gate[d][:, H:]
                        pe.matmul(pY[d][:, 0, 0:H], cum[d], la, start=True, stop=True)
                        pe.matmul(pY[d][:, 0, H:2 * H], B.ones[:], la, start=True, stop=True)
                        for h in range(H):
                            mm = pe.matmul(pX[d][:, h, :], la[:, h:h + 1].to_broadcast([P, P]), cum[d], start=True, stop=True)
                        mm.then_inc(fpe[d], 1)
                    if slot == 9:
                        pe.wait_ge(fdve[d], t * DVE_N + 6)
                        pe.sem_inc(passed, 1)
                        for h in range(H):
                            mm = pe.transpose(pY[d][0:GK, h, :], kd[d][:, h, :], B.ident)
                        mm.then_inc(fpe[d], 1)
                        for h in range(H):
                            mm = pe.transpose(pX[d][0:GK, h, :], qdl[d][:, h, :], B.ident)
                        mm.then_inc(fpe[d], 1)
                    if slot == 10:
                        pe.wait_ge(fact[d], t * ACT_N + 8)
                        for h in range(H):
                            pe.matmul(pX[d][:, h, :], kT[d][:, h, :], kT[d][:, h, :], start=True, stop=True)
                            mm = pe.matmul(pY[d][:, h, :], kT[d][:, h, :], qT[d][:, h, :], start=True, stop=True)
                        mm.then_inc(fpe[d], 1)
                    if slot == 0:
                        for g in range(2):
                            pe.wait_ge(t_made[d][g], t * LEVELS + LEVELS + 1)
                        pe.wait_ge(fpool[d], t * POOL_N + POOL_N + 1)
                        for h in range(H):
                            mm = pe.matmul(pX[d][0:GK, h, :], Rk[d][:, h, :], TT[d][:, h, :], start=True, stop=True)
                        mm.then_inc(fpe[d], 1)
                    if slot == 1:
                        pe.wait_ge(fact[d], t * ACT_N + 9)
                        for h in range(H):
                            pe.matmul(bank(pY[d], 0)[:, h, :], TT[d][:, h, :], Rv[d][:, h, :], start=True, stop=False)
                            mm = pe.matmul(bank(pY[d], 0)[:, h, :], nwT[d][:, h, :], s_d[d][:, h, :], start=False, stop=True)
                        mm.then_inc(fpe[d], 1)
                    if slot == 2:
                        pe.wait_ge(fdve[d], t * DVE_N + 8)
                        for h in range(H):
                            pe.matmul(bank(pX[d], 0)[:, h, :], qT[d][:, h, :], s_d[d][:, h, :], start=True, stop=True)
                            pe.matmul(bank(pX[d], 1)[:, h, :], A[d][:, h, :], VN[d][:, h, :], start=True, stop=True)
                            mm = pe.matmul(bank(pY[d], 1)[0:GK, h, :], kend[d][:, h, :], VN[d][:, h, :], start=True, stop=True)
                        mm.then_inc(fpe[d], 1)
                chunks(pe, levels, others, lambda: None)

            @block.scalar
            def _(act):
                own, step = asem, Steps()

                def levels(d, t, slot):
                    pass

                def others(d, t, slot):
                    if slot == 3:
                        act.wait_ge(fpe[d], t * PE_N + 2)
                        y = pY[d][:, 0:2, :].rearrange("p a c -> p (a c)")
                        act.activation(E[d][:].rearrange("p h e -> p (h e)"), y, ACT.Exp).then_inc(own, step())
                        act.activation(Ei[d][:].rearrange("p h e -> p (h e)"), y, ACT.Exp, scale=-1.0).then_inc(fact[d], 1)
                        act.wait_ge(fdve[d], t * DVE_N + 2)
                        act.activation(emid[d][:], mid[d][:], ACT.Exp).then_inc(fact[d], 1)
                    if slot == 5:
                        act.wait_ge(fpe[d], t * PE_N + 3)
                        act.activation(gT[d], pX[d][0:GK], ACT.Copy).then_inc(fact[d], 1)
                    if slot == 9:
                        act.wait_ge(fdve[d], t * DVE_N + 6)
                        act.activation(eg[d][:], gg[d][:], ACT.Exp).then_inc(fact[d], 1)
                        act.activation(decay[d][:], decay[d][:], ACT.Exp).then_inc(fact[d], 1)
                        act.wait_ge(fpe[d], t * PE_N + 7)
                        act.activation(kT[d][:], pY[d][0:GK], ACT.Copy).then_inc(fact[d], 1)
                        act.wait_ge(fpe[d], t * PE_N + 8)
                        act.activation(qT[d][:], pX[d][0:GK], ACT.Copy).then_inc(fact[d], 1)
                    if slot == 0:
                        act.wait_ge(fpe[d], t * PE_N + 10)
                        act.activation(nwT[d][:], pX[d][0:GK], ACT.Copy, scale=-1.0).then_inc(fact[d], 1)

                def settle():
                    act.wait_ge(own, step.n)
                    act.sem_clear(own)
                    step.restart()
                chunks(act, levels, others, settle)

            @block.gpsimd
            def _(pool):
                def levels(d, t, slot):
                    if slot % 2 and slot < 10:
                        v = slot // 2 + 2
                        for g in range(2):
                            pool.wait_ge(z_made[d][g], t * LEVELS + v)
                        pool.tensor_tensor(ST[v % 2][d][:], S[d][:], over(B.masks[:, 5 + 7 * d + v, :], H), ALU.mult).then_inc(fpool[d], 1)
                    if slot == 11:
                        pool.tensor_tensor(A[d][:], A[d][:], over(cum[d], H), ALU.mult)
                        pool.tensor_tensor(kend[d][:], kd[d], heads(eg[d][:, 2, :], H, GK), ALU.mult)
                        pool.tensor_tensor(Rv[d][:], vd[d], heads(gate[d][:, 0:H], H, GK), ALU.mult)
                        pool.tensor_tensor(Rk[d][:], kd[d], heads(gg[d][:, 1, :], H, GK), ALU.mult).then_inc(fpool[d], 1)

                def others(d, t, slot):
                    if slot == 11:
                        pool.wait_ge(fdve[d], t * DVE_N + 7)
                        for v in range(2):
                            pool.tensor_tensor(ST[v][d][:], S[d][:], over(B.masks[:, 5 + 7 * d + v, :], H), ALU.mult).then_inc(fpool[d], 1)
                chunks(pool, levels, others, lambda: None)

            @block.vector
            def _(dve):
                own, step = dsem, Steps()
                for d in range(2):
                    dve.memset(gA[d][:], 0.0).then_inc(own, step())
                    if prompt:
                        dve.memset(s_d[d][:], 0.0).then_inc(own, step())
                        dve.memset(s_g[d][:], 0.0).then_inc(own, step())
                    else:
                        dve.wait_ge(s_in[d], 33)
                dve.wait_ge(own, step.n)
                dve.sem_clear(own)
                step.restart()

                def levels(d, t, slot):
                    v = slot // 2
                    for g in range(2):
                        hs = half[g]
                        if slot % 2 == 0:
                            dve.wait_ge(z_made[d][g], t * LEVELS + v + 2)
                            dve.tensor_tensor(Y[d][:, hs], pX[d][:, hs], heads(gate[d][:, hs], H // 2, P), ALU.mult).then_inc(y_made[d][g], 1)
                        else:
                            dve.wait_ge(u_made[d][g], t * LEVELS + v + 2)
                            if v == 0:
                                dve.tensor_tensor(Ti[d][:, hs], over(B.ident, H // 2), Y[d][:, hs], ALU.subtract)
                                dve.tensor_tensor(TT[d][:, hs], over(B.ident, H // 2), pX[d][:, hs], ALU.subtract).then_inc(t_made[d][g], 1)
                            else:
                                if v < LEVELS - 1:
                                    dve.tensor_tensor(Ti[d][:, hs], Ti[d][:, hs], pY[d][:, hs], ALU.subtract)
                                dve.tensor_tensor(TT[d][:, hs], TT[d][:, hs], pX[d][:, hs], ALU.subtract).then_inc(t_made[d][g], 1)

                def others(d, t, slot):
                    if slot == 3:
                        dve.wait_ge(fpe[d], t * PE_N + 2)
                        mg = pX[d][0:GK, 0, 0:2 * G].rearrange("p (h a) -> p h a", a=2)
                        dve.tensor_copy(mid[d][:, :, 0:2], mg).then_inc(own, step())
                        dve.wait_ge(own, step.n)
                        dve.tensor_tensor(mid[d][:, :, 2], mid[d][:, :, 1], mid[d][:, :, 0], ALU.subtract).then_inc(fdve[d], 1)
                    if slot == 4:
                        dve.wait_ge(fact[d], t * ACT_N + 2)
                        dve.scalar_tensor_tensor(qd[d][:], gla[d][:, 0], float(GK) ** -0.5, E[d][:], ALU.mult, ALU.mult).then_inc(own, step())
                        dve.tensor_tensor(ki[d][:], gla[d][:, 1], Ei[d][:], ALU.mult).then_inc(fdve[d], 1)
                    if slot == 6:
                        dve.wait_ge(fact[d], t * ACT_N + 3)
                        dve.wait_ge(fpe[d], t * PE_N + 4)
                        dve.tensor_tensor(s_m[d][:], s_g[d][:], heads(emid[d][:, :, 0], G, GK), ALU.mult).then_inc(own, step())
                        dve.copy_predicated(gA[d][:], over(cum[d], G).bitcast(U32), pY[d][:, 0:G, :]).then_inc(fdve[d], 1)
                    if slot == 7:
                        dve.wait_ge(fpe[d], t * PE_N + 5)
                        dve.wait_ge(stored[d], t * 16 + 1)
                        dve.tensor_copy(out[d][:, 0:GQ].rearrange("p (h e) -> p h e", e=GK), bank(pX[d], 0)[:, 0:G, :]).then_inc(own, step())
                        dve.tensor_tensor(gkv[d][:], bank(pX[d], 1)[0:GK, 0:G, :], heads(emid[d][:, :, 2], G, GK), ALU.mult).then_inc(own, step())
                        dve.tensor_tensor(s_g[d][:], s_g[d][:], heads(emid[d][:, :, 1], G, GK), ALU.mult).then_inc(own, step())
                        dve.wait_ge(own, step.n)
                        dve.tensor_tensor(s_g[d][:], s_g[d][:], gkv[d][:], ALU.add).then_inc(fdve[d], 1)
                    if slot == 8:
                        dve.wait_ge(fpe[d], t * PE_N + 6)
                        dve.tensor_copy(gg[d][:, 0:2, :], pY[d][:, 0, 0:2 * H].rearrange("p (a h) -> p a h", h=H)).then_inc(own, step())
                        dve.wait_ge(own, step.n)
                        dve.tensor_tensor(gg[d][:, 2, :], gg[d][:, 1, :], gg[d][:, 0, :], ALU.subtract).then_inc(own, step())
                        for h in range(H):
                            dve.tensor_scalar(decay[d][:, h, :], pX[d][:, h, :], gg[d][:, 0, h:h + 1], 0.0, ALU.subtract, ALU.min).then_inc(own, step())
                        dve.wait_ge(own, step.n)
                        dve.sem_inc(fdve[d], 1)
                    if slot == 10:
                        dve.wait_ge(fact[d], t * ACT_N + 5)
                        dve.tensor_tensor(gg[d][:, 1, :], eg[d][:, 0, :], gate[d][:, 0:H], ALU.mult).then_inc(own, step())
                        dve.wait_ge(own, step.n)
                    if slot == 10:
                        dve.wait_ge(fpe[d], t * PE_N + 9)
                        dve.tensor_tensor(S[d][:], pX[d][:], decay[d][:], ALU.mult).then_inc(own, step())
                        dve.tensor_tensor(A[d][:], pY[d][:], decay[d][:], ALU.mult).then_inc(own, step())
                        dve.wait_ge(own, step.n)
                        dve.sem_inc(fdve[d], 1)
                    if slot == 1:
                        dve.wait_ge(fpe[d], t * PE_N + 11)
                        dve.tensor_copy(VN[d][:], bank(pY[d], 0)).then_inc(fdve[d], 1)
                    if slot == 2:
                        dve.wait_ge(fpe[d], t * PE_N + 12)
                        o = out[d][:, GQ:].rearrange("p (h e) -> p h e", e=GK)
                        dve.tensor_tensor(o, bank(pX[d], 0), heads(eg[d][:, 0, :], H, GK), ALU.mult).then_inc(own, step())
                        dve.tensor_tensor(s_d[d][:], s_d[d][:], heads(eg[d][0:GK, 1, :], H, GK), ALU.mult).then_inc(own, step())
                        dve.wait_ge(own, step.n)
                        dve.tensor_tensor(o, o, bank(pX[d], 1), ALU.add).then_inc(own, step())
                        dve.tensor_tensor(s_d[d][:], s_d[d][:], bank(pY[d], 1)[0:GK], ALU.add).then_inc(own, step())
                        dve.wait_ge(own, step.n)
                        dve.sem_inc(fdve[d], 1)

                def settle():
                    dve.wait_ge(own, step.n)
                    dve.sem_clear(own)
                    step.restart()
                chunks(dve, levels, others, settle)


def mixer_output(nc, T, B, l):
    W3 = 768
    NH = W3 // GK
    with stage(nc, "mixer") as st:
        wout = st.sb("wout", [P, KD, D])
        wr = st.sb("wr", [P, KD, E_N])
        gain = st.sb("gain", [P, 2, GK])
        o = st.sb("o", [P, D])
        ob, z = st.sb("ob", [P, W3]), st.sb("z", [P, W3])
        ss = st.sb("ss", [P, NH])
        rs = st.sb("rs", [P, 2])
        oT = st.sb("oT", [P, KD, P])
        sq = st.sb("sq", [P, D])
        branch = st.sb("branch", [P, D])
        xhat = st.sb("xhat", [P, 2, D])
        xT = st.sb("xT", [P, KD, P])
        mx, den = st.sb("mx", [P, 1]), st.sb("den", [P, 1])
        ex = st.sb("ex", [P, E_N])
        af = st.sb("af", [P, E_N + 2])
        affT = st.sb("affT", [E_N + 2, ROWS])
        tr, acc, xtr = st.ps("tr", [P, KD, P]), st.ps("acc", [P, D]), st.ps("xtr", [P, KD, P])
        lg, at = st.ps("lg", [P, 512]), st.ps("at", [P, 512])
        w_in, t_in, zsilu_done, ss_done, rs_done, o_done, o_turned, oT_done, y_prod = (st.sem(x) for x in (
            "w_in", "t_in", "zsilu_done", "ss_done", "rs_done", "o_done", "o_turned", "oT_done", "y_prod"))
        yrs_done, branch_done, x_done, xrs_done, xhat_done, x_turned, xT_done, logits = (st.sem(x) for x in (
            "yrs_done", "branch_done", "x_done", "xrs_done", "xhat_done", "x_turned", "xT_done", "logits"))
        max_done, exp_done, aff_done, aff_turned, affT_done, all_stored = (st.sem(x) for x in (
            "max_done", "exp_done", "aff_done", "aff_turned", "affT_done", "all_stored"))
        stored = [st.sem("stored0"), st.sem("stored1")]
        asem, dsem = st.sem("act_steps"), st.sem("dve_steps")

        def turns(eng, body):
            body(0, 0)
            body(1, 1)
            with eng.Fori(1, (TILES - 3) // 2) as i:
                for s in range(2):
                    body(i * 2 + s, s)
            for t in range(TILES - 3, TILES + 2):
                body(t, t % 2)

        def has(t, n=0):
            return not isinstance(t, int) or 0 <= t + n < TILES

        with st.block() as block:
            @block.sync
            def _(sp):
                for dst, src in ((wout[:], T["w_out"][l].rearrange("(k p) n -> p k n", p=P)),
                                 (wr[:], T["w_router"][l].rearrange("(k p) n -> p k n", p=P)),
                                 (gain[:, 0, :], T["gla_out_norm"][l].partition_broadcast(P)),
                                 (gain[:, 1, :], T["gdn_out_norm"][l].partition_broadcast(P))):
                    sp.dma_start(dst, src).then_inc(w_in, 16)

                def load(t):
                    row = t * P if isinstance(t, int) else sp.snap(t * P)
                    prow = proj_row(t) if isinstance(t, int) else sp.snap(t * P + 2)
                    R, Q = bass.ds(row, P), bass.ds(prow, P)
                    sp.wait_ge(o_turned, t + 1)
                    for dst, src in ((o[:, 0:256], T["mla_out"][R, :]), (o[:, 256:], T["scan_f"][R, :]), (ob[:], T["scan_b"][R, :]),
                                     (z[:, 0:GQ], T["proj"][Q, C_GZ:C_DQ]), (z[:, GQ:], T["proj"][Q, C_DZ:C_DB])):
                        sp.dma_start(dst, src).then_inc(t_in, 16)

                load(0)
                load(1)

                def body(t, s):
                    if not has(t):
                        return
                    row = t * P if isinstance(t, int) else sp.snap(t * P)
                    if has(t, 2):
                        load(t + 2)
                    sp.wait_ge(xhat_done, t + 2)
                    sp.dma_start(T["xhat"][bass.ds(row, P), :], xhat[:, s]).then_inc(stored[s], 16)
                turns(sp, body)
                sp.wait_ge(affT_done, TILES + 1)
                sp.dma_start(T["affT"], affT[:]).then_inc(all_stored, 16)
                sp.wait_ge(all_stored, 17)
                for s in range(2):
                    sp.wait_ge(stored[s], 16 * ((TILES + 1 - s) // 2) + 1)

            @block.scalar
            def _(act):
                own, step = asem, Steps()

                def gates(t):
                    act.wait_ge(t_in, t * 80 + 81)
                    act.activation(z[:], z[:], ACT.Silu).then_inc(zsilu_done, 1)

                def head_logs(t):
                    act.wait_ge(ss_done, t + 2)
                    act.activation(ss[:], ss[:], ACT.Ln, bias=B.eps[:, 0:1], scale=1.0 / GK).then_inc(own, step())

                def head_scales():
                    act.activation(ss[:], ss[:], ACT.Exp, scale=-0.5).then_inc(rs_done, 1)

                def turned(t):
                    act.wait_ge(o_turned, t + 2)
                    act.wait_ge(y_prod, t + 1)
                    act.activation(oT[:], tr[:], ACT.Copy).then_inc(oT_done, 1)

                for t in range(2):
                    gates(t)
                    head_logs(t)
                    act.wait_ge(own, step.n)
                    head_scales()
                    if t == 0:
                        turned(0)
                act.sem_clear(own)
                step.restart()

                def body(t, s):
                    if has(t):
                        act.wait_ge(y_prod, t + 2)
                        act.activation(sq[:], acc[:], ACT.Square, accum_out=rs[:, 0:1]).then_inc(own, step())
                        act.wait_ge(own, step.n)
                        act.activation(rs[:, 0:1], rs[:, 0:1], ACT.Ln, bias=B.eps[:, 0:1], scale=1.0 / D).then_inc(own, step())
                        act.wait_ge(own, step.n)
                        act.activation(rs[:, 0:1], rs[:, 0:1], ACT.Exp, scale=-0.5).then_inc(yrs_done, 1)
                    if has(t, 1):
                        turned(t + 1)
                    if has(t, 2):
                        gates(t + 2)
                    if has(t):
                        act.wait_ge(x_done, t + 2)
                        act.activation(sq[:], B.x[:, t, :], ACT.Square, accum_out=rs[:, 1:2]).then_inc(own, step())
                        act.wait_ge(own, step.n)
                        act.activation(rs[:, 1:2], rs[:, 1:2], ACT.Ln, bias=B.eps[:, 0:1], scale=1.0 / D).then_inc(own, step())
                        if has(t, 2):
                            head_logs(t + 2)
                        act.wait_ge(own, step.n)
                        act.activation(rs[:, 1:2], rs[:, 1:2], ACT.Exp, scale=-0.5).then_inc(xrs_done, 1)
                        if has(t, 2):
                            head_scales()
                    if has(t, -1):
                        act.wait_ge(max_done, t + 1)
                        act.activation(ex[:], lg[:, 0:E_N], ACT.Exp, bias=mx[:, 0:1], accum_out=den[:]).then_inc(exp_done, 1)
                    if has(t):
                        act.sem_clear(own)
                        step.restart()
                turns(act, body)

            @block.tensor
            def _(pe):
                pe.wait_ge(w_in, 65)

                def turn(t):
                    pe.wait_ge(o_done, t + 2)
                    pe.wait_ge(oT_done, t + 1)
                    for k in range(KD):
                        mm = pe.transpose(tr[:, k, :], o[:, k * P:(k + 1) * P], B.ident)
                    mm.then_inc(o_turned, 1)

                def project(t):
                    pe.wait_ge(oT_done, t + 2)
                    pe.wait_ge(branch_done, t + 1)
                    for n in range(2):
                        for k in range(KD):
                            mm = pe.matmul(acc[:, n * 512:(n + 1) * 512], oT[:, k, :], wout[:, k, n * 512:(n + 1) * 512], start=k == 0, stop=k == KD - 1)
                    mm.then_inc(y_prod, 1)

                turn(0)
                project(0)
                turn(1)

                def body(t, s):
                    if has(t, -1):
                        pe.wait_ge(xhat_done, t + 1)
                        for k in range(KD):
                            mm = pe.transpose(xtr[:, k, :], xhat[:, 1 - s, k * P:(k + 1) * P], B.ident)
                        mm.then_inc(x_turned, 1)
                        pe.wait_ge(xT_done, t + 1)
                        for k in range(KD):
                            mm = pe.matmul(lg[:, 0:E_N], xT[:, k, :], wr[:, k, :], start=k == 0, stop=k == KD - 1)
                        mm.then_inc(logits, 1)
                    if has(t, 1):
                        project(t + 1)
                    if has(t, 2):
                        turn(t + 2)
                    if has(t, -1):
                        pe.wait_ge(aff_done, t + 1)
                        pe.wait_ge(affT_done, t)
                        pe.transpose(at[0:E_N + 2, 0:P], af[:], B.ident).then_inc(aff_turned, 1)
                turns(pe, body)

            @block.vector
            def _(dve):
                own, step = dsem, Steps()
                dve.memset(af[:], 0.0).then_inc(own, step())
                dve.wait_ge(w_in, 65)

                def head_sums(t):
                    m = o[:, 256:]
                    dve.wait_ge(t_in, t * 80 + 81)
                    dve.tensor_tensor(m, m, ob[:], ALU.add).then_inc(own, step())
                    dve.wait_ge(own, step.n)
                    dve.tensor_tensor(ob[:], m, m, ALU.mult).then_inc(own, step())
                    dve.wait_ge(own, step.n)
                    dve.tensor_reduce(ss[:], ob[:].rearrange("p (h e) -> p h e", e=GK), AX.X, ALU.add).then_inc(ss_done, 1)

                def head_norms(t):
                    m = o[:, 256:]
                    mh = m.rearrange("p (h e) -> p h e", e=GK)
                    dve.wait_ge(zsilu_done, t + 2)
                    dve.tensor_tensor(m, m, z[:], ALU.mult).then_inc(own, step())
                    dve.wait_ge(own, step.n)
                    dve.tensor_tensor(mh[:, 0:H_GLA], mh[:, 0:H_GLA], gain[:, 0:1, :].to_broadcast([P, H_GLA, GK]), ALU.mult).then_inc(own, step())
                    dve.tensor_tensor(mh[:, H_GLA:], mh[:, H_GLA:], gain[:, 1:2, :].to_broadcast([P, H_GDN, GK]), ALU.mult).then_inc(own, step())
                    dve.wait_ge(own, step.n)
                    dve.wait_ge(rs_done, t + 2)
                    dve.tensor_tensor(mh, mh, ss[:].unsqueeze(2).to_broadcast([P, NH, GK]), ALU.mult).then_inc(o_done, 1)

                for t in range(2):
                    head_sums(t)
                    head_norms(t)
                dve.wait_ge(own, step.n)
                dve.sem_clear(own)
                step.restart()

                def tile_scale(t):
                    return 0 if isinstance(t, int) and t == 0 else 1

                def body(t, s):
                    if has(t, -2):
                        dve.wait_ge(aff_turned, t)
                        dve.tensor_copy(affT[:, bass.ds((t - 2) * P, P)], at[0:E_N + 2, 0:P]).then_inc(affT_done, 1)
                    if has(t, -1):
                        c = tile_scale(t - 1) if isinstance(t, int) else 1
                        dve.wait_ge(x_turned, t + 1)
                        for k in range(KD):
                            dve.tensor_scalar(xT[:, k, :], xtr[:, k, :], B.scale[:, c, 1, k:k + 1], B.shift[:, c, 1, k:k + 1], ALU.mult, ALU.add).then_inc(own, step())
                        dve.wait_ge(own, step.n)
                        dve.sem_inc(xT_done, 1)
                    if has(t):
                        dve.wait_ge(yrs_done, t + 2)
                        dve.scalar_tensor_tensor(branch[:], acc[:], rs[:, 0:1], B.gate[:, 0, tile_scale(t), :], ALU.mult, ALU.mult).then_inc(branch_done, 1)
                        dve.wait_ge(branch_done, t + 2)
                        dve.tensor_tensor(B.x[:, t, :], B.x[:, t, :], branch[:], ALU.add).then_inc(x_done, 1)
                    if has(t, 2):
                        head_sums(t + 2)
                    if has(t, -1):
                        dve.wait_ge(logits, t + 1)
                        dve.tensor_reduce(mx[:], lg[:, 0:E_N], AX.X, ALU.max).then_inc(own, step())
                        dve.wait_ge(own, step.n)
                        dve.tensor_scalar(mx[:], mx[:], -1.0, None, ALU.mult).then_inc(max_done, 1)
                    if has(t):
                        dve.wait_ge(xrs_done, t + 2)
                        dve.wait_ge(stored[s], (t // 2) * 16 + 1 if isinstance(t, int) else t * 8 + (1 - 8 * s))
                        dve.tensor_scalar(xhat[:, s], B.x[:, t, :], rs[:, 1:2], None, ALU.mult).then_inc(xhat_done, 1)
                    if has(t, 2):
                        head_norms(t + 2)
                    if has(t, -1):
                        dve.wait_ge(exp_done, t + 1)
                        dve.reciprocal(den[:], den[:]).then_inc(own, step())
                        dve.wait_ge(own, step.n)
                        dve.tensor_scalar(af[:, 0:E_N], ex[:], den[:, 0:1], None, ALU.mult).then_inc(own, step())
                        dve.wait_ge(own, step.n)
                        dve.sem_inc(aff_done, 1)
                        dve.tensor_copy(B.aff[:, t - 1, :], af[:]).then_inc(own, step())
                    if has(t, -1) or has(t, 2):
                        dve.wait_ge(own, step.n)
                        dve.sem_clear(own)
                        step.restart()
                turns(dve, body)


def experts(nc, T, B, l):
    RING = 4
    PER = KF // RING
    PER_BANK = 512 // CAP
    with stage(nc, "ffn") as st:
        w1, w3, w2 = (st.sb(x, [P, RING, KD, P]) for x in ("w1", "w3", "w2"))
        xe, xp = st.sb("xe", [P, D]), st.sb("xp", [CAP_P, D])
        g_idx, s_idx = st.sb("g_idx", [P, 2], I32), st.sb("s_idx", [P, 2], I32)
        xT = st.sb("xT", [P, 2, KD, CAP])
        en = st.sb("en", [P, 2, CAP])
        hT = st.sb("hT", [P, 2, CAP])
        yT = st.sb("yT", [P, KD, CAP])
        ye, yp = st.sb("ye", [P, D]), st.sb("yp", [CAP_P, D])
        row = st.sb("row", [P, ROWS])
        junk = st.sb("junk", [P, DEC])
        counts = st.sb("counts", [P, TILES, 3])
        rank = st.sb("rank", [P, TILES])
        sel = st.sb("sel", [P, TILES, P])
        pair = st.sb("pair", [P, TILES, 2])
        later = st.sb("later", [P, P])
        token, gate = st.sb("token", [P, 2, E_N + 2]), st.sb("gate", [P, 2, E_N + 2])
        acc, hb = st.ps("acc", [P, 3, 512]), st.ps("hb", [P, 2, 512])
        tr, trp = st.ps("tr", [P, D]), st.ps("trp", [P, 512])
        slot_s, slot_p = trp[:, 0:2], trp[0:CAP_P, 2:4]
        w_in = [st.sem(f"w_in{i}") for i in range(RING)]
        w_used = [st.sem(f"w_used{i}") for i in range(RING)]
        idx_done, turned, xT_done, h_prod, silu_done, h_done, yT_done = (
            st.sem(x) for x in ("idx_done", "turned", "xT_done", "h_prod", "silu_done", "h_done", "yT_done"))
        y_turned, y_done, rows_added, passed = (st.sem(x) for x in ("y_turned", "y_done", "rows_added", "passed"))
        half_done = st.sem("half_done")
        row_in, ranked, sel_done, picked = (st.sem(x) for x in ("row_in", "ranked", "sel_done", "picked"))
        zeroed, cleared, dsem = st.sem("zeroed"), st.sem("cleared"), st.sem("dve_steps")
        gathered, scattered = B.gathered, B.scattered
        part = lambda c: acc[:, c // PER_BANK, (c % PER_BANK) * CAP:(c % PER_BANK + 1) * CAP]

        def turns(eng, body):
            body(0, 0, True)
            body(1, 1, False)
            with eng.Fori(1, E_N // 2) as i:
                for s in range(2):
                    body(i * 2 + s, s, False)

        with st.block() as block:
            @block.sync
            def _(sp):
                for e in range(2):
                    sp.wait_ge(ranked, e + 1)
                    sp.dma_start(row[:], T["affT"][e:e + 1, :].to_broadcast([P, ROWS])).then_inc(row_in, 16)

                def body(e, s, first):
                    for j in range(KF):
                        r = j % RING
                        c = slice(j * P, (j + 1) * P)
                        sp.wait_ge(w_used[r], e * PER + j // RING + 1)
                        sp.dma_start(w1[:, r], T["w_e1"][l, bass.ds(e, 1), :, c].rearrange("a (k p) n -> p (a k) n", p=P)).then_inc(w_in[r], 16)
                        sp.dma_start(w3[:, r], T["w_e3"][l, bass.ds(e, 1), :, c].rearrange("a (k p) n -> p (a k) n", p=P)).then_inc(w_in[r], 16)
                        sp.dma_start(w2[:, r].rearrange("p k n -> p (k n)"), T["w_e2"][l, bass.ds(e, 1), c, :].rearrange("a p n -> p (a n)")).then_inc(w_in[r], 16)
                        if j == 1:
                            sp.wait_ge(ranked, e + 3)
                            sp.dma_start(row[:], T["affT"][bass.ds(e + 2, 1), :].to_broadcast([P, ROWS])).then_inc(row_in, 16)
                turns(sp, body)
                sp.wait_ge(row_in, 16 * (E_N + 2) + 1)

            @block.gpsimd
            def _(pool):
                pool.memset(ye[:], 0.0).then_inc(zeroed, 1)

                def gather():
                    for dst, n, k in ((xe, P, 0), (xp, CAP_P, 1)):
                        at = bass.IndirectOffsetOnAxis(ap=g_idx[0:n, k:k + 1].bitcast(U32), axis=0)
                        pool.indirect_dma_start(dst[:], None, T["xhat"], at).then_inc(gathered, 16)

                def scatter(e):
                    pool.wait_ge(y_done, e + 2)
                    pool.sem_inc(passed, 1)
                    for src, n, k in ((ye, P, 0), (yp, CAP_P, 1)):
                        at = bass.IndirectOffsetOnAxis(ap=s_idx[0:n, k:k + 1].bitcast(U32), axis=0)
                        pool.indirect_dma_start(T["moe"], at, src[:], None, compute_op=ALU.add).then_inc(scattered, 16)
                    pool.wait_ge(scattered, l * (E_N * 32) + (e * 32 + 32))
                    pool.sem_inc(rows_added, 1)

                pool.wait_ge(idx_done, 2)
                gather()
                pool.wait_ge(cleared, 16 * TILES + 1)

                def body(e, s, first):
                    pool.wait_ge(turned, e + 2)
                    pool.wait_ge(idx_done, e + 3)
                    pool.sem_inc(passed, 1)
                    gather()
                    if not first:
                        scatter(e - 1)
                turns(pool, body)
                scatter(E_N - 1)
                pool.wait_ge(gathered, l * ((E_N + 1) * 32) + (E_N + 1) * 32)

            @block.tensor
            def _(pe):
                def turn_x(e):
                    pe.wait_ge(gathered, l * ((E_N + 1) * 32) + (e * 32 + 32))
                    for k in range(KD):
                        pe.transpose(tr[:, k * P:(k + 1) * P], xe[:, k * P:(k + 1) * P], B.ident)
                    for k in range(KD):
                        mm = pe.transpose(trp[:, k * CAP_P:(k + 1) * CAP_P], xp[:, k * P:(k + 1) * P], B.ident[0:CAP_P, 0:CAP_P])
                    mm.then_inc(turned, 1)

                def turn_y(e, half):
                    if half == 0:
                        pe.wait_ge(yT_done, e * 2 + 3)
                        for k in range(KD):
                            pe.transpose(tr[:, k * P:(k + 1) * P], yT[:, k, 0:CAP_S], B.ident)
                    else:
                        pe.wait_ge(half_done, e + 2)
                    for k in range(4):
                        mm = pe.transpose(trp[0:CAP_P, k * P:(k + 1) * P], yT[:, 4 * half + k, CAP_S:], B.ident)
                    mm.then_inc(y_turned, 1)

                def pick(e):
                    pe.wait_ge(sel_done, e + 2)
                    for t in range(1, TILES):
                        pe.matmul(slot_s, sel[:, t, :], pair[:, t, :], start=t == 1, stop=t == TILES - 1)
                    pe.matmul(slot_p, sel[:, 0, 0:CAP_P], pair[:, 0, :], start=True, stop=True).then_inc(picked, 1)

                pick(0)
                pick(1)
                turn_x(0)

                def body(e, s, first):
                    def up_products(j):
                        r, b = j % RING, j % 2
                        pe.wait_ge(w_in[r], (e * PER + j // RING) * 48 + 49)
                        if j >= 2:
                            pe.wait_ge(h_done, e * KF + j)
                        for i, w in enumerate((w1, w3)):
                            for k in range(KD):
                                mm = pe.matmul(hb[:, b, i * CAP:(i + 1) * CAP], w[:, r, k, :], xT[:, s, k, :], start=k == 0, stop=k == KD - 1)
                        mm.then_inc(h_prod, 1)

                    def down_products(j):
                        r, b = j % RING, j % 2
                        pe.wait_ge(h_done, e * KF + j + 2)
                        for c in range(KD):
                            mm = pe.matmul(part(c), w2[:, r, c, :], hT[:, b, :], start=j == 0 and c % PER_BANK == 0,
                                           stop=j == KF - 1, skip_group_check=True)
                        mm.then_inc(w_used[r], 1)

                    pe.wait_ge(xT_done, e + 2)
                    up_products(0)
                    if not first:
                        turn_y(e - 1, 0)
                    up_products(1)
                    if not first:
                        pe.wait_ge(yT_done, e * 2 + 1)
                    down_products(0)
                    if not first:
                        turn_y(e - 1, 1)
                    for j in range(2, KF):
                        if j == 6:
                            pe.wait_ge(y_done, e + 1)
                            turn_x(e + 1)
                        up_products(j)
                        down_products(j - 1)
                    pe.wait_ge(xT_done, e + 3)
                    pick(e + 2)
                    down_products(KF - 1)
                turns(pe, body)
                turn_y(E_N - 1, 0)
                turn_y(E_N - 1, 1)

            @block.scalar
            def _(act):
                act.wait_ge(zeroed, 2)
                for t in range(TILES):
                    act.dma_start(T["moe"][t * P:(t + 1) * P, :], ye[:]).then_inc(cleared, 16)

                def body(e, s, first):
                    for j in range(KF):
                        act.wait_ge(h_prod, e * KF + j + 2)
                        if not (first and j < 2):
                            act.wait_ge(h_done, e * KF + j)
                        act.activation(en[:, j % 2], hb[:, j % 2, 0:CAP], ACT.Silu).then_inc(silu_done, 1)
                    act.wait_ge(w_used[RING - 1], e * PER + PER + 1)
                    for b in (1, 2):
                        n = min(PER_BANK, KD - b * PER_BANK)
                        ins = act.activation(yT[:, b * PER_BANK:b * PER_BANK + n, :].rearrange("p k n -> p (k n)"), acc[:, b, 0:n * CAP], ACT.Copy)
                    ins.then_inc(yT_done, 1)
                turns(act, body)

            @block.vector
            def _(dve):
                own, step = dsem, Steps()
                dve.memset(counts[:], 0.0).then_inc(own, step())
                dve.tensor_tensor(later[:], B.masks[:, 2, :], B.ident, ALU.subtract).then_inc(own, step())
                dve.tensor_copy(pair[:, :, 0], B.ids[:, 0:TILES]).then_inc(own, step())

                def rank_tile(t):
                    mine = pair[:, t, 1:2]
                    lo, hi = (0, SEQ) if t == 0 else (SEQ, ROWS)
                    a, b = t * P, (t + 1) * P
                    dve.wait_ge(own, step.n)
                    if a > lo:
                        dve.tensor_scalar(junk[:, 0:a - lo], row[:, lo:a], mine, 0.0, ALU.is_ge, ALU.add, accum_out=counts[:, t, 0:1]).then_inc(own, step())
                    dve.tensor_scalar(junk[:, a - lo:hi - lo], row[:, a:hi], mine, 0.0, ALU.is_gt, ALU.add, accum_out=counts[:, t, 1:2]).then_inc(own, step())
                    dve.wait_ge(own, step.n)
                    dve.scalar_tensor_tensor(junk[:, 0:P], row[:, a:b], mine, later[:], ALU.is_equal, ALU.mult, accum_out=counts[:, t, 2:3]).then_inc(own, step())

                def rank_start(e):
                    dve.wait_ge(row_in, e * 16 + 17)
                    dve.tensor_copy(pair[:, :, 1], B.aff[:, :, e]).then_inc(own, step())

                def rank_end():
                    dve.wait_ge(own, step.n)
                    dve.tensor_reduce(rank[:], counts[:], AX.X, ALU.add).then_inc(own, step())
                    dve.wait_ge(own, step.n)
                    dve.sem_inc(ranked, 1)
                    slots = B.ids[:, TILES:TILES + P].unsqueeze(1).to_broadcast([P, TILES, P])
                    dve.tensor_tensor(sel[:], slots, rank[:].unsqueeze(2).to_broadcast([P, TILES, P]), ALU.is_equal).then_inc(sel_done, 1)

                def rank_picked(e):
                    dve.wait_ge(picked, e + 2)
                    for src, n, k in ((slot_s, P, 0), (slot_p, CAP_P, 1)):
                        dve.tensor_copy(token[0:n, k, bass.ds(e, 1)], src[:, 0:1]).then_inc(own, step())
                        dve.tensor_copy(gate[0:n, k, bass.ds(e, 1)], src[:, 1:2]).then_inc(own, step())

                def index(idx, e, signal):
                    if step.count:
                        dve.wait_ge(own, step.n)
                    dve.tensor_copy(idx[:, 0:1], token[:, 0, bass.ds(e, 1)]).then_inc(own, step())
                    dve.tensor_copy(idx[0:CAP_P, 1:2], token[0:CAP_P, 1, bass.ds(e, 1)]).then_inc(own, step())
                    dve.wait_ge(own, step.n)
                    if signal:
                        dve.sem_inc(signal, 1)

                def modulate(e, s):
                    dve.wait_ge(turned, e + 2)
                    for k in range(KD):
                        dve.tensor_scalar(xT[:, s, k, 0:CAP_S], tr[:, k * P:(k + 1) * P], B.scale[:, 1, 1, k:k + 1], B.shift[:, 1, 1, k:k + 1], ALU.mult, ALU.add).then_inc(own, step())
                    tp = trp[:, 0:KD * CAP_P].rearrange("p (k n) -> p k n", n=CAP_P)
                    sc, sh = (a[:, 0, 1, :].unsqueeze(2).to_broadcast([P, KD, CAP_P]) for a in (B.scale, B.shift))
                    dve.tensor_tensor(xT[:, s, :, CAP_S:], tp, sc, ALU.mult).then_inc(own, step())
                    dve.wait_ge(own, step.n)
                    dve.tensor_tensor(xT[:, s, :, CAP_S:], xT[:, s, :, CAP_S:], sh, ALU.add).then_inc(xT_done, 1)

                def output(e, half):
                    dve.wait_ge(y_turned, e * 2 + half + 2)
                    if half == 0:
                        dve.tensor_scalar(ye[:], tr[:], gate[:, 0, bass.ds(e, 1)], None, ALU.mult).then_inc(own, step())
                    dve.tensor_scalar(yp[:, half * 512:(half + 1) * 512], trp[0:CAP_P, :], gate[0:CAP_P, 1, bass.ds(e, 1)], None, ALU.mult).then_inc(own, step())
                    dve.wait_ge(own, step.n)
                    dve.sem_inc(half_done if half == 0 else y_done, 1)

                for e in range(2):
                    rank_start(e)
                    for t in range(TILES):
                        rank_tile(t)
                    rank_end()
                    rank_picked(e)
                index(g_idx, 0, idx_done)
                modulate(0, 0)
                dve.wait_ge(cleared, 16 * TILES + 1)
                dve.wait_ge(own, step.n)
                dve.sem_clear(own)
                step.restart()

                def body(e, s, first):
                    for j in range(KF):
                        b = j % 2
                        dve.wait_ge(silu_done, e * KF + j + 2)
                        dve.tensor_tensor(hT[:, b, :], en[:, b], hb[:, b, CAP:2 * CAP], ALU.mult).then_inc(h_done, 1)
                        if j == 0:
                            dve.tensor_copy(pair[:, :, 1], B.aff[:, :, e + 2]).then_inc(own, step())
                            index(g_idx, e + 1, idx_done)
                            if not first:
                                dve.wait_ge(rows_added, e)
                                index(s_idx, e - 1, None)
                                output(e - 1, 0)
                            dve.wait_ge(row_in, e * 16 + 49)
                        if j == 1 and not first:
                            output(e - 1, 1)
                        if j == 5:
                            modulate(e + 1, 1 - s)
                        if j == 6:
                            rank_end()
                        for t in ((), (0, 1), (2, 3), (4, 5), (6, 7), (8,), (), ())[j]:
                            rank_tile(t)
                    rank_picked(e + 2)
                    dve.wait_ge(w_used[RING - 1], e * PER + PER + 1)
                    dve.tensor_copy(yT[:, 0:PER_BANK, :].rearrange("p k n -> p (k n)"), acc[:, 0, 0:PER_BANK * CAP]).then_inc(own, step())
                    dve.wait_ge(own, step.n)
                    dve.sem_clear(own)
                    step.restart()
                    dve.sem_inc(yT_done, 1)
                turns(dve, body)
                dve.wait_ge(rows_added, E_N)
                index(s_idx, E_N - 1, None)
                output(E_N - 1, 0)
                output(E_N - 1, 1)


def expert_residual(nc, T, B, l):
    G = 3
    with stage(nc, "resid") as st:
        y = st.sb("y", [P, TILES, D])
        sq = st.sb("sq", [P, G, D])
        rs = st.sb("rs", [P, TILES])
        y_in, rs_done = [st.sem(f"y_in{g}") for g in range(TILES // G)], st.sem("rs_done")
        asem, dsem = st.sem("act_steps"), st.sem("dve_steps")
        with st.block() as block:
            @block.sync
            def _(sp):
                for t in range(TILES):
                    sp.dma_start(y[:, t], T["moe"][t * P:(t + 1) * P, :]).then_inc(y_in[t // G], 16)

            @block.scalar
            def _(act):
                own, step = asem, Steps()
                for g in range(TILES // G):
                    r = rs[:, g * G:(g + 1) * G]
                    act.wait_ge(y_in[g], 16 * G + 1)
                    for j in range(G):
                        act.activation(sq[:, j], y[:, g * G + j], ACT.Square, accum_out=rs[:, g * G + j:g * G + j + 1]).then_inc(own, step())
                    act.wait_ge(own, step.n)
                    act.activation(r, r, ACT.Ln, bias=B.eps[:, 0:1], scale=1.0 / D).then_inc(own, step())
                    act.wait_ge(own, step.n)
                    act.activation(r, r, ACT.Exp, scale=-0.5).then_inc(rs_done, 1)

            @block.vector
            def _(dve):
                own, step = dsem, Steps()
                for t in range(TILES):
                    dve.wait_ge(rs_done, t // G + 2)
                    yt = y[:, t]
                    dve.scalar_tensor_tensor(yt, yt, rs[:, t:t + 1], B.gate[:, 1, 1 if t else 0, :], ALU.mult, ALU.mult).then_inc(own, step())
                    dve.wait_ge(own, step.n)
                    dve.tensor_tensor(B.x[:, t, :], B.x[:, t, :], yt, ALU.add).then_inc(own, step())


def store_outputs(nc, T, B):
    with stage(nc, "store") as st:
        stored = st.sem("stored")
        with st.block() as block:
            @block.sync
            def _(sp):
                sp.dma_start(T["y_prompt"][0], B.x[:, 0, :]).then_inc(stored, 16)
                sp.dma_start(T["y_sample"][0].rearrange("(t p) d -> p t d", p=P), B.x[:, 1:TILES, :]).then_inc(stored, 16)
                sp.wait_ge(stored, 33)


class Buffers:
    pass


def host_constants():
    j, i = np.arange(P)[:, None], np.arange(P)[None, :]
    up_f = (j <= i).astype(np.float32)
    up_b = (j >= i).astype(np.float32)
    m = [np.eye(P, dtype=np.float32), up_f, up_b,
         up_f - up_f[:, P // 2 - 1:P // 2], up_b - up_b[:, P // 2:P // 2 + 1]]
    for back in (0, 1):
        b = 1
        while b < P:
            lev = (j // (2 * b) == i // (2 * b)) & (i % (2 * b) >= b) & (j % (2 * b) < b)
            m.append((lev.T if back else lev).astype(np.float32))
            b *= 2
    masks = np.stack(m, 1)
    half = ROPE // 2
    freqs = (ROPE_BASE ** (-np.arange(0, half, 2, dtype=np.float32) / half)).astype(np.float32)
    t = np.arange(DEC)
    row, col = (t // GRID_W).astype(np.float32), (t % GRID_W).astype(np.float32)
    ang = np.concatenate([row[:, None] * freqs, col[:, None] * freqs], -1)
    rope = np.stack([np.cos(ang), np.sin(ang)], 1).astype(np.float32)
    rope = np.concatenate([np.stack([np.ones((P, half)), np.zeros((P, half))], 1).astype(np.float32), rope])
    rope = np.ascontiguousarray(rope.reshape(TILES, P, 2, half).transpose(1, 0, 2, 3))
    ids = np.zeros((P, TILES + P + 4), np.float32)
    ids[:, :TILES] = np.arange(ROWS).reshape(TILES, P).T
    ids[:, TILES:TILES + P] = np.arange(P)[None, :]
    ids[:, TILES + P:] = np.stack([up_f[:, P // 2 - 1], np.ones(P), up_b[:, P // 2], np.ones(P)], 1)
    return {"masks": masks, "rope": rope, "ids": ids}


OUTS = [("y_prompt", (1, SEQ, D)), ("y_sample", (1, DEC, D)), ("new_ckv", (1, DEPTH, SEQ, KVL)),
        ("new_krope", (1, DEPTH, SEQ, ROPE)), ("new_gla", (1, DEPTH, 2, H_GLA, GK, GK)),
        ("new_gdn", (1, DEPTH, 2, H_GDN, GK, GK))]
SCRATCH = [("mod", (2, 6 * D)), ("proj", (ROWS + 3, IN_DIM)), ("qkv", (ROWS, 3 * DQ)), ("gates", (ROWS, 32)),
           ("gla_la", (ROWS, 2 * GQ)), ("mla_out", (ROWS, 256)), ("scan_f", (ROWS, 768)), ("scan_b", (ROWS, 768)),
           ("xhat", (ROWS, D)), ("affT", (E_N + 2, ROWS)), ("moe", (ROWS, D))]


def build(nc, T, last_stage=99):
    with ExitStack() as ctx:
        B = Buffers()
        sb = lambda n, s: ctx.enter_context(nc.sbuf_tensor(n, s, F32))
        B.gathered = ctx.enter_context(nc.semaphore("gathered"))
        B.scattered = ctx.enter_context(nc.semaphore("scattered"))
        B.x = sb("x_res", [P, TILES, D])
        B.masks = sb("masks_sb", [P, 19, P])
        B.ident = B.masks[:, 0, :]
        B.rope = sb("rope_sb", [P, TILES, 2, ROPE // 2])
        B.ids = sb("ids_sb", [P, TILES + P + 4])
        B.midcols = B.ids[:, TILES + P:]
        B.zero = sb("zero", [P, 32])
        B.ones = sb("ones", [P, P])
        B.eps = sb("eps", [P, 1])
        B.scale = sb("scale", [P, 2, 2, KD])
        B.shift = sb("shift", [P, 2, 2, KD])
        B.gate = sb("gate", [P, 2, 2, D])
        B.aff = sb("aff", [P, TILES, E_N + 2])
        ctx.enter_context(nc.allow_non_contiguous_dma(reason="small tables are turned on the way in"))
        load_constants(nc, T, B)
        with nc.Fori(0, DEPTH if last_stage > 8 else 1) as l:
            modulation(nc, T, B, l)
            with nc.sbuf_tensor("xmT", [P, KD, ROWS], F32) as xmT:
                if last_stage > 0:
                    input_norm(nc, T, B, l, xmT)
                if last_stage > 1:
                    input_projection(nc, T, B, l, xmT)
            if last_stage > 2:
                latent_attention(nc, T, B, l)
            if last_stage > 4:
                scan(nc, T, B, l, True)
                scan(nc, T, B, l, False)
            if last_stage > 5:
                mixer_output(nc, T, B, l)
            if last_stage > 6:
                experts(nc, T, B, l)
            if last_stage > 7:
                expert_residual(nc, T, B, l)
        store_outputs(nc, T, B)


def kernel(**inputs):
    import concourse.bacc as bacc
    from concourse.bass_utils import run_bass_kernel_spmd

    nc = bacc.Bacc("TRN2", target_bir_lowering=False, num_devices=1)
    arrays, T = {}, {}
    for name, a in {**inputs, **host_constants()}.items():
        arrays[f"in_{name}"] = np.ascontiguousarray(a)
        T[name] = nc.dram_tensor(f"in_{name}", arrays[f"in_{name}"].shape, F32, kind="ExternalInput").ap()
    for name, shape in OUTS:
        T[name] = nc.dram_tensor(f"out_{name}", shape, F32, kind="ExternalOutput").ap()
    for name, shape in SCRATCH:
        T[name] = nc.dram_tensor(f"scratch_{name}", shape, F32, kind="Internal").ap()
    build(nc, T)
    r = run_bass_kernel_spmd(nc, [arrays], core_ids=[0])
    return tuple(r.results[0][f"out_{name}"] for name, _ in OUTS)
```
